# Optimizing a Trainium2 kernel written in Bass

```python
import math
import jax, jax.numpy as jnp
from jax import lax
import numpy as np

D_MODEL = 1024
BATCH = 1
SEQ = 1024
DEPTH = 1

HEAD_DIM = 64
ATTN_HEADS_PER_GROUP = 8
DILATED_GROUPS = ((128, 1), (512, 4), (2048, 16))
N_GROUPS = 3
ATTN_WIDTH = ATTN_HEADS_PER_GROUP * HEAD_DIM
N_ATTN_HEADS = N_GROUPS * ATTN_HEADS_PER_GROUP
QBLOCK = 128
N_BUCKETS = 32
MAX_DISTANCE = 2048
RWKV_HEADS = 8
RWKV_HEAD_SIZE = 64
RWKV_WIDTH = RWKV_HEADS * RWKV_HEAD_SIZE
DECAY_LORA = 64
AAA_LORA = 64
GN_EPS = 64e-5
RMS_EPS = 1e-6

QKV_COLS = 3 * N_GROUPS * ATTN_WIDTH
OFF_ATTN_GATE = QKV_COLS
OFF_RWKV = OFF_ATTN_GATE + ATTN_WIDTH
RWKV_SHIFT_COLS = 3 * RWKV_WIDTH + DECAY_LORA + AAA_LORA
OFF_RWKV_GATE = OFF_RWKV + RWKV_SHIFT_COLS
OFF_MERGE = OFF_RWKV_GATE + RWKV_WIDTH
IN_COLS = OFF_MERGE + 2 * D_MODEL


def rms_norm(x, g):
    xf = x.astype(jnp.float32)
    y = xf * lax.rsqrt(jnp.mean(xf * xf, axis=-1, keepdims=True) + RMS_EPS) * g.astype(jnp.float32)
    return y.astype(x.dtype)

def t5_causal_bucket(dist):
    d = np.maximum(np.asarray(dist), 0)
    max_exact = N_BUCKETS // 2
    ratio = np.log(np.maximum(d, 1).astype(np.float32) / max_exact) / np.float32(math.log(MAX_DISTANCE / max_exact))
    large = max_exact + (ratio * (N_BUCKETS - max_exact)).astype(np.int32)
    large = np.minimum(large, N_BUCKETS - 1)
    return np.where(d < max_exact, d, large).astype(np.int32)

def dilated_group_attention(q, k, v, bias_table_g, window, dilation):
    B, S, H, Dh = q.shape
    L = S // dilation
    steps = window // dilation
    nb = -(-L // QBLOCK)
    Lp = nb * QBLOCK

    def to_blocks(t):
        t = t.reshape(B, L, dilation, H, Dh).transpose(0, 2, 3, 1, 4)
        t = jnp.pad(t, ((0, 0), (0, 0), (0, 0), (0, Lp - L), (0, 0)))
        return t.reshape(B, dilation, H, nb, QBLOCK, Dh)

    def with_prev(t):
        prev = jnp.pad(t, ((0, 0), (0, 0), (0, 0), (1, 0), (0, 0), (0, 0)))[:, :, :, :-1]
        return jnp.concatenate([prev, t], axis=4)

    qb = to_blocks(q)
    kb = with_prev(to_blocks(k))
    vb = with_prev(to_blocks(v))

    qi = np.arange(QBLOCK)[:, None] + QBLOCK
    ki = np.arange(2 * QBLOCK)[None, :]
    rel = qi - ki
    band = (rel >= 0) & (rel <= steps)
    has_prev = (np.arange(nb)[:, None, None] > 0) | (ki >= QBLOCK)[None]
    valid = band[None] & has_prev
    bucket = t5_causal_bucket(np.maximum(rel, 0) * dilation)
    bias = bias_table_g.astype(jnp.float32)[bucket].transpose(2, 0, 1)

    scale = 1.0 / math.sqrt(Dh)
    logits = jnp.einsum('bdhnqc,bdhnkc->bdhnqk', qb, kb) * scale + bias[None, None, :, None]
    logits = jnp.where(valid, logits, -jnp.inf)
    m = jnp.max(logits, axis=-1)
    p = jnp.exp(logits - m[..., None])
    s = jnp.sum(p, axis=-1)
    num = jnp.einsum('bdhnqk,bdhnkc->bdhnqc', p, vb)

    def unblock(t):
        C = t.shape[-1]
        t = t.reshape(B, dilation, H, Lp, C)[:, :, :, :L]
        return t.transpose(0, 3, 1, 2, 4).reshape(B, S, H, C)

    return unblock(num), unblock(s[..., None])[..., 0], unblock(m[..., None])[..., 0]

def rwkv7_scan(r, decay, k, v, a_in, b_in):
    B, S, H, N = r.shape
    xs = tuple(t.transpose(1, 0, 2, 3) for t in (r, decay, k, v, a_in, b_in))

    def step(state, inp):
        r_t, w_t, k_t, v_t, a_t, b_t = inp
        sa = jnp.einsum('bhvk,bhk->bhv', state, a_t)
        state = (state * w_t[:, :, None, :] + sa[..., None] * b_t[:, :, None, :]
                 + v_t[..., None] * k_t[:, :, None, :])
        y = jnp.einsum('bhvk,bhk->bhv', state, r_t)
        return state, y

    s0 = jnp.zeros((B, H, N, N), jnp.float32)
    _, ys = lax.scan(step, s0, xs)
    return ys.transpose(1, 0, 2, 3)

def first_inputs(seed: int = 0) -> dict:
    key = jax.random.key(seed)
    ks = jax.random.split(key, 20)
    f32 = jnp.float32
    nrm = lambda k, shape: jax.random.normal(k, shape, f32)
    L = DEPTH
    return {
        "x": nrm(ks[0], (BATCH, SEQ, D_MODEL)),
        "pre_norm_gain": 1.0 + 0.05 * nrm(ks[1], (L, D_MODEL)),
        "w_in": nrm(ks[2], (L, D_MODEL, IN_COLS)) * D_MODEL ** -0.5,
        "rel_bias": 0.5 * nrm(ks[3], (N_BUCKETS, N_ATTN_HEADS)),
        "rwkv_shift_mix": jax.random.uniform(ks[4], (L, RWKV_SHIFT_COLS), f32),
        "rwkv_w0": jax.random.uniform(ks[5], (L, RWKV_WIDTH), f32, -6.0, 1.0),
        "rwkv_w_up": nrm(ks[6], (L, DECAY_LORA, RWKV_WIDTH)) * 0.5 * DECAY_LORA ** -0.5,
        "rwkv_a0": 0.5 * nrm(ks[7], (L, RWKV_WIDTH)),
        "rwkv_a_up": nrm(ks[8], (L, AAA_LORA, RWKV_WIDTH)) * 0.5 * AAA_LORA ** -0.5,
        "rwkv_k_k": 0.85 + 0.05 * nrm(ks[9], (L, RWKV_WIDTH)),
        "rwkv_k_a": 1.0 + 0.05 * nrm(ks[10], (L, RWKV_WIDTH)),
        "rwkv_r_k": 0.1 * nrm(ks[11], (L, RWKV_HEADS, RWKV_HEAD_SIZE)),
        "rwkv_ln_w": 1.0 + 0.05 * nrm(ks[12], (L, RWKV_WIDTH)),
        "rwkv_ln_b": 0.01 * nrm(ks[13], (L, RWKV_WIDTH)),
        "w_up_attn": nrm(ks[14], (L, ATTN_WIDTH, D_MODEL)) * ATTN_WIDTH ** -0.5,
        "w_up_rwkv": nrm(ks[15], (L, RWKV_WIDTH, D_MODEL)) * RWKV_WIDTH ** -0.5,
        "w_out": nrm(ks[16], (L, D_MODEL, D_MODEL)) * D_MODEL ** -0.5,
        "post_norm_gain": 1.0 + 0.05 * nrm(ks[17], (L, D_MODEL)),
    }

def first_block(x, pre_norm_gain, w_in, rel_bias, rwkv_shift_mix, rwkv_w0, rwkv_w_up,
              rwkv_a0, rwkv_a_up, rwkv_k_k, rwkv_k_a, rwkv_r_k, rwkv_ln_w, rwkv_ln_b,
              w_up_attn, w_up_rwkv, w_out, post_norm_gain):
    B, S, D = x.shape
    f32 = jnp.float32
    for l in range(DEPTH):
        h = rms_norm(x, pre_norm_gain[l])
        proj = h @ w_in[l]

        qkv = proj[..., :QKV_COLS].astype(f32).reshape(
            B, S, 3, N_GROUPS, ATTN_HEADS_PER_GROUP, HEAD_DIM)
        nums, dens, maxes = [], [], []
        for g, (window, dilation) in enumerate(DILATED_GROUPS):
            table_g = rel_bias[:, g * ATTN_HEADS_PER_GROUP:(g + 1) * ATTN_HEADS_PER_GROUP]
            num, den, mx = dilated_group_attention(
                qkv[:, :, 0, g], qkv[:, :, 1, g], qkv[:, :, 2, g], table_g, window, dilation)
            nums.append(num); dens.append(den); maxes.append(mx)
        m_all = jnp.max(jnp.stack(maxes), axis=0)
        wts = [jnp.exp(mx - m_all) for mx in maxes]
        num_tot = sum(w[..., None] * n for w, n in zip(wts, nums))
        den_tot = sum(w * d for w, d in zip(wts, dens))
        o_attn = (num_tot / den_tot[..., None]).reshape(B, S, ATTN_WIDTH).astype(x.dtype)
        z_attn = proj[..., OFF_ATTN_GATE:OFF_RWKV]
        y_attn = (o_attn * jax.nn.silu(z_attn)) @ w_up_attn[l]

        pr = proj[..., OFF_RWKV:OFF_RWKV_GATE].astype(f32)
        pr_prev = jnp.pad(pr, ((0, 0), (1, 0), (0, 0)))[:, :-1]
        pr = pr + (pr_prev - pr) * rwkv_shift_mix[l].astype(f32)
        r = pr[..., :RWKV_WIDTH]
        k = pr[..., RWKV_WIDTH:2 * RWKV_WIDTH]
        v = pr[..., 2 * RWKV_WIDTH:3 * RWKV_WIDTH]
        w_low = pr[..., 3 * RWKV_WIDTH:3 * RWKV_WIDTH + DECAY_LORA]
        a_low = pr[..., 3 * RWKV_WIDTH + DECAY_LORA:]
        w_log = -jax.nn.softplus(-(rwkv_w0[l].astype(f32) + jnp.tanh(w_low) @ rwkv_w_up[l].astype(f32))) - 0.5
        decay = jnp.exp(-jnp.exp(w_log))
        a = jax.nn.sigmoid(rwkv_a0[l].astype(f32) + a_low @ rwkv_a_up[l].astype(f32))
        hs = (B, S, RWKV_HEADS, RWKV_HEAD_SIZE)
        kk = (k * rwkv_k_k[l].astype(f32)).reshape(hs)
        kk = kk / jnp.maximum(jnp.linalg.norm(kk, axis=-1, keepdims=True), 1e-12)
        k = k * (1.0 + (a - 1.0) * rwkv_k_a[l].astype(f32))
        r4, k4, v4 = r.reshape(hs), k.reshape(hs), v.reshape(hs)
        y = rwkv7_scan(r4, decay.reshape(hs), k4, v4, -kk, kk * a.reshape(hs))
        mu = jnp.mean(y, axis=-1, keepdims=True)
        var = jnp.mean(jnp.square(y - mu), axis=-1, keepdims=True)
        y = ((y - mu) * lax.rsqrt(var + GN_EPS)).reshape(B, S, RWKV_WIDTH)
        y = y * rwkv_ln_w[l].astype(f32) + rwkv_ln_b[l].astype(f32)
        bonus = jnp.sum(r4 * k4 * rwkv_r_k[l].astype(f32), axis=-1, keepdims=True) * v4
        o_rwkv = (y + bonus.reshape(B, S, RWKV_WIDTH)).astype(x.dtype)
        z_rwkv = proj[..., OFF_RWKV_GATE:OFF_MERGE]
        y_rwkv = (o_rwkv * jax.nn.silu(z_rwkv)) @ w_up_rwkv[l]

        g_attn = proj[..., OFF_MERGE:OFF_MERGE + D_MODEL]
        g_rwkv = proj[..., OFF_MERGE + D_MODEL:]
        merged = jax.nn.sigmoid(g_attn) * y_attn + jax.nn.sigmoid(g_rwkv) * y_rwkv
        out = merged @ w_out[l]
        x = x + rms_norm(out, post_norm_gain[l])
    return x


GRID_W = 64
CTX_LEN = 256
MLA_HEADS = 8
QK_NOPE = 64
QK_ROPE = 32
QK_DIM = QK_NOPE + QK_ROPE
V_DIM = 64
Q_LORA = 384
KV_LORA = 256
ROPE_THETA = 10000.0
Q_BLOCK = 128
F_GROUPS = 4
F_GROUP_DIM = 128
D_F = F_GROUPS * F_GROUP_DIM
OFF_Q = 0
OFF_KV = OFF_Q + Q_LORA
OFF_KPE = OFF_KV + KV_LORA
OFF_F = OFF_KPE + QK_ROPE
OFF_GA = OFF_F + D_F
OFF_GB = OFF_GA + D_MODEL
N_IN = OFF_GB + D_MODEL
N_EXPERTS = 16
D_EXPERT = 512
CAPACITY_FACTOR = 2
EPS = 1e-6


def _rms(x, g):
    xf = x.astype(jnp.float32)
    y = xf * lax.rsqrt(jnp.mean(xf * xf, axis=-1, keepdims=True) + EPS)
    return (y * g.astype(jnp.float32)).astype(x.dtype)

def _modulate(h, shift, scale):
    return h * (1.0 + scale) + shift

def _axial_tables(pos_row, pos_col, dtype):
    half = QK_ROPE // 2
    n_freq = half // 2
    inv_freq = 1.0 / (ROPE_THETA ** (jnp.arange(n_freq, dtype=jnp.float32) / n_freq))

    def tab(pos):
        ang = pos.astype(jnp.float32)[:, None] * inv_freq[None, :]
        ang = jnp.concatenate([ang, ang], axis=-1)[None, :, None, :]
        return jnp.cos(ang).astype(dtype), jnp.sin(ang).astype(dtype)

    cr, sr = tab(pos_row)
    cc, scol = tab(pos_col)
    return cr, sr, cc, scol

def _rope_axis(x, cos, sin):
    x1, x2 = jnp.split(x, 2, axis=-1)
    return x * cos + jnp.concatenate([-x2, x1], axis=-1) * sin

def _rope_2d(x, tabs):
    cr, sr, cc, scol = tabs
    xr, xc = jnp.split(x, 2, axis=-1)
    return jnp.concatenate([_rope_axis(xr, cr, sr), _rope_axis(xc, cc, scol)], axis=-1)

def _mla_qkv(p, q_a_g, kv_a_g, w_q_up, w_kv_up, q_g, k_g, tabs):
    B, T, _ = p.shape
    cq = _rms(p[..., OFF_Q:OFF_KV], q_a_g)
    ckv = _rms(p[..., OFF_KV:OFF_KPE], kv_a_g)
    k_pe = p[..., OFF_KPE:OFF_F]
    q = (cq @ w_q_up).reshape(B, T, MLA_HEADS, QK_DIM)
    kv = (ckv @ w_kv_up).reshape(B, T, MLA_HEADS, QK_NOPE + V_DIM)
    k_nope, v = kv[..., :QK_NOPE], kv[..., QK_NOPE:]
    k = jnp.concatenate([k_nope, jnp.broadcast_to(k_pe[:, :, None, :], (B, T, MLA_HEADS, QK_ROPE))], axis=-1)
    q = _rms(q, q_g)
    k = _rms(k, k_g)
    if tabs is not None:
        q = jnp.concatenate([q[..., :QK_NOPE], _rope_2d(q[..., QK_NOPE:], tabs)], axis=-1)
        k = jnp.concatenate([k[..., :QK_NOPE], _rope_2d(k[..., QK_NOPE:], tabs)], axis=-1)
    return q, k, v

def _attend_dense(q, k, v):
    s = jnp.einsum('bqhd,bkhd->bhqk', q, k, preferred_element_type=jnp.float32) * (QK_DIM ** -0.5)
    pr = jax.nn.softmax(s, axis=-1).astype(v.dtype)
    return jnp.einsum('bhqk,bkhd->bqhd', pr, v)

def _attend_latent(q, k_lat, v_lat, k_ctx, v_ctx):
    B, T, H, _ = q.shape
    k_all = jnp.concatenate([k_lat, k_ctx], axis=1)
    v_all = jnp.concatenate([v_lat, v_ctx], axis=1)
    nb = T // Q_BLOCK
    qb = jnp.moveaxis(q.reshape(B, nb, Q_BLOCK, H, QK_DIM), 1, 0)
    o = lax.map(lambda qi: _attend_dense(qi, k_all, v_all), qb)
    return jnp.moveaxis(o, 0, 1).reshape(B, T, H * V_DIM)

def _fourier(f):
    B, T, _ = f.shape
    fg = f.reshape(B, T, F_GROUPS, F_GROUP_DIM).astype(jnp.float32)
    y = jnp.fft.fft2(fg, axes=(1, 3), norm="ortho").real
    return y.reshape(B, T, D_F).astype(f.dtype)

def _expert_choice(h, w_r, w_g, w_u, w_d):
    B, T, D = h.shape
    cap = (CAPACITY_FACTOR * T) // N_EXPERTS
    logits = jnp.einsum('btd,de->bte', h, w_r, preferred_element_type=jnp.float32)
    aff = jax.nn.softmax(logits, axis=-1)
    gate, idx = lax.top_k(jnp.swapaxes(aff, 1, 2), cap)
    xe = jax.vmap(lambda hb, ib: hb[ib])(h, idx)
    a = jnp.einsum('becd,edf->becf', xe, w_g)
    u = jnp.einsum('becd,edf->becf', xe, w_u)
    ye = jnp.einsum('becf,efd->becd', jax.nn.silu(a) * u, w_d) * gate[..., None].astype(h.dtype)
    return jax.vmap(lambda yb, ib: jnp.zeros((T, D), yb.dtype).at[ib.reshape(-1)].add(yb.reshape(-1, D)))(ye, idx)

def _merge(p, attn_o, four_o, w_o_attn, w_fourier, w_out):
    ga = jax.nn.sigmoid(p[..., OFF_GA:OFF_GB])
    gb = jax.nn.sigmoid(p[..., OFF_GB:N_IN])
    return (ga * (attn_o @ w_o_attn) + gb * (four_o @ w_fourier)) @ w_out

def second_inputs(seed: int = 0) -> dict:
    key = jax.random.key(seed)
    ks = jax.random.split(key, 24)
    L, D = DEPTH, D_MODEL

    def nrm(k, shape, fan_in, mult=1.0):
        return jax.random.normal(k, shape, jnp.float32) * (mult * fan_in ** -0.5)

    def gain(k, shape):
        return 1.0 + 0.02 * jax.random.normal(k, shape, jnp.float32)

    return {
        "x": jax.random.normal(ks[0], (BATCH, SEQ, D), jnp.float32),
        "c": jax.random.normal(ks[1], (BATCH, D), jnp.float32),
        "ctx": jax.random.normal(ks[2], (BATCH, CTX_LEN, D), jnp.float32),
        "c_ctx": 0.5 * jax.random.normal(ks[3], (D,), jnp.float32),
        "w_mod": nrm(ks[4], (L, D, 6 * D), D, 0.5),
        "b_mod": 0.02 * jax.random.normal(ks[5], (L, 6 * D), jnp.float32),
        "norm1_g": gain(ks[6], (L, D)),
        "w_in": nrm(ks[7], (L, D, N_IN), D),
        "q_a_norm_g": gain(ks[8], (L, Q_LORA)),
        "kv_a_norm_g": gain(ks[9], (L, KV_LORA)),
        "w_q_up": nrm(ks[10], (L, Q_LORA, MLA_HEADS * QK_DIM), Q_LORA),
        "w_kv_up": nrm(ks[11], (L, KV_LORA, MLA_HEADS * (QK_NOPE + V_DIM)), KV_LORA),
        "q_norm_g": gain(ks[12], (L, QK_DIM)),
        "k_norm_g": gain(ks[13], (L, QK_DIM)),
        "w_o_attn": nrm(ks[14], (L, MLA_HEADS * V_DIM, D), MLA_HEADS * V_DIM),
        "w_fourier": nrm(ks[15], (L, D_F, D), D_F),
        "w_out": nrm(ks[16], (L, D, D), D),
        "norm2_g": gain(ks[17], (L, D)),
        "w_router": nrm(ks[18], (L, D, N_EXPERTS), D),
        "w_e_gate": nrm(ks[19], (L, N_EXPERTS, D, D_EXPERT), D),
        "w_e_up": nrm(ks[20], (L, N_EXPERTS, D, D_EXPERT), D),
        "w_e_down": nrm(ks[21], (L, N_EXPERTS, D_EXPERT, D), D_EXPERT),
    }

def second_block(x, c, ctx, c_ctx, w_mod, b_mod, norm1_g, w_in, q_a_norm_g, kv_a_norm_g,
              w_q_up, w_kv_up, q_norm_g, k_norm_g, w_o_attn, w_fourier, w_out, norm2_g,
              w_router, w_e_gate, w_e_up, w_e_down):
    T = x.shape[1]
    rows = T // GRID_W
    pos_row = jnp.repeat(jnp.arange(rows, dtype=jnp.int32), GRID_W)
    pos_col = jnp.tile(jnp.arange(GRID_W, dtype=jnp.int32), rows)
    tabs = _axial_tables(pos_row, pos_col, x.dtype)
    s_lat = jax.nn.silu(c)
    s_ctx = jax.nn.silu(c_ctx)

    for l in range(DEPTH):
        last = l == DEPTH - 1
        mod_l = (s_lat @ w_mod[l] + b_mod[l])[:, None, :]
        mod_c = s_ctx @ w_mod[l] + b_mod[l]
        sh1, sc1, g1, sh2, sc2, g2 = jnp.split(mod_l, 6, axis=-1)
        csh1, csc1, cg1, csh2, csc2, cg2 = jnp.split(mod_c, 6, axis=-1)

        h = _modulate(_rms(x, norm1_g[l]), sh1, sc1)
        hc = _modulate(_rms(ctx, norm1_g[l]), csh1, csc1)
        p = h @ w_in[l]
        pc = hc @ w_in[l]
        mla_w = (q_a_norm_g[l], kv_a_norm_g[l], w_q_up[l], w_kv_up[l], q_norm_g[l], k_norm_g[l])
        q, k, v = _mla_qkv(p, *mla_w, tabs)
        qc, kc, vc = _mla_qkv(pc, *mla_w, None)
        attn_lat = _attend_latent(q, k, v, kc, vc)
        four_lat = _fourier(p[..., OFF_F:OFF_GA])
        x = x + g1 * _merge(p, attn_lat, four_lat, w_o_attn[l], w_fourier[l], w_out[l])

        if not last:
            B = ctx.shape[0]
            attn_ctx = _attend_dense(qc, kc, vc).reshape(B, CTX_LEN, MLA_HEADS * V_DIM)
            four_ctx = _fourier(pc[..., OFF_F:OFF_GA])
            ctx = ctx + cg1 * _merge(pc, attn_ctx, four_ctx, w_o_attn[l], w_fourier[l], w_out[l])

        moe_w = (w_router[l], w_e_gate[l], w_e_up[l], w_e_down[l])
        h2 = _modulate(_rms(x, norm2_g[l]), sh2, sc2)
        x = x + g2 * _expert_choice(h2, *moe_w)
        if not last:
            hc2 = _modulate(_rms(ctx, norm2_g[l]), csh2, csc2)
            ctx = ctx + cg2 * _expert_choice(hc2, *moe_w)
    return x


def setup_inputs(seed=0):
    out = dict(first_inputs(seed))
    for name, value in second_inputs(seed + 1).items():
        if name != "x":
            out[name + "_2"] = value
    return out


def reference(
    x, pre_norm_gain, w_in, rel_bias, rwkv_shift_mix, rwkv_w0, rwkv_w_up, rwkv_a0, rwkv_a_up,
    rwkv_k_k, rwkv_k_a, rwkv_r_k, rwkv_ln_w, rwkv_ln_b, w_up_attn, w_up_rwkv, w_out,
    post_norm_gain, c_2, ctx_2, c_ctx_2, w_mod_2, b_mod_2, norm1_g_2, w_in_2, q_a_norm_g_2,
    kv_a_norm_g_2, w_q_up_2, w_kv_up_2, q_norm_g_2, k_norm_g_2, w_o_attn_2, w_fourier_2,
    w_out_2, norm2_g_2, w_router_2, w_e_gate_2, w_e_up_2, w_e_down_2,
):
    x = first_block(
        x, pre_norm_gain, w_in, rel_bias, rwkv_shift_mix, rwkv_w0, rwkv_w_up, rwkv_a0,
        rwkv_a_up, rwkv_k_k, rwkv_k_a, rwkv_r_k, rwkv_ln_w, rwkv_ln_b, w_up_attn, w_up_rwkv,
        w_out, post_norm_gain,
    )
    return second_block(
        x, c_2, ctx_2, c_ctx_2, w_mod_2, b_mod_2, norm1_g_2, w_in_2, q_a_norm_g_2,
        kv_a_norm_g_2, w_q_up_2, w_kv_up_2, q_norm_g_2, k_norm_g_2, w_o_attn_2, w_fourier_2,
        w_out_2, norm2_g_2, w_router_2, w_e_gate_2, w_e_up_2, w_e_down_2,
    )


_drawn_inputs = setup_inputs


def setup_inputs(seed=0):
    import zlib

    import numpy as np

    out = dict(_drawn_inputs(seed))
    spreads = {}
    factors = {'rwkv_w_up': 3.317,
     'rwkv_ln_b': 7.772,
     'ctx_2': 8.0,
     'c_ctx_2': 8.0,
     'b_mod_2': 6.295,
     'norm1_g_2': 8.0,
     'q_a_norm_g_2': 8.0,
     'kv_a_norm_g_2': 8.0,
     'w_q_up_2': 6.768,
     'q_norm_g_2': 8.0,
     'k_norm_g_2': 8.0,
     'norm2_g_2': 8.0}
    for name, (base, spread) in spreads.items():
        noise = np.random.default_rng([zlib.crc32(name.encode()), seed]).standard_normal(out[name].shape)
        drawn = base * np.exp(spread * noise) if base else spread * noise
        out[name] = __import__('jax').numpy.asarray(drawn.astype(out[name].dtype))
    for name, factor in factors.items():
        out[name] = (out[name] * factor).astype(out[name].dtype)
    return out
```

```python
import math
from contextlib import ExitStack

import numpy as np

import concourse.bass as bass
from concourse import mybir

F32 = mybir.dt.float32
U32 = mybir.dt.uint32
ALU = mybir.AluOpType
ACT = mybir.ActivationFunctionType
X = mybir.AxisListType.X

P = 128
T = 1024
NT = T // P
D = 1024
KD = D // P
HEADS = 8
HD = 64
AW = HEADS * HD
DILATIONS = (1, 4, 16)
STEPS = 128
MASKED = -1e30
QKV = 9 * AW
OFF_Z = QKV
OFF_RWKV = OFF_Z + AW
OFF_ZR = OFF_RWKV + 3 * AW + 128
OFF_MERGE = OFF_ZR + AW
C = 64
SUB = 16
DECAY = math.exp(-0.5)
GN_EPS = 64e-5
EPS = 1e-6
CTX = 256
NTC = CTX // P
QKD, NOPE, ROPE, VD = 96, 64, 32, 64
QL, KVL = 384, 256
OFF_F = QL + KVL + ROPE
OFF_GA = OFF_F + 512
NE, DE, CAP = 16, 512, 128
NKEY = T + CTX
NKT = NKEY // P


def bucket(dist):
    d = np.maximum(np.asarray(dist), 0)
    ratio = np.log(np.maximum(d, 1).astype(np.float32) / 16) / np.float32(math.log(2048 / 16))
    large = np.minimum(16 + (ratio * 16).astype(np.int32), 31)
    return np.where(d < 16, d, large).astype(np.int32)


def stride_of(dil):
    return min(dil, T // P)


def constants():
    f = np.float32
    i = np.arange(P)
    c = {"c_ident": np.eye(P, dtype=f)}
    c["c_hones"] = (i[:, None] // HD == i[None] // HD).astype(f)
    c["c_ones"] = np.ones((P, P), f)
    c["c_resets"] = np.tile((np.arange(T) % C != 0).astype(f), (P, 1))
    same = i[:, None] // C == i[None] // C
    c["c_mask_ar"] = np.concatenate([same & (i[:, None] < i[None]), same & (i[:, None] <= i[None])], 1).astype(f)
    c["c_mask_off"] = (same & (i[:, None] > i[None]) & (i[:, None] // SUB != i[None] // SUB)).astype(f)
    c["c_eye64"] = np.tile(np.eye(C, dtype=f), (2, 1))
    y = np.arange(383)
    rel = 255 - y
    hot = np.zeros((33, 3, 384), f)
    for g, dil in enumerate(DILATIONS):
        step = stride_of(dil)
        valid = (rel >= 0) & (rel * step <= STEPS * dil) & (rel * step % dil == 0)
        b = bucket(np.maximum(rel, 0) * step)
        for n in range(383):
            hot[b[n] if valid[n] else 32, g, n] = 1
    c["c_hot"] = hot
    c["c_eye16"] = np.tile(np.eye(SUB, dtype=f).reshape(1, 1, -1), (P, 4, 1)).reshape(P, -1)
    a = 2 * np.pi * np.outer(i, i) / P
    c["c_dft_ch"] = np.concatenate([np.cos(a), np.sin(a)], 1).astype(f)
    p = np.arange(T // 2)[:, None]
    s = 1 / math.sqrt(T * P)
    pos = np.zeros((T // 2, 2, 2, T // 2), np.float64)
    for par in range(2):
        k = 2 * np.arange(T // 2)[None] + par
        a = 2 * np.pi * ((p * k) % T) / T
        pos[:, par, 0] = np.cos(a) * s
        pos[:, par, 1] = -np.sin(a) * s
    c["c_dft_pos"] = pos.astype(f)
    inv = (1.0 / (np.float32(10000.0) ** (np.arange(8, dtype=f) / 8))).astype(f)
    t = np.arange(T)
    ang = [np.concatenate([q.astype(f)[:, None] * inv] * 2, 1) for q in (t // 64, t % 64)]
    sign = np.concatenate([-np.ones(8), np.ones(8)]).astype(f)
    c["c_rope"] = np.stack([np.concatenate([np.cos(x) for x in ang], 1),
                            np.concatenate([np.sin(x) * sign for x in ang], 1)], 1).astype(f)
    c["c_slot"] = np.tile(np.arange(CAP, dtype=f), (P, 1))
    c["c_tok"] = (np.arange(NT)[None] * P + i[:, None]).astype(f)
    return c


def build(nc, A, out, debug=None):
    ctx = ExitStack()
    sems = {}

    def S(name):
        if name not in sems:
            sems[name] = ctx.enter_context(nc.semaphore(name))
        return sems[name]

    def sb(stack, name, shape, dt=F32):
        return stack.enter_context(nc.sbuf_tensor(name, shape, dt))

    def dram(name, shape, dt=F32):
        return nc.dram_tensor(name, shape, dt, kind="Internal").ap()

    def dump(name, ap):
        if debug is None or name not in debug:
            return
        with nc.Block() as block:
            @block.sync
            def _(sp):
                s = S("dbg")
                debug[name]["n"] = debug["_"] = debug.get("_", 0) + 16
                sp.dma_start(debug[name]["ap"], ap).then_inc(s, 16)
                sp.wait_ge(s, debug["_"])

    class Link:

        def __init__(self, eng, name):
            self.eng, self.sem = eng, S(name)
            self.n = Link.last.get(name, 0)
            self.name = name

        def __call__(self, ins):
            self.n += 1
            Link.last[self.name] = self.n
            ins.then_inc(self.sem, 1)
            self.eng.wait_ge(self.sem, self.n)

    Link.last = {}
    used = {}

    def base(name, count):
        b = used.get(name, 0)
        used[name] = b + count
        return b

    with ctx:
        ps = ctx.enter_context(nc.psum_tensor("ps", [P, 8, 512], F32))
        ident = sb(ctx, "ident", [P, P])
        ones = sb(ctx, "ones", [P, P])
        gains = sb(ctx, "gains", [P, 16, 8])

        def load(pairs):
            with nc.Block() as block:
                @block.sync
                def _(sp):
                    b = base("loaded", 16 * len(pairs))
                    for dst, src in pairs:
                        with nc.allow_non_contiguous_dma("per-channel vectors"):
                            sp.dma_start(dst, src).then_inc(S("loaded"), 16)
                    sp.wait_ge(S("loaded"), b + 16 * len(pairs))

        def start_load(name, pairs):
            b = base(name, 16 * len(pairs))
            with nc.Block() as block:
                @block.sync
                def _(sp):
                    for dst, src in pairs:
                        sp.dma_start(dst, src).then_inc(S(name), 16)
            return b + 16 * len(pairs)

        def vec(ap, n=KD):
            return ap.rearrange("(k p) -> p k", p=P)

        load([(ident[:, :], A["c_ident"]), (ones[:, :], A["c_ones"]),
              (gains[:, 0, :], vec(A["pre_norm_gain"][0]))])

        def gemm(chunks, kt, mode, act, evac, width=512, act_tiles=NT, halves=2, act_only=False):
            groups = []
            for ci, (w, cols) in enumerate(chunks):
                if mode == "T":
                    groups += [(ci, ct, hf) for ct in range(-(-cols // P)) for hf in range(halves)]
                else:
                    groups += [(ci, tt, 0) for tt in range(act_tiles)]
            last_group = {g[0]: n for n, g in enumerate(groups)}
            on_act = [(n % 2 == 0) if act_only is False else bool(act_only) for n in range(len(groups))]
            place = [sum(on_act[:n + 1]) if on_act[n] else n + 1 - sum(on_act[:n + 1])
                     for n in range(len(groups))]
            n_even = sum(on_act)
            n_odd = len(groups) - n_even
            bw = [base(f"gemm_w{b}", 16 * len(range(b, len(chunks), 2))) for b in range(2)]
            bp = base("gemm_mm", len(groups))
            be = base("gemm_ev0", n_even)
            bo = base("gemm_ev1", n_odd)
            with ExitStack() as st:
                wbuf = sb(st, f"wbuf{bp}", [P, 2, kt, width])
                block = st.enter_context(nc.Block())

                @block.sync
                def _(sp):
                    for ci, (w, cols) in enumerate(chunks):
                        if ci >= 2:
                            sp.wait_ge(S("gemm_mm"), bp + last_group[ci - 2] + 1)
                        sp.dma_start(wbuf[:, ci % 2, :, 0:cols], w).then_inc(S(f"gemm_w{ci % 2}"), 16)

                @block.tensor
                def _(pe):
                    seen = -1
                    for n, (ci, m, hf) in enumerate(groups):
                        if ci != seen:
                            pe.wait_ge(S(f"gemm_w{ci % 2}"), bw[ci % 2] + 16 * (ci // 2 + 1))
                            seen = ci
                        if n >= 8:
                            k = n - 8
                            pe.wait_ge(S("gemm_ev0" if on_act[k] else "gemm_ev1"), (be if on_act[k] else bo) + place[k])
                        cols = chunks[ci][1]
                        for k in range(kt):
                            if mode == "T":
                                cw = min(P, cols - m * P)
                                tw = min(512, act.shape[2] - hf * 512)
                                mm = pe.matmul(ps[0:cw, n % 8, 0:tw], wbuf[:, ci % 2, k, m * P:m * P + cw],
                                               act[:, k, hf * 512:hf * 512 + tw], start=(k == 0), stop=(k == kt - 1))
                            else:
                                rows = act(k, m) if callable(act) else act[:, k, m * P:(m + 1) * P]
                                mm = pe.matmul(ps[:, n % 8, 0:cols], rows,
                                               wbuf[:, ci % 2, k, 0:cols], start=(k == 0), stop=(k == kt - 1))
                        mm.then_inc(S("gemm_mm"), 1)

                @block.scalar
                def _(act_e):
                    for n, (ci, m, hf) in enumerate(groups):
                        if on_act[n]:
                            act_e.wait_ge(S("gemm_mm"), bp + n + 1)
                            evac("act", act_e, ps[:, n % 8, :], ci, m, hf).then_inc(S("gemm_ev0"), 1)

                @block.vector
                def _(dve):
                    for n, (ci, m, hf) in enumerate(groups):
                        if not on_act[n]:
                            dve.wait_ge(S("gemm_mm"), bp + n + 1)
                            evac("dve", dve, ps[:, n % 8, :], ci, m, hf).then_inc(S("gemm_ev1"), 1)

        def copy(kind, eng, dst, src):
            if kind == "act":
                return eng.activation(dst, src, ACT.Copy)
            return eng.tensor_copy(dst, src)

        def wcols(w, a, b):
            return w[:, a:b].rearrange("(k p) n -> p k n", p=P)

        def norm_T(src, nt, dstT, gain, shift, rows_out=None, tag="n"):
            with ExitStack() as st:
                xa = sb(st, f"{tag}_x", [P, nt, D])
                sq = sb(st, f"{tag}_sq", [P, D])
                ss = sb(st, f"{tag}_ss", [P, nt])
                bx = base("norm_x", 16)
                bs = base("norm_ss", nt)
                bn = base("norm_xn", nt)
                br = base("norm_root", 1)
                bm = base("norm_mean", 1)
                ng = KD * (-(-nt // 4))
                bt = base("norm_t", ng)
                be = base("norm_ev", ng)
                block = st.enter_context(nc.Block())

                @block.sync
                def _(sp):
                    sp.dma_start(xa[:, :, :], src.rearrange("(t p) d -> p t d", p=P)).then_inc(S("norm_x"), 16)
                    if rows_out is not None:
                        sp.wait_ge(S("norm_xn"), bn + nt)
                        sp.dma_start(rows_out.rearrange("(t p) d -> p t d", p=P), xa[:, :, :]).then_inc(S("norm_out"), 16)
                        sp.wait_ge(S("norm_out"), 16)

                @block.scalar
                def _(act):
                    act.wait_ge(S("norm_x"), bx + 16)
                    for t in range(nt):
                        if t:
                            act.wait_ge(S("norm_ss"), bs + t)
                        act.activation(sq[:, :], xa[:, t, :], ACT.Square,
                                       accum_out=ss[:, t:t + 1]).then_inc(S("norm_ss"), 1)
                    act.wait_ge(S("norm_mean"), bm + 1)
                    act.activation(ss[:, :], ss[:, :], ACT.Sqrt).then_inc(S("norm_root"), 1)

                @block.vector
                def _(dve):
                    link = Link(dve, "dve_link")
                    dve.wait_ge(S("norm_ss"), bs + nt)
                    dve.tensor_scalar(ss[:, :], ss[:, :], 1.0 / D, EPS, ALU.mult, ALU.add).then_inc(S("norm_mean"), 1)
                    dve.wait_ge(S("norm_root"), br + 1)
                    link(dve.reciprocal(ss[:, :], ss[:, :]))
                    for t in range(nt):
                        dve.tensor_scalar(xa[:, t, :], xa[:, t, :], ss[:, t:t + 1], None,
                                          ALU.mult).then_inc(S("norm_xn"), 1)
                    n = 0
                    for q in range(0, nt, 4):
                        w = min(4, nt - q) * P
                        for k in range(KD):
                            dve.wait_ge(S("norm_t"), bt + n + 1)
                            dst = dstT[:, k, q * P:q * P + w]
                            dve.tensor_scalar(dst, ps[:, n % 8, 0:w], gain[:, k:k + 1],
                                              shift[:, k:k + 1] if shift is not None else None,
                                              ALU.mult, ALU.add if shift is not None else ALU.bypass
                                              ).then_inc(S("norm_ev"), 1)
                            n += 1

                @block.tensor
                def _(pe):
                    pe.wait_ge(S("norm_xn"), bn + nt)
                    n = 0
                    for q in range(0, nt, 4):
                        for k in range(KD):
                            if n >= 8:
                                pe.wait_ge(S("norm_ev"), be + n - 7)
                            for j in range(min(4, nt - q)):
                                tr = pe.transpose(ps[:, n % 8, j * P:(j + 1) * P],
                                                  xa[:, q + j, k * P:(k + 1) * P], ident[:, :])
                            tr.then_inc(S("norm_t"), 1)
                            n += 1

        def rwkv():
            low_stack = ExitStack()
            keep = ExitStack()
            kv = sb(keep, "kv", [P, 8, T + 1])
            ar = sb(keep, "ar", [P, 4, NT, 2, P])
            bt = sb(keep, "bt", [P, 4, T])
            bonus = sb(keep, "bonus", [P, 4, T])
            pc = sb(keep, "pc", [P, 4, T // C])
            vecs = sb(keep, "rw_vecs", [P, 8, 4])
            mix = sb(keep, "rw_mix", [P, 13])
            hones = sb(keep, "hones", [P, P])
            rl = sb(low_stack, "rl", [P, 5, T + 1])
            lora = sb(low_stack, "lora", [P, AW])
            resets = sb(low_stack, "resets", [P, T])
            names = ["rwkv_w0", "rwkv_a0", "rwkv_k_k", "rwkv_k_a", None, "rwkv_ln_w", "rwkv_ln_b"]
            pairs = [(vecs[:, i, :], vec(A[n][0], 4)) for i, n in enumerate(names) if n]
            pairs += [(vecs[:, 4, :], vec(A["rwkv_r_k"][0].rearrange("h n -> (h n)"), 4)),
                      (mix[:, :], vec(A["rwkv_shift_mix"][0], 13)), (hones[:, :], A["c_hones"]),
                      (resets[:, :], A["c_resets"]),
                      (lora[0:64, :], A["rwkv_w_up"][0]), (lora[64:P, :], A["rwkv_a_up"][0])]
            load(pairs)

            def place_of(c):
                return rl[:, c, :] if c < 4 else rl[:, 4, :] if c == 12 else kv[:, c - 4, :]

            gemm([(wcols(w_in, OFF_RWKV + 512 * i, OFF_RWKV + 512 * (i + 1)), 512) for i in range(3)]
                 + [(wcols(w_in, OFF_RWKV + 1536, OFF_RWKV + 1664), 128)], KD, "T", hT,
                 lambda kind, eng, src, ci, ct, hf: copy(
                     kind, eng, place_of(4 * ci + ct)[:, 1 + hf * 512:513 + hf * 512], src))

            with ExitStack() as st:
                diff = sb(st, "diff", [P, T])
                block = st.enter_context(nc.Block())

                @block.vector
                def _(dve):
                    link = Link(dve, "dve_link")
                    dve.memset(rl[:, :, 0:1], 0.0)
                    link(dve.memset(kv[:, :, 0:1], 0.0))
                    link(dve.tensor_scalar(vecs[:, 7, :], vecs[:, 3, :], -1.0, 1.0, ALU.mult, ALU.add))
                    for c in range(13):
                        pr = place_of(c)
                        link(dve.tensor_tensor(diff[:, :], pr[:, 0:T], pr[:, 1:T + 1], ALU.subtract))
                        link(dve.scalar_tensor_tensor(pr[:, 1:T + 1], diff[:, :], mix[:, c:c + 1],
                                                      pr[:, 1:T + 1], ALU.mult, ALU.add))

            with ExitStack() as st:
                def t_(n):
                    return sb(st, "rw_" + n, [P, T])
                sig, a, cs, csm, pi, kk, w1, w2 = map(t_, ["sig", "a", "cs", "csm", "pi", "kk", "w1", "w2"])
                pr_, pp = sig, csm
                block = st.enter_context(nc.Block())
                pair = lambda b: ps[:, b:b + 2, :].rearrange("p a b -> p (a b)")

                @block.tensor
                def _(pe):
                    pe.wait_ge(S("rw_tanh"), 1)
                    for c in range(4):
                        if c:
                            pe.wait_ge(S("rw_sig"), 2 * c)
                        for hf in range(2):
                            cols = slice(1 + hf * 512, 513 + hf * 512)
                            pe.matmul(ps[:, hf, :], lora[0:64, c * P:(c + 1) * P], rl[0:64, 4, cols],
                                      start=True, stop=True)
                            mm = pe.matmul(ps[:, 2 + hf, :], lora[64:P, c * P:(c + 1) * P], rl[64:P, 4, cols],
                                           start=True, stop=True)
                        mm.then_inc(S("rw_lora"), 1)
                        for name, src, b in (("rw_ksq", w1, 4), ("rw_rk", w2, 6)):
                            pe.wait_ge(S(name), c + 1)
                            for hf in range(2):
                                mm = pe.matmul(ps[:, b + hf, :], hones[:, :], src[:, hf * 512:(hf + 1) * 512],
                                               start=True, stop=True)
                            mm.then_inc(S(name + "_sum"), 1)

                @block.scalar
                def _(act):
                    act.activation(rl[0:64, 4, 1:T + 1], rl[0:64, 4, 1:T + 1], ACT.Tanh).then_inc(S("rw_tanh"), 1)
                    for c in range(4):
                        act.wait_ge(S("rw_lora"), c + 1)
                        if c:
                            act.wait_ge(S("rw_tile"), c)
                        act.activation(sig[:, :], pair(0), ACT.Sigmoid, bias=vecs[:, 0, c:c + 1]).then_inc(S("rw_sig"), 1)
                        act.activation(a[:, :], pair(2), ACT.Sigmoid, bias=vecs[:, 1, c:c + 1]).then_inc(S("rw_sig"), 1)
                        act.wait_ge(S("rw_cs"), c + 1)
                        act.activation(pr_[:, :], cs[:, :], ACT.Exp, scale=-DECAY).then_inc(S("rw_exp"), 1)
                        act.activation(pi[:, :], cs[:, :], ACT.Exp, scale=DECAY).then_inc(S("rw_exp"), 1)
                        act.activation(pp[:, :], csm[:, :], ACT.Exp, scale=-DECAY).then_inc(S("rw_exp"), 1)
                        act.wait_ge(S("rw_nrm"), c + 1)
                        act.activation(w1[:, :], w1[:, :], ACT.Sqrt).then_inc(S("rw_root"), 1)

                @block.vector
                def _(dve):
                    link = Link(dve, "dve_link")
                    for c in range(4):
                        k_ = kv[:, c, 1:T + 1]
                        v_ = kv[:, 4 + c, 1:T + 1]
                        r_ = rl[:, c, 1:T + 1]
                        by_tile = lambda ap: ap.rearrange("p (n t) -> p n t", t=P)
                        link(dve.tensor_scalar(kk[:, :], k_, vecs[:, 2, c:c + 1], None, ALU.mult))
                        dve.tensor_tensor(w1[:, :], kk[:, :], kk[:, :], ALU.mult).then_inc(S("rw_ksq"), 1)
                        dve.wait_ge(S("rw_sig"), 2 * c + 2)
                        link(dve.tensor_tensor_scan(cs[:, :], resets[:, :], sig[:, :], 0.0, ALU.mult, ALU.add))
                        dve.tensor_tensor(csm[:, :], cs[:, :], sig[:, :], ALU.subtract).then_inc(S("rw_cs"), 1)
                        dve.wait_ge(S("rw_ksq_sum"), c + 1)
                        dve.tensor_scalar(w1[:, :], pair(4), 1e-24, None, ALU.max).then_inc(S("rw_nrm"), 1)
                        link(dve.tensor_scalar(w2[:, :], a[:, :], vecs[:, 3, c:c + 1], vecs[:, 7, c:c + 1],
                                               ALU.mult, ALU.add))
                        link(dve.tensor_tensor(k_, k_, w2[:, :], ALU.mult))
                        link(dve.scalar_tensor_tensor(w2[:, :], r_, vecs[:, 4, c:c + 1], k_, ALU.mult, ALU.mult))
                        dve.engine_nop().then_inc(S("rw_rk"), 1)
                        dve.wait_ge(S("rw_exp"), 3 * c + 3)
                        dve.tensor_tensor(by_tile(k_), by_tile(k_), by_tile(pi[:, :]), ALU.mult)
                        dve.tensor_tensor(ar[:, c, :, 1, :], by_tile(r_), by_tile(pr_[:, :]), ALU.mult)
                        dve.tensor_copy(pc[:, c, :], pr_[:, C - 1:T:C])
                        dve.wait_ge(S("rw_root"), c + 1)
                        link(dve.reciprocal(w1[:, :], w1[:, :]))
                        link(dve.tensor_tensor(kk[:, :], kk[:, :], w1[:, :], ALU.mult))
                        dve.scalar_tensor_tensor(ar[:, c, :, 0, :], by_tile(kk[:, :]), -1.0, by_tile(pp[:, :]),
                                                 ALU.mult, ALU.mult)
                        link(dve.tensor_tensor(w1[:, :], kk[:, :], a[:, :], ALU.mult))
                        dve.tensor_tensor(bt[:, c, :], w1[:, :], pi[:, :], ALU.mult)
                        dve.wait_ge(S("rw_rk_sum"), c + 1)
                        dve.tensor_tensor(bonus[:, c, :], pair(6), v_, ALU.mult).then_inc(S("rw_tile"), 1)
                        dve.wait_ge(S("rw_tile"), c + 1)
            low_stack.close()
            dump("ar", ar[:, :, :, :, :].rearrange("p a b c d -> p (a b c d)"))
            dump("bt", bt[:, :, :])
            dump("bonus", bonus[:, :, :])

            l_d = dram("rw_l", [NT * HEADS, P, P])
            w_d = dram("rw_w", [P, 4 * SUB * SUB])
            masks = sb(keep, "rw_masks", [P, 4, P])
            eye64 = sb(keep, "eye64", [P, C])
            load([(masks[:, 0, :], A["c_mask_off"]), (masks[:, 1, :], A["c_mask_ar"][:, P:2 * P]),
                  (masks[:, 2, :], A["c_mask_ar"][:, 0:P]), (masks[:, 3, :], A["c_mask_ar"][:, P:2 * P]),
                  (eye64[:, :], A["c_eye64"])])
            with ExitStack() as st:
                lbuf = sb(st, "lbuf", [P, 2, HEADS, P])
                lt = sb(st, "lt", [P, 4, SUB, SUB])
                wt = sb(st, "wt", [P, 4, SUB, SUB])
                tmp = sb(st, "wtmp", [P, 4 * SUB * SUB])
                block = st.enter_context(nc.Block())

                @block.tensor
                def _(pe):
                    for tt in range(NT):
                        if tt >= 4:
                            pe.wait_ge(S("rw_lev"), 2 * (tt - 3))
                        for h in range(HEADS):
                            rows = slice(64 * (h % 2), 64 * (h % 2) + 64)
                            mm = pe.matmul(ps[:, 2 * (tt % 4) + h % 2, (h // 2) * P:(h // 2 + 1) * P],
                                           bt[rows, h // 2, tt * P:(tt + 1) * P], ar[rows, h // 2, tt, 0, :],
                                           start=True, stop=True)
                        mm.then_inc(S("rw_lmm"), 1)

                @block.vector
                def _(dve):
                    link = Link(dve, "dve_link")
                    for tt in range(NT):
                        dve.wait_ge(S("rw_lmm"), tt + 1)
                        if tt >= 2:
                            dve.wait_ge(S(f"rw_ldump{tt % 2}"), 16 * (tt // 2))
                        for par in range(2):
                            dve.tensor_tensor(lbuf[:, tt % 2, par::2, :],
                                              ps[:, 2 * (tt % 4) + par, :].rearrange("p (h t) -> p h t", t=P),
                                              masks[:, 2:3, :].to_broadcast([P, 4, P]),
                                              ALU.mult).then_inc(S("rw_lev"), 1)
                    dve.wait_ge(S("rw_lin"), 16 * 9)
                    for t in range(1, SUB):
                        v = tmp[:, 0:4 * t * t].rearrange("p (b j s) -> p b j s", b=4, j=t)
                        coef = lt[:, :, 0:t, t:t + 1].rearrange("p b s o -> p b o s").to_broadcast([P, 4, t, t])
                        if t == 1:
                            link(dve.tensor_copy(wt[:, :, 0, 1], lt[:, :, 0, 1]))
                            continue
                        link(dve.tensor_tensor(v, wt[:, :, 0:t, 0:t], coef, ALU.mult))
                        link(dve.tensor_reduce(wt[:, :, 0:t, t], v, X, ALU.add))
                    dve.engine_nop().then_inc(S("rw_inv"), 1)

                @block.sync
                def _(sp):
                    sp.dma_start(wt[:, :, :, :].rearrange("p a b c -> p (a b c)"), A["c_eye16"]).then_inc(S("rw_lin"), 16)
                    for tt in range(NT):
                        sp.wait_ge(S("rw_lev"), 2 * tt + 2)
                        sp.dma_start(l_d[tt * HEADS:(tt + 1) * HEADS].rearrange("h s t -> s h t"),
                                     lbuf[:, tt % 2, :, :]).then_inc(S(f"rw_ldump{tt % 2}"), 16)
                    for b in range(2):
                        sp.wait_ge(S(f"rw_ldump{b}"), 16 * NT // 2)
                    for half in range(2):
                        for blk in range(4):
                            o = half * 64 + blk * SUB
                            sp.dma_start(lt[half * 64:half * 64 + 64, blk, :, :],
                                         l_d[:, o:o + SUB, o:o + SUB]).then_inc(S("rw_lin"), 16)
                    sp.wait_ge(S("rw_inv"), 1)
                    sp.dma_start(w_d, wt[:, :, :, :].rearrange("p a b c -> p (a b c)")).then_inc(S("rw_wout"), 16)
                    sp.wait_ge(S("rw_wout"), 16)

            with ExitStack() as st:
                ti = sb(st, "ti", [P, 2, HEADS, P])
                m = sb(st, "rw_m", [P, 4, 4, P])
                rhs = sb(st, "rw_rhs", [P, 4, 2 * C])
                tb = sb(st, "rw_tb", [P, 4, C])
                tkv = sb(st, "rw_tkv", [P, 2, 4, C])
                ft = sb(st, "rw_ft", [P, 4, P])
                z = sb(st, "rw_z", [P, 4, P])
                xb = sb(st, "rw_x", [P, 2, 4, P])
                gb = sb(st, "rw_gb", [P, 2, 2, C])
                hb = sb(st, "rw_hb", [P, 2, 2, C])
                qb = sb(st, "rw_qb", [P, 2, P])
                yi = sb(st, "rw_yi", [P, 2, P])
                state = sb(st, "rw_state", [P, 3, 4, C])
                s1 = sb(st, "rw_s1", [P, 2, C])
                gw = sb(st, "gate_w", [P, 3, KD, P])
                go = sb(st, "gate_out", [P, 2, 512])
                w_v = w_d.rearrange("(x u) (b s t) -> x b s u t", x=2, b=4, s=SUB)
                block = st.enter_context(nc.Block())
                rounds = [(tt, rd) for tt in range(NT) for rd in range(2)]
                GATES = 24
                assert 2 * GATES == 3 * len(rounds)

                @block.sync
                def _(sp):
                    def blocks(tt):
                        for half in range(2):
                            for blk in range(4):
                                o = half * 64 + blk * SUB
                                sp.dma_start(ti[o:o + SUB, tt % 2, :, o:o + SUB],
                                             w_v[half, blk, :, tt * HEADS:(tt + 1) * HEADS, :]
                                             ).then_inc(S(f"rw_ti{tt % 2}"), 16)

                    def gate_weights(m):
                        off = (OFF_ZR + m * P, OFF_Z + (m - 4) * P, OFF_MERGE + (m - 8) * P)[min(m // 4, 2)]
                        sp.dma_start(gw[:, m % 3], wcols(w_in, off, off + P)).then_inc(S(f"gate_w{m % 3}"), 16)

                    sp.wait_ge(S("rw_zeroed"), 2)
                    blocks(0)
                    for m in range(3):
                        gate_weights(m)
                    for r in range(len(rounds)):
                        if r % 2 == 0 and r // 2 + 1 < NT:
                            if r:
                                sp.wait_ge(S("rw_ymm"), r)
                            blocks(r // 2 + 1)
                        for n in range(3 * r, 3 * r + 3):
                            m, hf = divmod(n, 2)
                            sp.wait_ge(S("gate_ev"), n + 1)
                            sp.dma_start(gates_d[:, m, hf * 512:(hf + 1) * 512], go[:, n % 2, :]
                                         ).then_inc(S(f"gate_out{n % 2}"), 16)
                            if hf == 1 and m + 3 < GATES:
                                gate_weights(m + 3)
                    for x in range(2):
                        sp.wait_ge(S(f"gate_out{x}"), 16 * GATES)

                @block.tensor
                def _(pe):
                    queue = [(n, k) for n in range(2 * GATES) for k in range(KD)]

                    def gate_products(count):
                        for _i in range(count):
                            n, k = queue.pop(0)
                            m, hf = divmod(n, 2)
                            if k == 0:
                                pe.wait_ge(S(f"gate_w{m % 3}"), 16 * (m // 3 + 1))
                                if n:
                                    pe.wait_ge(S("gate_ev"), n)
                            mm = pe.matmul(ps[:, 7, :], gw[:, m % 3, k, :], hT[:, k, hf * 512:(hf + 1) * 512],
                                           start=(k == 0), stop=(k == KD - 1))
                            if k == KD - 1:
                                mm.then_inc(S("gate_mm"), 1)

                    for r, (tt, rd) in enumerate(rounds):
                        tok = slice(tt * P, (tt + 1) * P)
                        pe.wait_ge(S("rw_y"), r) if r else None
                        for cc in range(2):
                            c = 2 * rd + cc
                            pe.transpose(ps[:, 0, cc * P:(cc + 1) * P], ar[:, c, tt, 0, :], ident[:, :])
                            pe.transpose(ps[:, 0, 256 + cc * P:256 + (cc + 1) * P], bt[:, c, tok], ident[:, :])
                            pe.transpose(ps[:, 1, cc * P:(cc + 1) * P],
                                         kv[:, c, 1 + tt * P:1 + (tt + 1) * P], ident[:, :])
                            tr = pe.transpose(ps[:, 1, 256 + cc * P:256 + (cc + 1) * P],
                                              kv[:, 4 + c, 1 + tt * P:1 + (tt + 1) * P], ident[:, :])
                        tr.then_inc(S("rw_tr"), 1)
                        for hh in range(4):
                            c, rows = 2 * rd + hh // 2, slice(64 * (hh % 2), 64 * (hh % 2) + 64)
                            b_, k_ = bt[rows, c, tok], kv[rows, c, 1 + tt * P:1 + (tt + 1) * P]
                            pe.matmul(ps[:, 2 + hh, 0:P], ar[rows, c, tt, 0, :], b_, start=True, stop=True)
                            pe.matmul(ps[:, 2 + hh, P:2 * P], b_, ar[rows, c, tt, 1, :], start=True, stop=True)
                            mm = pe.matmul(ps[:, 2 + hh, 2 * P:4 * P], k_,
                                           ar[rows, c, tt, :, :].rearrange("p a b -> p (a b)"),
                                           start=True, stop=True)
                            mm.then_inc(S("rw_mat"), 1)
                        gate_products(3)
                        pe.wait_ge(S("rw_tok"), 3 * r + 3)
                        pe.wait_ge(S("rw_m"), 4 * r + 4)
                        pe.wait_ge(S(f"rw_ti{tt % 2}"), 128 * (tt // 2 + 1))
                        for hh in range(4):
                            pe.matmul(ps[:, 6, hh * C:(hh + 1) * C], m[:, hh, 2, :], tkv[:, 1, hh, :],
                                      start=True, stop=True)
                            mm = pe.matmul(ps[:, 2, hh * P:(hh + 1) * P], m[:, hh, 0, :], ti[:, tt % 2, 4 * rd + hh, :],
                                           start=True, stop=True)
                        mm.then_inc(S("rw_kav"), 1)
                        gate_products(3)
                        pe.wait_ge(S("rw_kf"), 2 * r + 2)
                        for hh in range(4):
                            mm = pe.matmul(ps[:, 0, hh * P:(hh + 1) * P], ti[:, tt % 2, 4 * rd + hh, :], rhs[:, hh, :],
                                           start=True, stop=True)
                        mm.then_inc(S("rw_zmm"), 1)
                        gate_products(2)
                        for i in range(3):
                            pe.wait_ge(S("rw_x"), 4 * r + i + 1)
                            src = z if i == 0 else xb[:, (i - 1) % 2]
                            for hh in range(4):
                                mm = pe.matmul(ps[:, 1 + i, hh * P:(hh + 1) * P], ft[:, hh, :], src[:, hh, :],
                                               start=True, stop=True)
                            mm.then_inc(S("rw_xmm"), 1)
                            gate_products(2 if i == 2 else 3)
                        pe.wait_ge(S("rw_x"), 4 * r + 4)
                        xf = xb[:, 0]
                        for hh in range(4):
                            cc, o = hh // 2, 64 * (hh % 2)
                            out_ = slice(o, o + 64)
                            for half in range(2):
                                t_ = slice(64 * half, 64 * half + 64)
                                pe.matmul(ps[out_, 4 + half, cc * C:(cc + 1) * C], xf[t_, hh, 0:C], tb[t_, hh, :],
                                          start=True, stop=True)
                                h_ = ps[out_, 4 + half, 128 + cc * C:128 + (cc + 1) * C]
                                pe.matmul(h_, tb[t_, hh, :], xf[t_, hh, C:2 * C], start=True, stop=False)
                                pe.matmul(h_, tkv[t_, 0, hh, :], tkv[t_, 1, hh, :], start=False, stop=True)
                            pe.matmul(ps[out_, 6, cc * P:(cc + 1) * P], xf[:, hh, 0:C], m[:, hh, 1, :],
                                      start=True, stop=True)
                            y_ = ps[out_, 1, 256 + cc * P:256 + (cc + 1) * P]
                            pe.matmul(y_, xf[:, hh, C:2 * C], m[:, hh, 1, :], start=True, stop=False)
                            mm = pe.matmul(y_, tkv[:, 1, hh, :], m[:, hh, 3, :], start=False, stop=True)
                        mm.then_inc(S("rw_gmm"), 1)
                        gate_products(3)
                        pe.wait_ge(S("rw_gq"), 3 * r + 3)
                        pe.wait_ge(S("rw_zeroed"), 2)
                        for half in range(2):
                            n = 2 * tt + half
                            if half:
                                pe.wait_ge(S("rw_st"), 2 * r + 1)
                            for hh in range(4):
                                cc, o = hh // 2, 64 * (hh % 2)
                                o = slice(o, o + 64)
                                mm = pe.matmul(ps[o, 2 + half, cc * C:(cc + 1) * C], gb[o, half, cc, :],
                                               state[o, n % 3, 2 * rd + cc, :], start=True, stop=True)
                            mm.then_inc(S("rw_cmm"), 1)
                            gate_products(3 if half == 0 else 0)
                            for hh in range(4):
                                cc, o = hh // 2, 64 * (hh % 2)
                                o = slice(o, o + 64)
                                mm = pe.matmul(ps[o, 0, cc * P + half * C:cc * P + half * C + C],
                                               state[o, n % 3, 2 * rd + cc, :], qb[o, cc, half * C:(half + 1) * C],
                                               start=True, stop=True)
                        mm.then_inc(S("rw_ymm"), 1)
                        gate_products(2)

                @block.scalar
                def _(act):
                    def gate_out(n):
                        act.wait_ge(S("gate_mm"), n + 1)
                        if n >= 2:
                            act.wait_ge(S(f"gate_out{n % 2}"), 16 * (n // 2))
                        act.activation(go[:, n % 2, :], ps[:, 7, :], ACT.Silu if n < 16 else ACT.Sigmoid
                                       ).then_inc(S("gate_ev"), 1)

                    for r, (tt, rd) in enumerate(rounds):
                        act.wait_ge(S("rw_tr"), r + 1)
                        act.activation(rhs[:, :, 0:C], ps[:, 0, 0:256].rearrange("p (h c) -> p h c", c=C),
                                       ACT.Copy).then_inc(S("rw_tok"), 1)
                        act.activation(tb[:, :, :].rearrange("p h c -> p (h c)"), ps[:, 0, 256:512],
                                       ACT.Copy).then_inc(S("rw_tok"), 1)
                        act.activation(tkv[:, :, :, :].rearrange("p a h c -> p (a h c)"), ps[:, 1, :],
                                       ACT.Copy).then_inc(S("rw_tok"), 1)
                        act.wait_ge(S("rw_kav"), r + 1)
                        act.activation(rhs[:, :, C:2 * C], ps[:, 6, 0:256].rearrange("p (h c) -> p h c", c=C),
                                       ACT.Copy).then_inc(S("rw_kf"), 1)
                        act.activation(ft[:, :, :].rearrange("p h t -> p (h t)"), ps[:, 2, :],
                                       ACT.Copy).then_inc(S("rw_kf"), 1)
                        gate_out(3 * r)
                        gate_out(3 * r + 1)
                        act.wait_ge(S("rw_gmm"), r + 1)
                        act.activation(yi[:, :, :].rearrange("p a t -> p (a t)"), ps[:, 1, 256:512],
                                       ACT.Copy).then_inc(S("rw_yi"), 1)
                        gate_out(3 * r + 2)

                @block.vector
                def _(dve):
                    link = Link(dve, "dve_link")
                    dve.memset(ti[:, :, :, :], 0.0).then_inc(S("rw_zeroed"), 1)
                    dve.memset(state[:, 0, :, :], 0.0).then_inc(S("rw_zeroed"), 1)
                    for r, (tt, rd) in enumerate(rounds):
                        for hh in range(4):
                            dve.wait_ge(S("rw_mat"), 4 * r + hh + 1)
                            dve.tensor_tensor(m[:, hh, :, :].rearrange("p a t -> p (a t)"), ps[:, 2 + hh, :],
                                              masks[:, :, :].rearrange("p a t -> p (a t)"),
                                              ALU.mult).then_inc(S("rw_m"), 1)
                        dve.wait_ge(S("rw_zmm"), r + 1)
                        flat = lambda ap: ap.rearrange("p h t -> p (h t)")
                        dve.tensor_copy(flat(z[:, :, :]), ps[:, 0, :]).then_inc(S("rw_x"), 1)
                        dve.wait_ge(S("rw_x"), 4 * r + 1)
                        for i in range(3):
                            dve.wait_ge(S("rw_xmm"), 3 * r + i + 1)
                            dve.tensor_tensor(flat(xb[:, i % 2]), ps[:, 1 + i, :], flat(z[:, :, :]),
                                              ALU.add).then_inc(S("rw_x"), 1)
                        dve.wait_ge(S("rw_gmm"), r + 1)
                        dve.tensor_tensor(gb[:, :, :, :], ps[:, 4:6, 0:P].rearrange("p a (c k) -> p a c k", k=C),
                                          eye64[:, :].unsqueeze(1).unsqueeze(1).to_broadcast([P, 2, 2, C]),
                                          ALU.add).then_inc(S("rw_gq"), 1)
                        dve.tensor_copy(hb[:, :, :, :].rearrange("p a c k -> p a (c k)"),
                                        ps[:, 4:6, P:2 * P]).then_inc(S("rw_gq"), 1)
                        dve.tensor_tensor(qb[:, :, :], ps[:, 6, 0:256].rearrange("p (c t) -> p c t", t=P),
                                          ar[:, 2 * rd:2 * rd + 2, tt, 1, :], ALU.add).then_inc(S("rw_gq"), 1)
                        dve.wait_ge(S("rw_gq"), 3 * r + 3)
                        for half in range(2):
                            n = 2 * tt + half
                            dve.wait_ge(S("rw_cmm"), 2 * r + half + 1)
                            link(dve.tensor_tensor(s1[:, :, :], ps[:, 2 + half, 0:P].rearrange("p (c k) -> p c k", k=C),
                                                   hb[:, half, :, :], ALU.add))
                            dve.tensor_tensor(state[:, (n + 1) % 3, 2 * rd:2 * rd + 2, :], s1[:, :, :],
                                              pc[:, 2 * rd:2 * rd + 2, n:n + 1].to_broadcast([P, 2, C]),
                                              ALU.mult).then_inc(S("rw_st"), 1)
                        dve.wait_ge(S("rw_ymm"), r + 1)
                        dve.wait_ge(S("rw_yi"), r + 1)
                        dve.tensor_tensor(ozr[:, 2 * rd:2 * rd + 2, tt * P:(tt + 1) * P],
                                          ps[:, 0, 0:256].rearrange("p (c t) -> p c t", t=P), yi[:, :, :],
                                          ALU.add).then_inc(S("rw_y"), 1)
            dump("y", ozr[:, :, :])

            with ExitStack() as st:
                sq = sb(st, "gn_sq", [P, 4, T])
                rs = sb(st, "gn_rs", [P, 4, T])
                block = st.enter_context(nc.Block())
                pair = lambda b: ps[:, b:b + 2, :].rearrange("p a b -> p (a b)")

                @block.tensor
                def _(pe):
                    for i, src in enumerate((ozr, sq)):
                        if i:
                            pe.wait_ge(S("gn_sq"), 4)
                        for c in range(4):
                            for hf in range(2):
                                mm = pe.matmul(ps[:, 2 * c + hf, :], hones[:, :], src[:, c, hf * 512:(hf + 1) * 512],
                                               start=True, stop=True)
                            mm.then_inc(S("gn_sum"), 1)

                @block.scalar
                def _(act):
                    for c in range(4):
                        act.wait_ge(S("gn_c"), c + 1)
                        act.activation(sq[:, c, :], ozr[:, c, :], ACT.Square).then_inc(S("gn_sq"), 1)
                    act.wait_ge(S("gn_v"), 4)
                    act.activation(rs[:, :, :], rs[:, :, :], ACT.Sqrt).then_inc(S("gn_root"), 1)

                @block.vector
                def _(dve):
                    link = Link(dve, "dve_link")
                    for c in range(4):
                        dve.wait_ge(S("gn_sum"), c + 1)
                        dve.scalar_tensor_tensor(ozr[:, c, :], pair(2 * c), -1.0 / HD, ozr[:, c, :],
                                                 ALU.mult, ALU.add).then_inc(S("gn_c"), 1)
                    for c in range(4):
                        dve.wait_ge(S("gn_sum"), 5 + c)
                        dve.tensor_scalar(rs[:, c, :], pair(2 * c), 1.0 / HD, GN_EPS, ALU.mult, ALU.add
                                          ).then_inc(S("gn_v"), 1)
                    dve.wait_ge(S("gn_root"), 1)
                    link(dve.reciprocal(rs[:, :, :], rs[:, :, :]))
                    for c in range(4):
                        link(dve.tensor_tensor(ozr[:, c, :], ozr[:, c, :], rs[:, c, :], ALU.mult))
                        link(dve.tensor_scalar(ozr[:, c, :], ozr[:, c, :], vecs[:, 5, c:c + 1], vecs[:, 6, c:c + 1],
                                               ALU.mult, ALU.add))
                        link(dve.tensor_tensor(ozr[:, c, :], ozr[:, c, :], bonus[:, c, :], ALU.add))
            dump("ozr", ozr[:, :, :])
            keep.close()

        def attention():
            ag_d = dram("attn_groups", [3, T, 528])
            lines_d = dram("bias_lines", [3, HEADS, P, 384])
            REC = 528
            with ExitStack() as st:
                tab = sb(st, "rel_tab", [33, 24])
                tabw = sb(st, "rel_tabw", [33, 24, P])
                hot = sb(st, "hot", [33, 3, 384])
                line = sb(st, "line", [P, 24, 384])
                load([(tab[0:32, :], A["rel_bias"]), (hot[:, :, :], A["c_hot"])])
                block = st.enter_context(nc.Block())

                @block.vector
                def _(dve):
                    link = Link(dve, "dve_link")
                    link(dve.memset(tab[32:33, :], MASKED))
                    dve.tensor_copy(tabw[:, :, :], tab[:, :].unsqueeze(2).to_broadcast([33, 24, P])
                                    ).then_inc(S("at_tab"), 1)
                    for n in range(1, 24, 2):
                        dve.wait_ge(S("at_line_mm"), n + 1)
                        dve.tensor_copy(line[:, n, :], ps[:, n % 8, 0:384]).then_inc(S("at_line1"), 1)

                @block.scalar
                def _(act):
                    for n in range(0, 24, 2):
                        act.wait_ge(S("at_line_mm"), n + 1)
                        act.activation(line[:, n, :], ps[:, n % 8, 0:384], ACT.Copy).then_inc(S("at_line0"), 1)

                @block.tensor
                def _(pe):
                    pe.wait_ge(S("at_tab"), 1)
                    for n in range(24):
                        if n >= 8:
                            pe.wait_ge(S(f"at_line{n % 2}"), (n - 8) // 2 + 1)
                        pe.matmul(ps[:, n % 8, 0:384], tabw[:, n, :], hot[:, n // 8, :],
                                  start=True, stop=True).then_inc(S("at_line_mm"), 1)

                @block.sync
                def _(sp):
                    for g in range(3):
                        for x in range(2):
                            sp.wait_ge(S(f"at_line{x}"), 4 * g + 4)
                        sp.dma_start(lines_d[g].rearrange("h q y -> q h y"), line[:, g * HEADS:(g + 1) * HEADS, :]
                                     ).then_inc(S("at_line_out"), 16)
                    sp.wait_ge(S("at_line_out"), 48)

            for g, dil in enumerate(DILATIONS):
                step = stride_of(dil)
                length = T // step
                with ExitStack() as gst:
                    qk = sb(gst, f"qk{g}", [P, 8, T])
                    v = sb(gst, f"v{g}", [P, NT, AW])
                    off = [(which * 3 + g) * AW for which in range(3)]

                    def put_qk(kind, eng, src, ci, ct, hf, step=step, qk=qk):
                        w = 512 // step
                        dst = qk[:, 4 * ci + ct, :].rearrange("p (r i) -> p i r", r=step)[:, hf * w:(hf + 1) * w, :]
                        return copy(kind, eng, dst, src.rearrange("p (i r) -> p i r", r=step))
                    gemm([(wcols(w_in, off[i], off[i] + AW), AW) for i in range(2)], KD, "T", hT, put_qk)
                    by_residue = hT[:, :, :].rearrange("p k (i r) -> p k r i", r=step)

                    def v_tokens(k, m, length=length, by_residue=by_residue):
                        r, i0 = divmod(m * P, length)
                        return by_residue[:, k, r, i0:i0 + P]
                    gemm([(wcols(w_in, off[2], off[2] + AW), AW)], KD, "N", v_tokens,
                         lambda kind, eng, src, ci, tt, hf: copy(kind, eng, v[:, tt, :], src))
                    bias = sb(gst, f"bias{g}", [P, 2, 4, 2 * P])
                    sbuf = sb(gst, f"sc{g}", [P, 2, 2, 4, 2 * P])
                    pt = sb(gst, f"pt{g}", [P, 2, 2, 2, 4, P])
                    og = sb(gst, f"og{g}", [P, 2, REC])
                    nkey = [2 if (j * P) % length and length > P else 1 for j in range(NT)]
                    ngrp = [2 * n for n in nkey]
                    gsum = [sum(ngrp[:j]) for j in range(NT + 1)]
                    load([(bias[:, par, :, :],
                           bass.AP(tensor=lines_d.tensor, offset=(g * HEADS + par) * P * 384 + 127,
                                   ap=[[383, P], [2 * P * 384, 4], [1, 2 * P]])) for par in range(2)])
                    block = gst.enter_context(nc.Block())
                    sn = {n: S(f"at_{n}") for n in ("sc", "sb", "exp", "tr", "pt0", "pt1", "pv", "og", "out0", "out1", "nm")}
                    bs = {"sc": base("at_sc", NT), "sb": base("at_sb", NT), "exp": base("at_exp", NT),
                          "tr": base("at_tr", gsum[NT]), "pt0": base("at_pt0", gsum[NT] // 2),
                          "pt1": base("at_pt1", gsum[NT] // 2), "pv": base("at_pv", NT),
                          "og": base("at_og", NT), "nm": base("at_nm", NT),
                          "out0": base("at_out0", 16 * NT // 2), "out1": base("at_out1", 16 * NT // 2)}
                    gv = ag_d[g].rearrange("(i r) c -> r i c", r=step)

                    @block.tensor
                    def _(pe):
                        def scores(j):
                            if j:
                                pe.wait_ge(sn["sb"], bs["sb"] + j)
                            k0 = (j + 1 - nkey[j]) * P
                            for h in range(HEADS):
                                rows = slice(64 * (h % 2), 64 * (h % 2) + 64)
                                w = nkey[j] * P
                                bank, o = 2 * (h % 2) + (h // 2) // 2, ((h // 2) % 2) * 256 + 256 - w
                                mm = pe.matmul(ps[:, bank, o:o + w], qk[rows, h // 2, j * P:(j + 1) * P],
                                               qk[rows, 4 + h // 2, k0:k0 + w], start=True, stop=True)
                            mm.then_inc(sn["sc"], 1)

                        scores(0)
                        for j in range(NT):
                            if j + 1 < NT:
                                scores(j + 1)
                            pe.wait_ge(sn["exp"], bs["exp"] + j + 1)
                            for n in range(ngrp[j]):
                                kb, par = n // 2, n % 2
                                w = gsum[j] + n
                                if w >= 3:
                                    pe.wait_ge(sn[f"pt{(w - 3) % 2}"], bs[f"pt{(w - 3) % 2}"] + (w - 3) // 2 + 1)
                                o = (2 - nkey[j] + kb) * P
                                for hh in range(4):
                                    tr = pe.transpose(ps[:, 4 + w % 3, hh * P:(hh + 1) * P],
                                                      sbuf[:, j % 2, par, hh, o:o + P], ident[:, :])
                                tr.then_inc(sn["tr"], 1)
                            for x in range(2):
                                pe.wait_ge(sn[f"pt{x}"], bs[f"pt{x}"] + gsum[j + 1] // 2)
                            if j:
                                pe.wait_ge(sn["og"], bs["og"] + j)
                            for h in range(HEADS):
                                for kb in range(nkey[j]):
                                    mm = pe.matmul(ps[:, 7, h * HD:(h + 1) * HD], pt[:, j % 2, kb, h % 2, h // 2, :],
                                                   v[:, j + 1 - nkey[j] + kb, h * HD:(h + 1) * HD],
                                                   start=(kb == 0), stop=(kb == nkey[j] - 1))
                            mm.then_inc(sn["pv"], 1)

                    @block.vector
                    def _(dve):
                        link = Link(dve, "dve_link")

                        def soft(j):
                            w = 2 * P - nkey[j] * P
                            dve.wait_ge(sn["sc"], bs["sc"] + j + 1)
                            if j >= 2:
                                dve.wait_ge(sn["tr"], bs["tr"] + gsum[j - 1])
                                dve.wait_ge(sn[f"out{j % 2}"], bs[f"out{j % 2}"] + 16 * (j // 2))
                            for par in range(2):
                                ins = dve.scalar_tensor_tensor(
                                    sbuf[:, j % 2, par, :, w:], ps[:, 2 * par:2 * par + 2, :].rearrange(
                                        "p a (b k) -> p (a b) k", b=2)[:, :, w:], 0.125,
                                    bias[:, par, :, w:], ALU.mult, ALU.add)
                                if par == 0:
                                    link(ins)
                                else:
                                    ins.then_inc(sn["sb"], 1)
                            dve.wait_ge(sn["sb"], bs["sb"] + j + 1)
                            dve.tensor_reduce(og[:, j % 2, 520:528].rearrange("p (hh two) -> p two hh", two=2),
                                              sbuf[:, j % 2, :, :, w:], X, ALU.max, negate=True
                                              ).then_inc(sn["nm"], 1)

                        soft(0)
                        for j in range(NT):
                            if j + 1 < NT:
                                soft(j + 1)
                            for n in range(1, ngrp[j], 2):
                                w = gsum[j] + n
                                dve.wait_ge(sn["tr"], bs["tr"] + w + 1)
                                if j >= 2:
                                    dve.wait_ge(sn["pv"], bs["pv"] + j - 1)
                                dve.tensor_copy(pt[:, j % 2, n // 2, n % 2, :, :].rearrange("p a b -> p (a b)"),
                                                ps[:, 4 + w % 3, :]).then_inc(sn["pt1"], 1)

                    @block.scalar
                    def _(act):
                        for j in range(NT):
                            w0 = 2 * P - nkey[j] * P
                            act.wait_ge(sn["nm"], bs["nm"] + j + 1)
                            for h in range(HEADS):
                                part = sbuf[:, j % 2, h % 2, h // 2, w0:]
                                e = act.activation(part, part, ACT.Exp, bias=og[:, j % 2, 520 + h:521 + h],
                                                   accum_out=og[:, j % 2, 512 + h:513 + h])
                            e.then_inc(sn["exp"], 1)
                            for n in range(0, ngrp[j], 2):
                                w = gsum[j] + n
                                act.wait_ge(sn["tr"], bs["tr"] + w + 1)
                                if j >= 2:
                                    act.wait_ge(sn["pv"], bs["pv"] + j - 1)
                                act.activation(pt[:, j % 2, n // 2, n % 2, :, :].rearrange("p a b -> p (a b)"),
                                               ps[:, 4 + w % 3, :], ACT.Copy).then_inc(sn["pt0"], 1)
                            act.wait_ge(sn["pv"], bs["pv"] + j + 1)
                            act.activation(og[:, j % 2, 0:512], ps[:, 7, :], ACT.Copy).then_inc(sn["og"], 1)

                    @block.sync
                    def _(sp):
                        for j in range(NT):
                            sp.wait_ge(sn["og"], bs["og"] + j + 1)
                            r, i0 = divmod(j * P, length)
                            sp.dma_start(gv[r, i0:i0 + P, :], og[:, j % 2, :]).then_inc(sn[f"out{j % 2}"], 16)
                        for x in range(2):
                            sp.wait_ge(sn[f"out{x}"], bs[f"out{x}"] + 16 * NT // 2)

            free_h()
            oza = sb(first, "oza", [P, 4, T])
            mga = sb(first, "mga", [P, KD, T])
            mgb = sb(first, "mgb", [P, KD, T])
            with ExitStack() as st:
                zg = sb(st, "zg", [P, 8, T])
                ga = sb(st, "cg", [P, NT, 3, REC])
                mn = sb(st, "cmn", [P, NT, HEADS])
                wg = sb(st, "cwg", [P, NT, 3, HEADS])
                wd = sb(st, "cwd", [P, NT, 3, HEADS])
                block = st.enter_context(nc.Block())

                mg_ready = 32

                @block.sync
                def _(sp):
                    for g in range(3):
                        sp.dma_start(ga[:, :, g, :], ag_d[g].rearrange("(t p) c -> p t c", p=P)
                                     ).then_inc(S("cm_in"), 16)
                    sp.dma_start(zg[:, :, :], gates_d[:, 0:8, :]).then_inc(S("cm_z"), 16)
                    sp.dma_start(mga[:, :, :], gates_d[:, 8:16, :]).then_inc(S("mg_in"), 16)
                    sp.dma_start(mgb[:, :, :], gates_d[:, 16:24, :]).then_inc(S("mg_in"), 16)

                @block.scalar
                def _(act):
                    act.wait_ge(S("cm_dif"), 3)
                    act.activation(wg[:, :, :, :], wg[:, :, :, :], ACT.Exp).then_inc(S("cm_w"), 1)

                @block.vector
                def _(dve):
                    link = Link(dve, "dve_link")
                    nm = lambda g: ga[:, :, g, 520:528]
                    dve.wait_ge(S("cm_in"), 48)
                    link(dve.tensor_tensor(mn[:, :, :], nm(0), nm(1), ALU.min))
                    link(dve.tensor_tensor(mn[:, :, :], mn[:, :, :], nm(2), ALU.min))
                    for g in range(3):
                        dve.tensor_tensor(wg[:, :, g, :], mn[:, :, :], nm(g), ALU.subtract).then_inc(S("cm_dif"), 1)
                    dve.wait_ge(S("cm_w"), 1)
                    link(dve.tensor_tensor(wd[:, :, :, :], wg[:, :, :, :], ga[:, :, :, 512:520], ALU.mult))
                    link(dve.tensor_tensor(mn[:, :, :], wd[:, :, 0, :], wd[:, :, 1, :], ALU.add))
                    link(dve.tensor_tensor(mn[:, :, :], mn[:, :, :], wd[:, :, 2, :], ALU.add))
                    link(dve.reciprocal(mn[:, :, :], mn[:, :, :]))
                    for g in range(3):
                        link(dve.tensor_tensor(wg[:, :, g, :], wg[:, :, g, :], mn[:, :, :], ALU.mult))
                    for tt in range(NT):
                        for g in range(3):
                            num = ga[:, tt, g, 0:512].rearrange("p (h c) -> p h c", c=HD)
                            link(dve.tensor_tensor(num, num, wg[:, tt, g, :].unsqueeze(2).to_broadcast([P, HEADS, HD]),
                                                   ALU.mult))
                        o = ga[:, tt, 0, 0:512]
                        link(dve.tensor_tensor(o, o, ga[:, tt, 1, 0:512], ALU.add))
                        dve.tensor_tensor(o, o, ga[:, tt, 2, 0:512], ALU.add).then_inc(S("cm_o"), 1)
                        dve.wait_ge(S("cm_tr"), tt + 1)
                        if tt == 0:
                            dve.wait_ge(S("cm_z"), 16)
                        dve.tensor_tensor(oza[:, :, tt * P:(tt + 1) * P],
                                          ps[:, tt % 8, :].rearrange("p (c t) -> p c t", t=P),
                                          zg[:, 4:8, tt * P:(tt + 1) * P], ALU.mult)
                    dve.tensor_tensor(ozr[:, :, :], ozr[:, :, :], zg[:, 0:4, :], ALU.mult)

                @block.tensor
                def _(pe):
                    for tt in range(NT):
                        pe.wait_ge(S("cm_o"), tt + 1)
                        for c in range(4):
                            tr = pe.transpose(ps[:, tt % 8, c * P:(c + 1) * P], ga[:, tt, 0, c * P:(c + 1) * P], ident[:, :])
                        tr.then_inc(S("cm_tr"), 1)
            dump("oza", oza[:, :, :])
            return oza, mga, mgb, mg_ready

        def merge(ga, gb, ready, wa, wb, oa, ob, w_o, rows):
            for src_o, w_u, acc in ((oa, wa, False), (ob, wb, True)):
                link = [None]

                def up(kind, eng, src, ci, ct, hf, acc=acc, link=link):
                    m, cols = 4 * ci + ct, slice(hf * 512, (hf + 1) * 512)
                    if link[0] is None:
                        link[0] = Link(eng, "dve_link")
                        if ready:
                            eng.wait_ge(S(ready[0]), ready[1])
                    if not acc:
                        return eng.tensor_tensor(ga[:, m, cols], src, ga[:, m, cols], ALU.mult)
                    link[0](eng.tensor_tensor(gb[:, m, cols], src, gb[:, m, cols], ALU.mult))
                    return eng.tensor_tensor(ga[:, m, cols], ga[:, m, cols], gb[:, m, cols], ALU.add)
                gemm([(wcols(w_u, 512 * i, 512 * i + 512), 512) for i in range(2)], 4, "T",
                     src_o, up, act_only=None)
            dump("merged", ga[:, :, :])
            gemm([(wcols(w_o, 512 * i, 512 * i + 512), 512) for i in range(2)], KD, "N", ga,
                 lambda kind, eng, src, ci, tt, hf: copy(kind, eng, rows[:, tt, ci * 512:(ci + 1) * 512], src))

        def row(ap):
            return bass.AP(tensor=ap.tensor, offset=ap.offset, ap=[[0, P], [1, D]])

        def merge_first():
            rows = mgb
            merge(mga, mgb, ("mg_in", mg_ready), A["w_up_attn"][0], A["w_up_rwkv"][0], oza, ozr, A["w_out"][0], rows)
            with ExitStack() as st:
                xr = sb(st, "x_res", [P, NT, D])
                pg = sb(st, "post_gain", [P, D])
                sq = sb(st, "pn_sq", [P, D])
                ss = sb(st, "pn_ss", [P, NT])
                load([(xr[:, :, :], x_rows.rearrange("(t p) d -> p t d", p=P)), (pg[:, :], row(A["post_norm_gain"][0]))])
                block = st.enter_context(nc.Block())

                @block.scalar
                def _(act):
                    for t in range(NT):
                        if t:
                            act.wait_ge(S("pn_ss"), t)
                        act.activation(sq[:, :], rows[:, t, :], ACT.Square, accum_out=ss[:, t:t + 1]).then_inc(S("pn_ss"), 1)
                    act.wait_ge(S("pn_mean"), 1)
                    act.activation(ss[:, :], ss[:, :], ACT.Sqrt).then_inc(S("pn_root"), 1)

                @block.vector
                def _(dve):
                    link = Link(dve, "dve_link")
                    dve.wait_ge(S("pn_ss"), NT)
                    dve.tensor_scalar(ss[:, :], ss[:, :], 1.0 / D, EPS, ALU.mult, ALU.add).then_inc(S("pn_mean"), 1)
                    dve.wait_ge(S("pn_root"), 1)
                    link(dve.reciprocal(ss[:, :], ss[:, :]))
                    for t in range(NT):
                        link(dve.scalar_tensor_tensor(rows[:, t, :], rows[:, t, :], ss[:, t:t + 1], pg[:, :],
                                                      ALU.mult, ALU.mult))
                        dve.tensor_tensor(xr[:, t, :], xr[:, t, :], rows[:, t, :], ALU.add).then_inc(S("pn_x"), 1)

                @block.sync
                def _(sp):
                    for t in range(NT):
                        sp.wait_ge(S("pn_x"), t + 1)
                        sp.dma_start(x1_d[t * P:(t + 1) * P, :], xr[:, t, :]).then_inc(S("pn_out"), 16)
                    sp.wait_ge(S("pn_out"), 16 * NT)


        def chan_norm(buf, kt, slices, gain, width, tag):
            n_tok = buf.shape[2]
            with ExitStack() as st:
                sq = sb(st, f"cn_sq{tag}", [P, kt, n_tok])
                rs = sb(st, f"cn_rs{tag}", [P, n_tok])
                b = {n: base(f"cn_{n}", c) for n, c in (("sq", 1), ("mm", 1), ("mean", len(slices)), ("root", 1))}
                block = st.enter_context(nc.Block())

                @block.scalar
                def _(act):
                    act.activation(sq[:, :, :], buf[:, :, :], ACT.Square).then_inc(S("cn_sq"), 1)
                    act.wait_ge(S("cn_mean"), b["mean"] + len(slices))
                    act.activation(rs[:, :], rs[:, :], ACT.Sqrt).then_inc(S("cn_root"), 1)

                @block.tensor
                def _(pe):
                    pe.wait_ge(S("cn_sq"), b["sq"] + 1)
                    for n, (o, w) in enumerate(slices):
                        for k in range(kt):
                            mm = pe.matmul(ps[:, n, 0:w], ones[:, :], sq[:, k, o:o + w], start=(k == 0), stop=(k == kt - 1))
                    mm.then_inc(S("cn_mm"), 1)

                @block.vector
                def _(dve):
                    link = Link(dve, "dve_link")
                    dve.wait_ge(S("cn_mm"), b["mm"] + 1)
                    for n, (o, w) in enumerate(slices):
                        dve.tensor_scalar(rs[:, o:o + w], ps[:, n, 0:w], 1.0 / width, EPS, ALU.mult, ALU.add
                                          ).then_inc(S("cn_mean"), 1)
                    dve.wait_ge(S("cn_root"), b["root"] + 1)
                    link(dve.reciprocal(rs[:, :], rs[:, :]))
                    for k in range(kt):
                        dve.scalar_tensor_tensor(buf[:, k, :], buf[:, k, :], gain[:, k:k + 1], rs[:, :], ALU.mult, ALU.mult)

        def head_norm_rope(buf, nt, gain_row, rope_tiles, tag):
            with ExitStack() as st:
                ss = sb(st, f"hn_ss{tag}", [P, nt, HEADS])
                sq = sb(st, f"hn_sq{tag}", [P, 2, HEADS, QKD])
                t1 = sb(st, f"hn_t1{tag}", [P, HEADS, ROPE])
                t2 = sb(st, f"hn_t2{tag}", [P, HEADS, ROPE])
                rope = sb(st, f"hn_rope{tag}", [P, NT, 2, ROPE])
                load([(rope[:, :, :, :].rearrange("p t a c -> p t (a c)"),
                       A["c_rope"].rearrange("(t p) a c -> p t (a c)", p=P))])
                b = {n: base(f"hn_{n}", c) for n, c in (("sq", nt), ("ss", nt), ("root", 1), ("mean", 1))}
                block = st.enter_context(nc.Block())

                @block.scalar
                def _(act):
                    for t in range(nt):
                        if t >= 2:
                            act.wait_ge(S("hn_ss"), b["ss"] + t - 1)
                        act.activation(sq[:, t % 2, :, :], buf[:, t, :, :], ACT.Square).then_inc(S("hn_sq"), 1)
                    act.wait_ge(S("hn_mean"), b["mean"] + 1)
                    act.activation(ss[:, :, :], ss[:, :, :], ACT.Sqrt).then_inc(S("hn_root"), 1)

                @block.vector
                def _(dve):
                    link = Link(dve, "dve_link")
                    for t in range(nt):
                        dve.wait_ge(S("hn_sq"), b["sq"] + t + 1)
                        dve.tensor_reduce(ss[:, t, :], sq[:, t % 2, :, :], X, ALU.add).then_inc(S("hn_ss"), 1)
                    dve.wait_ge(S("hn_ss"), b["ss"] + nt)
                    dve.tensor_scalar(ss[:, :, :], ss[:, :, :], 1.0 / QKD, EPS, ALU.mult, ALU.add).then_inc(S("hn_mean"), 1)
                    dve.wait_ge(S("hn_root"), b["root"] + 1)
                    link(dve.reciprocal(ss[:, :, :], ss[:, :, :]))
                    for t in range(nt):
                        link(dve.tensor_tensor(buf[:, t, :, :], buf[:, t, :, :],
                                               ss[:, t, :].unsqueeze(2).to_broadcast([P, HEADS, QKD]), ALU.mult))
                        link(dve.tensor_tensor(buf[:, t, :, :], buf[:, t, :, :],
                                               gain_row.unsqueeze(1).to_broadcast([P, HEADS, QKD]), ALU.mult))
                        if t < rope_tiles:
                            xr = buf[:, t, :, NOPE:QKD]
                            tab = lambda i: rope[:, t, i, :].unsqueeze(1).to_broadcast([P, HEADS, ROPE])
                            halves = lambda ap, s: ap.rearrange("p h (a s e) -> p h a s e", a=2, s=2)[:, :, :, s, :]
                            dve.tensor_tensor(t1[:, :, :], xr, tab(0), ALU.mult)
                            dve.tensor_copy(halves(t2[:, :, :], 0), halves(xr, 1))
                            link(dve.tensor_copy(halves(t2[:, :, :], 1), halves(xr, 0)))
                            link(dve.tensor_tensor(t2[:, :, :], t2[:, :, :], tab(1), ALU.mult))
                            link(dve.tensor_tensor(xr, t1[:, :, :], t2[:, :, :], ALU.add))

        def second():
            w_in2 = A["w_in_2"][0]
            outer = ExitStack()
            modv = sb(outer, "modv", [P, 6, KD, 2])
            g1r = sb(outer, "g1r", [P, D])
            g2r = sb(outer, "g2r", [P, D])
            SLOTS = {0: "sh1", 1: "sc1", 3: "sh2", 4: "sc2"}
            with ExitStack() as st:
                cv = sb(st, "cv", [P, KD, 2])
                cb = sb(st, "cb", [P, KD, P])
                bm = sb(st, "bm", [P, 6, KD])
                brow = sb(st, "brow", [P, 2, D])
                wb = sb(st, "mod_w", [P, 2, KD, 512])
                bvec = A["b_mod_2"][0]
                load([(cv[:, :, 0], vec(A["c_2"][0])), (cv[:, :, 1], vec(A["c_ctx_2"][0])),
                      (bm[:, :, :], bvec.rearrange("(s k p) -> p s k", p=P, s=6)),
                      (brow[:, 0, :], row(bvec[2 * D:3 * D])), (brow[:, 1, :], row(bvec[5 * D:6 * D])),
                      (gains[:, 7, :], vec(A["norm1_g_2"][0])), (gains[:, 8, :], vec(A["norm2_g_2"][0]))])
                block = st.enter_context(nc.Block())

                @block.sync
                def _(sp):
                    for j in range(12):
                        if j >= 2:
                            sp.wait_ge(S("mod_mm"), j - 1)
                        sp.dma_start(wb[:, j % 2, :, :], wcols(A["w_mod_2"][0], j * 512, (j + 1) * 512)
                                     ).then_inc(S(f"mod_w{j % 2}"), 16)

                @block.scalar
                def _(act):
                    act.activation(cv[:, :, :], cv[:, :, :], ACT.Silu).then_inc(S("mod_c"), 1)
                    act.wait_ge(S("mod_c"), 1)
                    act.activation(cb[:, :, :], cv[:, :, 0:1].to_broadcast([P, KD, P]), ACT.Copy).then_inc(S("mod_c"), 1)

                @block.tensor
                def _(pe):
                    pe.wait_ge(S("mod_c"), 2)
                    for j in range(12):
                        pe.wait_ge(S(f"mod_w{j % 2}"), 16 * (j // 2 + 1))
                        if j >= 8:
                            pe.wait_ge(S("mod_ev"), j - 7)
                        if j // 2 in (2, 5):
                            for k in range(KD):
                                mm = pe.matmul(ps[:, j % 8, :], cb[:, k, :], wb[:, j % 2, k, :],
                                               start=(k == 0), stop=(k == KD - 1))
                        else:
                            for ct in range(4):
                                for k in range(KD):
                                    mm = pe.matmul(ps[:, j % 8, 2 * ct:2 * ct + 2], wb[:, j % 2, k, ct * P:(ct + 1) * P],
                                                   cv[:, k, :], start=(k == 0), stop=(k == KD - 1))
                        mm.then_inc(S("mod_mm"), 1)

                @block.vector
                def _(dve):
                    link = Link(dve, "dve_link")
                    for j in range(12):
                        s, half = divmod(j, 2)
                        dve.wait_ge(S("mod_mm"), j + 1)
                        if s in (2, 5):
                            dst = (g1r, g2r)[s == 5][:, half * 512:(half + 1) * 512]
                            dve.tensor_tensor(dst, ps[:, j % 8, :], brow[:, int(s == 5), half * 512:(half + 1) * 512],
                                              ALU.add).then_inc(S("mod_ev"), 1)
                        else:
                            dve.tensor_tensor(modv[:, s, 4 * half:4 * half + 4, :],
                                              ps[:, j % 8, 0:8].rearrange("p (c v) -> p c v", v=2),
                                              bm[:, s, 4 * half:4 * half + 4].unsqueeze(2).to_broadcast([P, 4, 2]),
                                              ALU.add).then_inc(S("mod_ev"), 1)
                    dve.wait_ge(S("mod_ev"), 12)
                    for dst, g, s, v in ((1, 7, 1, 0), (3, 7, 1, 1), (5, 8, 4, 0)):
                        dve.scalar_tensor_tensor(gains[:, dst, :], modv[:, s, :, v], 1.0, gains[:, g, :], ALU.add, ALU.mult)
                    for dst, s, v in ((2, 0, 0), (4, 0, 1), (6, 3, 0)):
                        dve.tensor_copy(gains[:, dst, :], modv[:, s, :, v])
            mix = ExitStack()
            hA = sb(mix, "hA", [P, KD, NKEY])
            aoT = sb(mix, "aoT", [P, 4, T])
            foT = sb(mix, "foT", [P, 4, T])
            norm_T(x1_d, NT, hA[:, :, 0:T], gains[:, 1, :], gains[:, 2, :], tag="n2")
            norm_T(A["ctx_2"][0], NTC, hA[:, :, T:NKEY], gains[:, 3, :], gains[:, 4, :], tag="n3")
            dump("hA", hA[:, :, :])

            with ExitStack() as st:
                fT = foT
                gemm([(wcols(w_in2, OFF_F, OFF_F + 512), 512)], KD, "T", hA,
                     lambda kind, eng, src, ci, ct, hf: copy(kind, eng, fT[:, ct, hf * 512:(hf + 1) * 512], src))
                dc = sb(st, "dft_ch", [P, 2 * P])
                dp = sb(st, "dft_pos", [P, 4, 4, 512])
                ab = sb(st, "dft_ab", [P, NT, 4, 2, P])
                fold = sb(st, "dft_fold", [P, 4, 2, 4, 2, P])
                load([(dc[:, :], A["c_dft_ch"]), (dp[:, :, :, :].rearrange("p t a k -> p t (a k)"),
                                                  A["c_dft_pos"].rearrange("(t p) a b k -> p t (a b k)", p=P))])
                block = st.enter_context(nc.Block())

                @block.tensor
                def _(pe):
                    for tt in range(NT):
                        if tt >= 4:
                            pe.wait_ge(S("ft_ab"), 2 * (tt - 3))
                        for g in range(4):
                            mm = pe.matmul(ps[:, 2 * (tt % 4) + g // 2, (g % 2) * 256:(g % 2 + 1) * 256],
                                           fT[:, g, tt * P:(tt + 1) * P], dc[:, :], start=True, stop=True)
                        mm.then_inc(S("ft_mm"), 1)
                    pe.wait_ge(S("ft_fold"), 8)
                    for n, (g, par) in enumerate([(g, par) for g in range(4) for par in range(2)]):
                        for pt_ in range(4):
                            for x in range(2):
                                mm = pe.matmul(ps[:, n, :], fold[:, pt_, par, g, x, :], dp[:, pt_, 2 * par + x, :],
                                               start=(pt_ + x == 0), stop=(pt_ + x == 4))
                        mm.then_inc(S("ft_out"), 1)

                @block.scalar
                def _(act):
                    for tt in range(NT):
                        act.wait_ge(S("ft_mm"), tt + 1)
                        for x in range(2):
                            act.activation(ab[:, tt, 2 * x:2 * x + 2, :, :].rearrange("p g x c -> p (g x c)"),
                                           ps[:, 2 * (tt % 4) + x, :], ACT.Copy).then_inc(S("ft_ab"), 1)

                @block.vector
                def _(dve):
                    flat = lambda ap: ap.rearrange("p g x c -> p (g x c)")
                    dve.wait_ge(S("ft_ab"), 2 * NT)
                    for tt in range(4):
                        for par, op in ((0, ALU.add), (1, ALU.subtract)):
                            dve.tensor_tensor(flat(fold[:, tt, par]), flat(ab[:, tt]), flat(ab[:, tt + 4]), op
                                              ).then_inc(S("ft_fold"), 1)
                    for n in range(8):
                        g, par = divmod(n, 2)
                        dve.wait_ge(S("ft_out"), n + 1)
                        dve.tensor_copy(foT[:, g, par::2], ps[:, n, :])
            dump("foT", foT[:, :, :])

            kv_slices = [(0, 512), (512, 512), (1024, 256)]
            mla = ExitStack()
            q = sb(mla, "mla_q", [P, NT, HEADS, QKD])
            kb = sb(mla, "mla_k", [P, NKT, HEADS, QKD])
            vb = sb(mla, "mla_v", [P, NKT, HEADS, VD])
            rowg = sb(mla, "mla_rowg", [P, 2, QKD])
            with ExitStack() as st:
                cq = sb(st, "cq", [P, 3, T])
                ckv = sb(st, "ckv", [P, 2, NKEY])
                gv = sb(st, "mla_gv", [P, 5])
                kpe = sb(st, "kpe", [P, NKT, ROPE])
                rowv = lambda ap: bass.AP(tensor=ap.tensor, offset=ap.offset, ap=[[0, P], [1, QKD]])
                load([(gv[:, 0:3], vec(A["q_a_norm_g_2"][0], 3)), (gv[:, 3:5], vec(A["kv_a_norm_g_2"][0], 2)),
                      (rowg[:, 0, :], rowv(A["q_norm_g_2"][0])), (rowg[:, 1, :], rowv(A["k_norm_g_2"][0]))])
                gemm([(wcols(w_in2, 0, QL), QL)], KD, "T", hA,
                     lambda kind, eng, src, ci, ct, hf: copy(kind, eng, cq[:, ct, hf * 512:(hf + 1) * 512], src), width=QL)
                gemm([(wcols(w_in2, QL, QL + KVL), KVL)], KD, "T", hA,
                     lambda kind, eng, src, ci, ct, hf: copy(
                         kind, eng, ckv[:, ct, kv_slices[hf][0]:sum(kv_slices[hf])], src[:, 0:kv_slices[hf][1]]),
                     width=KVL, halves=3)
                gemm([(wcols(w_in2, QL + KVL, OFF_F), ROPE)], KD, "N", hA,
                     lambda kind, eng, src, ci, tt, hf: copy(kind, eng, kpe[:, tt, :], src[:, 0:ROPE]),
                     width=ROPE, act_tiles=NKT)
                chan_norm(cq, 3, [(0, 512), (512, 512)], gv[:, 0:3], QL, "q")
                chan_norm(ckv, 2, kv_slices, gv[:, 3:5], KVL, "kv")
                wq = A["w_q_up_2"][0]
                qf = q[:, :, :, :].rearrange("p t h c -> p t (h c)")
                gemm([(wcols(wq, 0, 384), 384), (wcols(wq, 384, 768), 384)], 3, "N", cq,
                     lambda kind, eng, src, ci, tt, hf: copy(kind, eng, qf[:, tt, ci * 384:(ci + 1) * 384], src[:, 0:384]),
                     width=384)

                def split_kv(kind, eng, src, ci, tt, hf):
                    s4 = src.rearrange("p (h c) -> p h c", c=P)
                    copy(kind, eng, kb[:, tt, 4 * ci:4 * ci + 4, 0:NOPE], s4[:, :, 0:NOPE])
                    return copy(kind, eng, vb[:, tt, 4 * ci:4 * ci + 4, :], s4[:, :, NOPE:])
                gemm([(wcols(A["w_kv_up_2"][0], 512 * i, 512 * i + 512), 512) for i in range(2)], 2, "N", ckv,
                     split_kv, act_tiles=NKT)
                with nc.Block() as block:
                    @block.vector
                    def _(dve):
                        for t in range(NKT):
                            dve.tensor_copy(kb[:, t, :, NOPE:QKD],
                                            kpe[:, t, :].unsqueeze(1).to_broadcast([P, HEADS, ROPE]))
                head_norm_rope(q, NT, rowg[:, 0, :], NT, "q")
                head_norm_rope(kb, NKT, rowg[:, 1, :], NT, "k")
            dump("q", q[:, :, :, :].rearrange("p t h c -> p (t h c)"))
            dump("k", kb[:, :, :, :].rearrange("p t h c -> p (t h c)"))
            SC = QKD ** -0.5
            with ExitStack() as st:
                qT = sb(st, "qT", [QKD, 2, T])
                kT = sb(st, "kT", [QKD, 2, NKEY])
                pr = sb(st, "mla_p", [P, 2, NKEY])
                pT = sb(st, "mla_pT", [P, 2, NKT, P])
                nm = sb(st, "mla_nm", [P, HEADS * NT])
                den = sb(st, "mla_den", [P, HEADS * NT])
                ao = aoT[:, :, :].rearrange("p c t -> p (c t)").rearrange("p (t c) -> p t c", c=512)
                block = st.enter_context(nc.Block())
                its = [(h, t) for h in range(HEADS) for t in range(NT)]
                GR = [(0, 4), (4, 4), (8, 2)]

                N = len(its)
                s3 = lambda n: ps[:, 3 * (n % 2):3 * (n % 2) + 3, :].rearrange("p a b -> p (a b)")[:, 0:NKEY]
                out_bank = lambda n: ps[:, 3 * ((n + 1) % 2) + 2, 256:256 + VD]

                def head_group(h, i):
                    src, dst, t0, n_ = (q, qT, 4 * i, NT) if i < 2 else (kb, kT, 4 * (i - 2), NKT)
                    return src, t0, min(4, n_ - t0), dst

                def next_head(n):
                    h, t = its[n]
                    return (h + 1, t - 1) if 1 <= t <= 5 and h + 1 < HEADS else None

                @block.tensor
                def _(pe):
                    def head(h, i):
                        src, t0, w, _d = head_group(h, i)
                        n = 5 * h + i
                        if n:
                            pe.wait_ge(S("ml_hev"), n)
                        for j in range(w):
                            tr = pe.transpose(ps[0:QKD, 7, j * P:(j + 1) * P], src[:, t0 + j, h, :], ident[:, :])
                        tr.then_inc(S("ml_htr"), 1)

                    def scores(n):
                        h, t = its[n]
                        if t == 0:
                            pe.wait_ge(S("ml_hev"), 5 * h + 5)
                        if n >= 2:
                            pe.wait_ge(S("ml_e"), n - 1)
                        for i in range(3):
                            w = 512 if i < 2 else 256
                            if i == 2 and n >= 3:
                                pe.wait_ge(S("ml_o"), n - 2)
                            mm = pe.matmul(ps[:, 3 * (n % 2) + i, 0:w], qT[:, h % 2, t * P:(t + 1) * P],
                                           kT[:, h % 2, i * 512:i * 512 + w], start=True, stop=True)
                        mm.then_inc(S("ml_s"), 1)

                    def transposes(n, i):
                        g0, w = GR[i]
                        for j in range(w):
                            tr = pe.transpose(ps[:, 6 + i % 2, j * P:(j + 1) * P],
                                              pr[:, n % 2, (g0 + j) * P:(g0 + j + 1) * P], ident[:, :])
                        tr.then_inc(S("ml_t"), 1)

                    def output(n):
                        h = its[n][0]
                        pe.wait_ge(S("ml_pd"), n + 1)
                        pe.wait_ge(S("ml_pa"), 2 * n + 2)
                        for k in range(NKT):
                            mm = pe.matmul(out_bank(n), pT[:, n % 2, k, :], vb[:, k, h, :],
                                           start=(k == 0), stop=(k == NKT - 1))
                        mm.then_inc(S("ml_pv"), 1)

                    for i in range(5):
                        head(0, i)
                    scores(0)
                    for n in range(N):
                        if n + 1 < N:
                            scores(n + 1)
                        pe.wait_ge(S("ml_e"), n + 1)
                        if n:
                            pe.wait_ge(S("ml_pa"), 2 * n)
                            pe.wait_ge(S("ml_pd"), n)
                        if n and next_head(n - 1):
                            hh, i = next_head(n - 1)
                            pe.wait_ge(S("ml_hev"), 5 * hh + i + 1)
                        transposes(n, 0)
                        transposes(n, 1)
                        if n:
                            output(n - 1)
                        pe.wait_ge(S("ml_pa"), 2 * n + 1)
                        transposes(n, 2)
                        if next_head(n):
                            pe.wait_ge(S("ml_pd"), n + 1)
                            head(*next_head(n))
                    output(N - 1)

                @block.scalar
                def _(act):
                    def exponentials(n):
                        act.wait_ge(S("ml_m"), n + 1)
                        if n >= 2:
                            act.wait_ge(S("ml_t"), 3 * (n - 1))
                        act.activation(pr[:, n % 2, :], s3(n), ACT.Exp, bias=nm[:, n:n + 1], scale=SC,
                                       accum_out=den[:, n:n + 1]).then_inc(S("ml_e"), 1)

                    def probs(n, i):
                        g0, w = GR[i]
                        act.wait_ge(S("ml_t"), 3 * n + i + 1)
                        if i == 0 and n >= 2:
                            act.wait_ge(S("ml_pv"), n - 1)
                        act.activation(pT[:, n % 2, g0:g0 + w, :].rearrange("p k t -> p (k t)"), ps[:, 6, 0:w * P],
                                       ACT.Copy).then_inc(S("ml_pa"), 1)

                    exponentials(0)
                    for n in range(N):
                        probs(n, 0)
                        if n + 1 < N:
                            exponentials(n + 1)
                        probs(n, 2)

                @block.vector
                def _(dve):
                    link = Link(dve, "dve_link")

                    def head(h, i):
                        _s, t0, w, dst = head_group(h, i)
                        dve.wait_ge(S("ml_htr"), 5 * h + i + 1)
                        dve.tensor_copy(dst[:, h % 2, t0 * P:(t0 + w) * P], ps[0:QKD, 7, 0:w * P]
                                        ).then_inc(S("ml_hev"), 1)

                    def row_max(n):
                        dve.wait_ge(S("ml_s"), n + 1)
                        link(dve.tensor_reduce(nm[:, n:n + 1], s3(n), X, ALU.max))
                        dve.tensor_scalar(nm[:, n:n + 1], nm[:, n:n + 1], -SC, None, ALU.mult).then_inc(S("ml_m"), 1)

                    def output(n):
                        h, t = its[n]
                        dve.wait_ge(S("ml_e"), n + 1)
                        link(dve.reciprocal(den[:, n:n + 1], den[:, n:n + 1]))
                        dve.wait_ge(S("ml_pv"), n + 1)
                        dve.tensor_scalar(ao[:, t, h * VD:(h + 1) * VD], out_bank(n), den[:, n:n + 1], None, ALU.mult
                                          ).then_inc(S("ml_o"), 1)

                    for i in range(5):
                        head(0, i)
                    row_max(0)
                    for n in range(N):
                        if n + 1 < N:
                            row_max(n + 1)
                        dve.wait_ge(S("ml_t"), 3 * n + 2)
                        if n >= 2:
                            dve.wait_ge(S("ml_pv"), n - 1)
                        dve.tensor_copy(pT[:, n % 2, 4:8, :].rearrange("p k t -> p (k t)"), ps[:, 7, :]
                                        ).then_inc(S("ml_pd"), 1)
                        if n:
                            output(n - 1)
                        if next_head(n):
                            head(*next_head(n))
                    output(N - 1)
            with ExitStack() as st:
                block = st.enter_context(nc.Block())

                @block.tensor
                def _(pe):
                    for t in range(NT):
                        for c in range(4):
                            tr = pe.transpose(ps[:, t, c * P:(c + 1) * P], ao[:, t, c * P:(c + 1) * P], ident[:, :])
                        tr.then_inc(S("ml_at"), 1)

                @block.vector
                def _(dve):
                    dve.wait_ge(S("ml_at"), NT)
                    for t in range(NT):
                        dve.tensor_copy(aoT[:, :, t * P:(t + 1) * P], ps[:, t, :].rearrange("p (c x) -> p c x", x=P))
            mla.close()
            dump("aoT", aoT[:, :, :])

            with ExitStack() as st:
                rows = hA[:, :, 0:T]
                with ExitStack() as s2:
                    mga = sb(s2, "mga2", [P, KD, T])
                    mgb = sb(s2, "mgb2", [P, KD, T])
                    gemm([(wcols(w_in2, OFF_GA + 512 * i, OFF_GA + 512 * i + 512), 512) for i in range(4)], KD, "T", hA,
                         lambda kind, eng, src, ci, ct, hf: eng.activation(
                             (mga, mgb)[ci // 2][:, 4 * (ci % 2) + ct, hf * 512:(hf + 1) * 512], src, ACT.Sigmoid),
                         act_only=True)
                    merge(mga, mgb, None, A["w_o_attn_2"][0], A["w_fourier_2"][0], aoT, foT, A["w_out_2"][0], rows)
                xv = sb(st, "x1_res", [P, NT, D])
                load([(xv[:, :, :], x1_d.rearrange("(t p) d -> p t d", p=P))])
                block = st.enter_context(nc.Block())

                @block.vector
                def _(dve):
                    link = Link(dve, "dve_link")
                    for t in range(NT):
                        link(dve.tensor_tensor(rows[:, t, :], rows[:, t, :], g1r[:, :], ALU.mult))
                        dve.tensor_tensor(rows[:, t, :], rows[:, t, :], xv[:, t, :], ALU.add).then_inc(S("r2_x"), 1)

                @block.sync
                def _(sp):
                    for t in range(NT):
                        sp.wait_ge(S("r2_x"), t + 1)
                        sp.dma_start(x2_d[t * P:(t + 1) * P, :], rows[:, t, :]).then_inc(S("r2_out"), 16)
                    sp.wait_ge(S("r2_out"), 16 * NT)
            mix.close()

            xn_d = dram("xn_rows", [T, D])
            y_d = dram("y_rows", [T, D])
            moe = ExitStack()
            slot = sb(moe, "slot", [P, NT, NE])
            tg = sb(moe, "tg", [P, NT, NE, 2])
            sel = sb(moe, "sel", [P, NE, 2])
            idx = sb(moe, "idx", [P, NE], U32)
            iota = sb(moe, "iota", [P, CAP])
            with ExitStack() as st:
                h2T = sb(st, "h2T", [P, KD, T])
                norm_T(x2_d, NT, h2T, gains[:, 5, :], gains[:, 6, :], rows_out=xn_d, tag="n4")
                wr = sb(st, "wr", [P, KD, NE])
                tok = sb(st, "tok", [P, NT])
                lg = sb(st, "lg", [P, NT, NE])
                m1 = sb(st, "lg_m", [P, NT])
                affT = sb(st, "affT", [NE, T])
                work = sb(st, "work", [NE, T])
                one = sb(st, "one", [NE, T])
                m8 = sb(st, "m8", [NE, 8])
                zero = sb(st, "zero", [P, D])
                oh = sb(st, "oh", [P, 4, CAP])
                load([(wr[:, :, :], A["w_router_2"][0].rearrange("(k p) e -> p k e", p=P)), (tok[:, :], A["c_tok"]),
                      (iota[:, :], A["c_slot"])])
                block = st.enter_context(nc.Block())

                @block.tensor
                def _(pe):
                    for t in range(NT):
                        for k in range(KD):
                            mm = pe.matmul(ps[:, 0, t * NE:(t + 1) * NE], h2T[:, k, t * P:(t + 1) * P], wr[:, k, :],
                                           start=(k == 0), stop=(k == KD - 1))
                    mm.then_inc(S("ro_l"), 1)
                    pe.wait_ge(S("ro_a"), 1)
                    for t in range(NT):
                        tr = pe.transpose(ps[0:NE, 1 + t // 4, (t % 4) * P:(t % 4 + 1) * P], lg[:, t, :], ident[:, :])
                    tr.then_inc(S("ro_t"), 1)
                    pe.wait_ge(S("ro_s"), 1)
                    for t in range(NT):
                        tr = pe.transpose(ps[:, 3, t * NE:(t + 1) * NE], work[:, t * P:(t + 1) * P], ident[0:NE, 0:NE])
                    tr.then_inc(S("ro_st"), 1)
                    for n in range(NE * NT):
                        e, t = divmod(n, NT)
                        pe.wait_ge(S("ro_oh"), n + 1)
                        pe.matmul(ps[:, 4, 2 * e:2 * e + 2], oh[:, n % 4, :], tg[:, t, e, :],
                                  start=(t == 0), stop=(t == NT - 1)).then_inc(S("ro_sel"), 1)

                @block.scalar
                def _(act):
                    act.wait_ge(S("ro_m"), 1)
                    act.activation(lg[:, :, :], lg[:, :, :], ACT.Exp).then_inc(S("ro_e"), 1)

                @block.sync
                def _(sp):
                    sp.wait_ge(S("ro_zero"), 1)
                    for t in range(NT):
                        sp.dma_start(y_d[t * P:(t + 1) * P, :], zero[:, :]).then_inc(S("ro_y0"), 16)
                    sp.wait_ge(S("ro_y0"), 16 * NT)

                @block.vector
                def _(dve):
                    link = Link(dve, "dve_link")
                    dve.memset(zero[:, :], 0.0).then_inc(S("ro_zero"), 1)
                    link(dve.memset(one[:, :], 1.0))
                    dve.wait_ge(S("ro_l"), 1)
                    lgp = ps[:, 0, 0:NT * NE].rearrange("p (t e) -> p t e", e=NE)
                    wide = lambda ap: ap.unsqueeze(2).to_broadcast([P, NT, NE])
                    link(dve.tensor_reduce(m1[:, :], lgp, X, ALU.max))
                    dve.tensor_tensor(lg[:, :, :], lgp, wide(m1[:, :]), ALU.subtract).then_inc(S("ro_m"), 1)
                    dve.wait_ge(S("ro_e"), 1)
                    link(dve.tensor_reduce(m1[:, :], lg[:, :, :], X, ALU.add))
                    link(dve.reciprocal(m1[:, :], m1[:, :]))
                    dve.tensor_tensor(lg[:, :, :], lg[:, :, :], wide(m1[:, :]), ALU.mult).then_inc(S("ro_a"), 1)
                    dve.wait_ge(S("ro_a"), 1)
                    dve.tensor_copy(tg[:, :, :, 1], lg[:, :, :])
                    dve.tensor_copy(tg[:, :, :, 0], wide(tok[:, :]))
                    dve.wait_ge(S("ro_t"), 1)
                    for dst in (affT, work):
                        ins = dve.tensor_copy(dst[:, :].rearrange("p (a b) -> p a b", a=2), ps[0:NE, 1:3, :])
                    link(ins)
                    for _i in range(CAP // 8):
                        link(dve.max(m8[:, :], work[:, :]))
                        link(dve.match_replace(work[:, :], m8[:, :], work[:, :], -1.0))
                    link(dve.tensor_scalar(work[:, :], work[:, :], 0.0, None, ALU.is_lt))
                    link(dve.tensor_tensor_scan(affT[:, :], one[:, :], work[:, :], 0.0, ALU.mult, ALU.add))
                    link(dve.tensor_tensor(work[:, :], affT[:, :], work[:, :], ALU.mult))
                    dve.tensor_scalar(work[:, :], work[:, :], -1.0, None, ALU.add).then_inc(S("ro_s"), 1)
                    dve.wait_ge(S("ro_st"), 1)
                    link(dve.tensor_copy(slot[:, :, :].rearrange("p t e -> p (t e)"), ps[:, 3, 0:NT * NE]))
                    for n in range(NE * NT):
                        e, t = divmod(n, NT)
                        if n >= 4:
                            dve.wait_ge(S("ro_sel"), n - 3)
                        dve.tensor_scalar(oh[:, n % 4, :], iota[:, :], slot[:, t, e:e + 1], None, ALU.is_equal
                                          ).then_inc(S("ro_oh"), 1)
                    dve.wait_ge(S("ro_sel"), NE * NT)
                    link(dve.tensor_copy(sel[:, :, :].rearrange("p e x -> p (e x)"), ps[:, 4, 0:2 * NE]))
                    dve.tensor_copy(idx[:, :], sel[:, :, 0])
            dump("sel", sel[:, :, :].rearrange("p e x -> p (e x)"))

            with ExitStack() as st:
                wg = sb(st, "wg", [P, 2, KD, DE])
                wu = sb(st, "wu", [P, 2, KD, DE])
                wd = sb(st, "wd", [P, 2, 4, D])
                xe = sb(st, "xe", [P, 2, D])
                xeT = sb(st, "xeT", [P, KD, P])
                ag = sb(st, "ag", [P, DE])
                au = sb(st, "au", [P, DE])
                aT = sb(st, "aT", [P, 4, P])
                ye = sb(st, "ye", [P, 2, D])
                block = st.enter_context(nc.Block())

                @block.sync
                def _(sp):
                    for e in range(NE):
                        if e >= 2:
                            sp.wait_ge(S("mo_gu"), e - 1)
                        sp.dma_start(wg[:, e % 2], A["w_e_gate_2"][0, e].rearrange("(k p) f -> p k f", p=P)
                                     ).then_inc(S(f"mo_w{e % 2}"), 16)
                        sp.dma_start(wu[:, e % 2], A["w_e_up_2"][0, e].rearrange("(k p) f -> p k f", p=P)
                                     ).then_inc(S(f"mo_w{e % 2}"), 16)
                        if e >= 2:
                            sp.wait_ge(S("mo_d"), e - 1)
                        sp.dma_start(wd[:, e % 2], A["w_e_down_2"][0, e].rearrange("(k p) n -> p k n", p=P)
                                     ).then_inc(S(f"mo_wd{e % 2}"), 16)

                @block.gpsimd
                def _(pool):
                    def gather(e):
                        if e >= 2:
                            pool.wait_ge(S("mo_xt"), e - 1)
                        pool.indirect_dma_start(xe[:, e % 2, :], None, xn_d,
                                                bass.IndirectOffsetOnAxis(ap=idx[:, e:e + 1], axis=0),
                                                ).then_inc(S(f"mo_x{e % 2}"), 16)
                    gather(0)
                    for e in range(NE):
                        if e + 1 < NE:
                            gather(e + 1)
                        pool.wait_ge(S("mo_ye"), 2 * e + 2)
                        if e:
                            pool.wait_ge(S("mo_y"), 16 * e)
                        pool.indirect_dma_start(y_d, bass.IndirectOffsetOnAxis(ap=idx[:, e:e + 1], axis=0),
                                                ye[:, e % 2, :], None, compute_op=ALU.add).then_inc(S("mo_y"), 16)
                    pool.wait_ge(S("mo_y"), 16 * NE)

                @block.tensor
                def _(pe):
                    def xT(e):
                        pe.wait_ge(S(f"mo_x{e % 2}"), 16 * (e // 2 + 1))
                        if e:
                            pe.wait_ge(S("mo_xev"), 8 * e)
                        for k in range(KD):
                            tr = pe.transpose(ps[:, k // 4, (k % 4) * P:(k % 4 + 1) * P], xe[:, e % 2, k * P:(k + 1) * P],
                                              ident[:, :])
                        tr.then_inc(S("mo_xt"), 1)
                    xT(0)
                    for e in range(NE):
                        pe.wait_ge(S("mo_xev"), 8 * e + 8)
                        pe.wait_ge(S(f"mo_w{e % 2}"), 32 * (e // 2 + 1))
                        if e:
                            pe.wait_ge(S("mo_h"), e)
                        for w, b in ((wg, 2), (wu, 3)):
                            for k in range(KD):
                                mm = pe.matmul(ps[:, b, :], xeT[:, k, :], w[:, e % 2, k, :], start=(k == 0), stop=(k == KD - 1))
                            mm.then_inc(S("mo_a"), 1)
                        mm = pe.transpose(ps[:, 7, 0:P], ident[:, :], ident[:, :])
                        mm.then_inc(S("mo_gu"), 1)
                        if e + 1 < NE:
                            xT(e + 1)
                        pe.wait_ge(S("mo_h"), e + 1)
                        for f in range(4):
                            tr = pe.transpose(ps[:, 4, f * P:(f + 1) * P], au[:, f * P:(f + 1) * P], ident[:, :])
                        tr.then_inc(S("mo_ht"), 1)
                        pe.wait_ge(S("mo_hev"), e + 1)
                        pe.wait_ge(S(f"mo_wd{e % 2}"), 16 * (e // 2 + 1))
                        if e:
                            pe.wait_ge(S("mo_ye"), 2 * e)
                        for c in range(2):
                            for f in range(4):
                                mm = pe.matmul(ps[:, 5 + c, :], aT[:, f, :], wd[:, e % 2, f, c * 512:(c + 1) * 512],
                                               start=(f == 0), stop=(f == 3))
                        mm.then_inc(S("mo_d"), 1)

                @block.scalar
                def _(act):
                    for e in range(NE):
                        act.wait_ge(S("mo_a"), 2 * e + 1)
                        if e:
                            act.wait_ge(S("mo_h"), e)
                        act.activation(ag[:, :], ps[:, 2, :], ACT.Silu).then_inc(S("mo_s"), 1)
                        act.wait_ge(S("mo_ht"), e + 1)
                        if e:
                            act.wait_ge(S("mo_d"), e)
                        act.activation(aT[:, :, :].rearrange("p f t -> p (f t)"), ps[:, 4, :], ACT.Copy
                                       ).then_inc(S("mo_hev"), 1)
                        act.wait_ge(S("mo_d"), e + 1)
                        if e >= 2:
                            act.wait_ge(S("mo_y"), 16 * (e - 1))
                        for c in range(2):
                            act.activation(ye[:, e % 2, c * 512:(c + 1) * 512], ps[:, 5 + c, :], ACT.Copy,
                                           scale=sel[:, e, 1:2]).then_inc(S("mo_ye"), 1)

                @block.vector
                def _(dve):
                    def xev(e):
                        dve.wait_ge(S("mo_xt"), e + 1)
                        if e:
                            dve.wait_ge(S("mo_a"), 2 * e)
                        for k in range(KD):
                            dve.tensor_scalar(xeT[:, k, :], ps[:, k // 4, (k % 4) * P:(k % 4 + 1) * P],
                                              gains[:, 5, k:k + 1], gains[:, 6, k:k + 1], ALU.mult, ALU.add
                                              ).then_inc(S("mo_xev"), 1)
                    xev(0)
                    for e in range(NE):
                        dve.wait_ge(S("mo_s"), e + 1)
                        dve.wait_ge(S("mo_a"), 2 * e + 2)
                        if e:
                            dve.wait_ge(S("mo_ht"), e)
                        dve.tensor_tensor(au[:, :], ps[:, 3, :], ag[:, :], ALU.mult).then_inc(S("mo_h"), 1)
                        if e + 1 < NE:
                            xev(e + 1)
            moe.close()

            with ExitStack() as st:
                xf = sb(st, "xf", [P, NT, D])
                yf = sb(st, "yf", [P, NT, D])
                block = st.enter_context(nc.Block())

                @block.sync
                def _(sp):
                    for t in range(NT):
                        sp.dma_start(yf[:, t, :], y_d[t * P:(t + 1) * P, :]).then_inc(S(f"fi_in{t % 4}"), 16)
                        sp.dma_start(xf[:, t, :], x2_d[t * P:(t + 1) * P, :]).then_inc(S(f"fi_in{t % 4}"), 16)
                    for t in range(NT):
                        sp.wait_ge(S("fi_x"), t + 1)
                        sp.dma_start(out[0, t * P:(t + 1) * P, :], xf[:, t, :]).then_inc(S("fi_out"), 16)
                    sp.wait_ge(S("fi_out"), 16 * NT)

                @block.vector
                def _(dve):
                    link = Link(dve, "dve_link")
                    for q_ in range(4):
                        dve.wait_ge(S(f"fi_in{q_}"), 64)
                    for t in range(NT):
                        link(dve.tensor_tensor(yf[:, t, :], yf[:, t, :], g2r[:, :], ALU.mult))
                        dve.tensor_tensor(xf[:, t, :], xf[:, t, :], yf[:, t, :], ALU.add).then_inc(S("fi_x"), 1)
            outer.close()

        w_in = A["w_in"][0]
        x_rows = A["x"][0]
        x1_d = dram("x1_rows", [T, D])
        gates_d = dram("gates", [P, 24, T])
        x2_d = dram("x2_rows", [T, D])
        first = ExitStack()
        ozr = sb(first, "ozr", [P, 4, T])
        h_stack = ExitStack()
        hT = sb(h_stack, "hT", [P, KD, T])
        free_h = h_stack.close
        norm_T(x_rows, NT, hT, gains[:, 0, :], None, tag="n1")
        dump("hT", hT[:, :, :])

        rwkv()
        oza, mga, mgb, mg_ready = attention()
        merge_first()
        first.close()
        if debug is not None and "x1_in" in debug:
            with nc.Block() as block:
                @block.sync
                def _(sp):
                    sp.dma_start(x1_d, A["x1_in"]).then_inc(S("dbgx"), 16)
                    sp.wait_ge(S("dbgx"), 16)
        if debug is None or debug.get("second", 1):
            second()
        dump("end", ident[:, :])


def kernel(**inputs):
    import numpy as _np
    import concourse.bacc as _bacc
    from concourse import mybir as _mybir
    from concourse.bass_utils import run_bass_kernel_spmd as _run

    nc = _bacc.Bacc("TRN2", target_bir_lowering=False, num_devices=1)
    arrays, aps = {}, {}
    for name, a in list(inputs.items()) + list(constants().items()):
        a = _np.ascontiguousarray(a)
        if name == "c_ctx_2":
            a = a.reshape(1, -1)
        arrays[name] = a
        aps[name] = nc.dram_tensor(name, a.shape, _mybir.dt.from_np(a.dtype), kind="ExternalInput").ap()
    out = nc.dram_tensor("out_0", (1, T, D), F32, kind="ExternalOutput").ap()
    build(nc, aps, out)
    r = _run(nc, [arrays], core_ids=[0])
    return r.results[0]["out_0"]
```

```python
import math
from contextlib import ExitStack

import numpy as np

import concourse.bass as bass
from concourse import mybir

F32 = mybir.dt.float32
F32R = mybir.dt.float32r
U32 = mybir.dt.uint32
ALU = mybir.AluOpType
ACT = mybir.ActivationFunctionType
X = mybir.AxisListType.X

P = 128
T = 1024
NT = T // P
D = 1024
KD = D // P
HEADS = 8
HD = 64
AW = HEADS * HD
DILATIONS = (1, 4, 16)
STEPS = 128
MASKED = -1e30
QKV = 9 * AW
OFF_Z = QKV
OFF_RWKV = OFF_Z + AW
OFF_ZR = OFF_RWKV + 3 * AW + 128
OFF_MERGE = OFF_ZR + AW
C = 64
SUB = 16
DECAY = math.exp(-0.5)
GN_EPS = 64e-5
EPS = 1e-6
CTX = 256
NTC = CTX // P
QKD, NOPE, ROPE, VD = 96, 64, 32, 64
QL, KVL = 384, 256
OFF_F = QL + KVL + ROPE
OFF_GA = OFF_F + 512
NE, DE, CAP = 16, 512, 128
NKEY = T + CTX
NKT = NKEY // P


def bucket(dist):
    d = np.maximum(np.asarray(dist), 0)
    ratio = np.log(np.maximum(d, 1).astype(np.float32) / 16) / np.float32(math.log(2048 / 16))
    large = np.minimum(16 + (ratio * 16).astype(np.int32), 31)
    return np.where(d < 16, d, large).astype(np.int32)


def stride_of(dil):
    return min(dil, T // P)


def constants():
    f = np.float32
    i = np.arange(P)
    c = {"c_ident": np.eye(P, dtype=f)}
    c["c_hones"] = (i[:, None] // HD == i[None] // HD).astype(f)
    c["c_ones"] = np.ones((P, P), f)
    c["c_resets"] = np.tile((np.arange(T) % C != 0).astype(f), (P, 1))
    same = i[:, None] // C == i[None] // C
    c["c_mask_ar"] = np.concatenate([same & (i[:, None] < i[None]), same & (i[:, None] <= i[None])], 1).astype(f)
    c["c_mask_off"] = (same & (i[:, None] > i[None]) & (i[:, None] // SUB != i[None] // SUB)).astype(f)
    c["c_eye64"] = np.tile(np.eye(C, dtype=f), (2, 1))
    y = np.arange(383)
    rel = 255 - y
    hot = np.zeros((33, 3, 384), f)
    for g, dil in enumerate(DILATIONS):
        step = stride_of(dil)
        valid = (rel >= 0) & (rel * step <= STEPS * dil) & (rel * step % dil == 0)
        b = bucket(np.maximum(rel, 0) * step)
        for n in range(383):
            hot[b[n] if valid[n] else 32, g, n] = 1
    c["c_hot"] = hot
    c["c_eye16"] = np.tile(np.eye(SUB, dtype=f).reshape(1, 1, -1), (P, 4, 1)).reshape(P, -1)
    a = 2 * np.pi * np.outer(i, i) / P
    c["c_dft_ch"] = np.concatenate([np.cos(a), np.sin(a)], 1).astype(f)
    p = np.arange(T // 2)[:, None]
    s = 1 / math.sqrt(T * P)
    pos = np.zeros((T // 2, 2, 2, T // 2), np.float64)
    for par in range(2):
        k = 2 * np.arange(T // 2)[None] + par
        a = 2 * np.pi * ((p * k) % T) / T
        pos[:, par, 0] = np.cos(a) * s
        pos[:, par, 1] = -np.sin(a) * s
    c["c_dft_pos"] = pos.astype(f)
    inv = (1.0 / (np.float32(10000.0) ** (np.arange(8, dtype=f) / 8))).astype(f)
    t = np.arange(T)
    ang = [np.concatenate([q.astype(f)[:, None] * inv] * 2, 1) for q in (t // 64, t % 64)]
    sign = np.concatenate([-np.ones(8), np.ones(8)]).astype(f)
    c["c_rope"] = np.stack([np.concatenate([np.cos(x) for x in ang], 1),
                            np.concatenate([np.sin(x) * sign for x in ang], 1)], 1).astype(f)
    c["c_slot"] = np.tile(np.arange(CAP, dtype=f), (P, 1))
    c["c_tok"] = (np.arange(NT)[None] * P + i[:, None]).astype(f)
    return c


def build(nc, A, out, debug=None):
    ctx = ExitStack()
    sems = {}
    used = {}

    def S(name):
        if name not in sems:
            sems[name] = nc.alloc_semaphore(name=name)
        return sems[name]

    def retire(*prefixes):
        over = [n for n in sems if n.startswith(prefixes)]
        nc.clear_and_free_semaphores([sems.pop(n) for n in over])
        for n in over:
            used.pop(n, None)
        with nc.Block() as block:
            @block.gpsimd
            def _(gp):
                gp.engine_nop()

    def sb(stack, name, shape, dt=F32):
        return stack.enter_context(nc.sbuf_tensor(name, shape, dt))

    def dram(name, shape, dt=F32):
        return nc.dram_tensor(name, shape, dt, kind="Internal").ap()

    def dump(name, ap):
        if debug is None or name not in debug:
            return
        with nc.Block() as block:
            @block.sync
            def _(sp):
                s = S("dbg")
                debug[name]["n"] = debug["_"] = debug.get("_", 0) + 16
                sp.dma_start(debug[name]["ap"], ap).then_inc(s, 16)
                sp.wait_ge(s, debug["_"])

    class Link:

        def __init__(self, eng, name):
            self.eng, self.sem = eng, S(name)
            self.n = Link.last.get(name, 0)
            self.name = name

        def __call__(self, ins):
            self.n += 1
            Link.last[self.name] = self.n
            ins.then_inc(self.sem, 1)
            self.eng.wait_ge(self.sem, self.n)

    Link.last = {}

    def base(name, count):
        b = used.get(name, 0)
        used[name] = b + count
        return b

    with ctx:
        ps = ctx.enter_context(nc.psum_tensor("ps", [P, 8, 512], F32))
        S("fi_out")
        ident = sb(ctx, "ident", [P, P])
        ones = sb(ctx, "ones", [P, P])
        gains = sb(ctx, "gains", [P, 9, 8])
        modv = sb(ctx, "modv", [P, 6, KD, 2])

        def load(pairs):
            with nc.Block() as block:
                @block.sync
                def _(sp):
                    b = base("loaded", 16 * len(pairs))
                    for dst, src in pairs:
                        with nc.allow_non_contiguous_dma("per-channel vectors"):
                            sp.dma_start(dst, src).then_inc(S("loaded"), 16)
                    sp.wait_ge(S("loaded"), b + 16 * len(pairs))

        def start_load(name, pairs):
            b = base(name, 16 * len(pairs))
            with nc.Block() as block:
                @block.sync
                def _(sp):
                    for dst, src in pairs:
                        sp.dma_start(dst, src).then_inc(S(name), 16)
            return b + 16 * len(pairs)

        def vec(ap, n=KD):
            return ap.rearrange("(k p) -> p k", p=P)


        def pair(stack, name, shape):
            return sb(stack, name + "_hi", shape, F32R), sb(stack, name + "_lo", shape, F32R)

        def high(act, dst, src):
            return act.activation(dst, src, ACT.Copy)

        def low(dve, dst, src, hi):
            return dve.tensor_tensor(dst, src, hi.bitcast(F32), ALU.subtract)

        def products(pe, out, a, b, first, last):
            pe.matmul(out, a[1], b[0], start=first, stop=False)
            pe.matmul(out, a[0], b[1], start=False, stop=False)
            return pe.matmul(out, a[0], b[0], start=False, stop=last)

        SPLIT = 1024

        def gemm(jobs, ring=6, banks=8, side=None, pool=None):
            pieces, groups = [], []
            for job in jobs:
                w = job["w"]
                kt, cols = w.shape[1], w.shape[2]
                first = len(pieces)
                if job["mode"] == "T":
                    for m in range(cols // P):
                        pieces.append((w[:, :, m * P:(m + 1) * P], kt, P))
                        groups += [(job, m, x, [(first + m, k, k) for k in range(kt)]) for x in range(job["tiles"])]
                else:
                    per = min(kt, SPLIT // cols)
                    for k in range(0, kt, per):
                        pieces.append((w[:, k:min(k + per, kt), :], min(per, kt - k), cols))
                    groups += [(job, m, 0, [(first + k // per, k % per, k) for k in range(kt)])
                               for m in range(job["tiles"])]
            NP, NG = len(pieces), len(groups)
            last_use = [max(n for n, g in enumerate(groups) if any(u[0] == i for u in g[3])) for i in range(NP)]
            on_act = []
            for job, m, x, _u in groups:
                on = job.get("on", "alt")
                on_act.append(len(on_act) % 2 == 0 if on == "alt" else on == "act")
            place = [sum(a == on_act[n] for a in on_act[:n + 1]) for n in range(NG)]
            order = [("split", i) for i in range(min(ring, NP))]
            for n in range(NG):
                order += [("split", i) for i in range(ring, NP) if last_use[i - ring] == n]
                order.append(("evac", n))
            braw = [base(f"gemm_raw{b}", 16 * len(range(b, NP, 2))) for b in range(2)]
            bhi, blo, bmm = base("gemm_hi", NP), base("gemm_lo", NP), base("gemm_mm", NG)
            bev = [base("gemm_ev0", sum(on_act)), base("gemm_ev1", NG - sum(on_act))]
            ev = lambda n: (S("gemm_ev0" if on_act[n] else "gemm_ev1"), bev[not on_act[n]] + place[n])
            with ExitStack() as st:
                raw = sb(st, f"raw{bmm}", [P, 2, SPLIT])
                whi, wlo = pair(st, f"w{bmm}", [P, ring, SPLIT])
                view = lambda ap, i: ap[:, 0:pieces[i][1] * pieces[i][2]]
                block = st.enter_context(nc.Block())

                @block.sync
                def _(sp):
                    for i, (w, kn, cols) in enumerate(pieces):
                        if i >= 2:
                            sp.wait_ge(S("gemm_hi"), bhi + i - 1)
                            sp.wait_ge(S("gemm_lo"), blo + i - 1)
                        sp.dma_start(raw[:, i % 2, 0:kn * cols].rearrange("p (k n) -> p k n", k=kn), w
                                     ).then_inc(S(f"gemm_raw{i % 2}"), 16)

                if pool is not None:
                    @block.gpsimd
                    def _(gp):
                        pool(gp)

                @block.tensor
                def _(pe):
                    ready = -1
                    for n, (job, m, x, uses) in enumerate(groups):
                        if m == 0 and x == 0 and job.get("ready"):
                            for name, value in job["ready"]:
                                pe.wait_ge(S(name), value)
                        if n >= banks:
                            pe.wait_ge(*ev(n - banks))
                        for i, at, k in uses:
                            if i > ready:
                                pe.wait_ge(S("gemm_hi"), bhi + i + 1)
                                pe.wait_ge(S("gemm_lo"), blo + i + 1)
                                ready = i
                            cols = pieces[i][2]
                            w = (whi[:, i % ring, at * cols:(at + 1) * cols], wlo[:, i % ring, at * cols:(at + 1) * cols])
                            first, last = k == uses[0][2], k == uses[-1][2]
                            if job["mode"] == "T":
                                a = job["act"](k, x)
                                mm = products(pe, ps[:, n % banks, 0:a[0].shape[-1]], w, a, first, last)
                            else:
                                mm = products(pe, ps[:, n % banks, 0:cols], job["act"](k, m), w, first, last)
                        mm.then_inc(S("gemm_mm"), 1)
                        if side is not None and n in side["at"]:
                            side["pe"](pe, side["at"][n])

                @block.scalar
                def _(act):
                    for what, n in order:
                        if what == "split":
                            act.wait_ge(S(f"gemm_raw{n % 2}"), braw[n % 2] + 16 * (n // 2 + 1))
                            if n >= ring:
                                act.wait_ge(S("gemm_mm"), bmm + last_use[n - ring] + 1)
                            high(act, view(whi[:, n % ring, :], n), view(raw[:, n % 2, :], n)).then_inc(S("gemm_hi"), 1)
                        else:
                            job, m, x, _u = groups[n]
                            if on_act[n]:
                                act.wait_ge(S("gemm_mm"), bmm + n + 1)
                                job["evac"]("act", act, ps[:, n % banks, :], m, x).then_inc(S("gemm_ev0"), 1)
                            if "act_step" in job:
                                job["act_step"](act, m, x, ev(n))

                @block.vector
                def _(dve):
                    for what, n in order:
                        if what == "split":
                            dve.wait_ge(S("gemm_hi"), bhi + n + 1)
                            low(dve, view(wlo[:, n % ring, :], n), view(raw[:, n % 2, :], n),
                                view(whi[:, n % ring, :], n)).then_inc(S("gemm_lo"), 1)
                        else:
                            job, m, x, _u = groups[n]
                            if not on_act[n]:
                                dve.wait_ge(S("gemm_mm"), bmm + n + 1)
                                job["evac"]("dve", dve, ps[:, n % banks, :], m, x).then_inc(S("gemm_ev1"), 1)
                            if "dve_step" in job:
                                job["dve_step"](dve, m, x)
                            if side is not None and n in side["at"]:
                                side["dve"](dve, side["at"][n])

        def copy(kind, eng, dst, src):
            if kind == "act":
                return eng.activation(dst, src, ACT.Copy)
            return eng.tensor_copy(dst, src)

        def wcols(w, a, b):
            return w[:, a:b].rearrange("(k p) n -> p k n", p=P)

        def norm_T(src, nt, gain, shift, to, dst=None, rows_out=None, tag="n"):
            with ExitStack() as st:
                xa = sb(st, f"{tag}_x", [P, 3, D])
                sq = sb(st, f"{tag}_sq", [P, D])
                ss = sb(st, f"{tag}_ss", [P, nt])
                tmp = sb(st, f"{tag}_tmp", [P, 4, 4, P]) if dst is None else None
                place = lambda t, b: (tmp[:, (2 * t + b) % 4] if dst is None else
                                      dst[:, 4 * b:4 * b + 4, t * P:(t + 1) * P])
                names = {"x0": 16 * len(range(0, nt, 3)), "x1": 16 * len(range(1, nt, 3)), "x2": 16 * len(range(2, nt, 3)),
                         "ss": nt, "mean": nt, "root": nt, "rcp": nt, "xn": nt, "t": 2 * nt, "ev": 2 * nt,
                         "hi": 2 * nt if to else 0, "lo": 2 * nt if to else 0, "out": 16 * nt if rows_out is not None else 0}
                b0 = {n: base("norm_" + n, c) for n, c in names.items()}
                at = lambda eng, n, v: eng.wait_ge(S("norm_" + n), b0[n] + v)
                block = st.enter_context(nc.Block())

                @block.sync
                def _(sp):
                    for t in range(nt):
                        if t >= 3:
                            at(sp, "t", 2 * (t - 2))
                            if rows_out is not None:
                                at(sp, "out", 16 * (t - 2))
                        sp.dma_start(xa[:, t % 3, :], src[t * P:(t + 1) * P, :]).then_inc(S(f"norm_x{t % 3}"), 16)

                if rows_out is not None:
                    @block.gpsimd
                    def _(gp):
                        for t in range(nt):
                            at(gp, "xn", t + 1)
                            gp.dma_start(rows_out[t * P:(t + 1) * P, :], xa[:, t % 3, :]).then_inc(S("norm_out"), 16)
                            at(gp, "out", 16 * (t + 1))

                @block.scalar
                def _(act):
                    def squares(t):
                        at(act, f"x{t % 3}", 16 * (t // 3 + 1))
                        if t:
                            at(act, "ss", t)
                        act.activation(sq[:, :], xa[:, t % 3, :], ACT.Square, accum_out=ss[:, t:t + 1]
                                       ).then_inc(S("norm_ss"), 1)

                    def highs(t):
                        for b in range(2):
                            at(act, "ev", 2 * t + b + 1)
                            high(act, to[0][:, 4 * b:4 * b + 4, t * P:(t + 1) * P], place(t, b)).then_inc(S("norm_hi"), 1)
                    squares(0)
                    for t in range(nt):
                        if t + 1 < nt:
                            squares(t + 1)
                        at(act, "mean", t + 1)
                        act.activation(ss[:, t:t + 1], ss[:, t:t + 1], ACT.Sqrt).then_inc(S("norm_root"), 1)
                        if t and to:
                            highs(t - 1)
                        at(act, "rcp", t + 1)
                        act.activation(xa[:, t % 3, :], xa[:, t % 3, :], ACT.Copy, scale=ss[:, t:t + 1]
                                       ).then_inc(S("norm_xn"), 1)
                    if to:
                        highs(nt - 1)

                @block.vector
                def _(dve):
                    link = Link(dve, "dve_link")
                    wide = lambda v, b: v[:, 4 * b:4 * b + 4].unsqueeze(2).to_broadcast([P, 4, P])

                    def evacs(t):
                        if t >= 2 and dst is None:
                            at(dve, "lo", 2 * (t - 1))
                        for b in range(2):
                            at(dve, "t", 2 * t + b + 1)
                            src_ = ps[:, (2 * t + b) % 8, :].rearrange("p (k t) -> p k t", t=P)
                            ins = dve.tensor_tensor(place(t, b), src_, wide(gain, b), ALU.mult)
                            if shift is not None:
                                link(ins)
                                ins = dve.tensor_tensor(place(t, b), place(t, b), wide(shift, b), ALU.add)
                            ins.then_inc(S("norm_ev"), 1)

                    def lows(t):
                        for b in range(2):
                            at(dve, "hi", 2 * t + b + 1)
                            cut_ = (slice(None), slice(4 * b, 4 * b + 4), slice(t * P, (t + 1) * P))
                            low(dve, to[1][cut_], place(t, b), to[0][cut_]).then_inc(S("norm_lo"), 1)
                    for t in range(nt):
                        at(dve, "ss", t + 1)
                        dve.tensor_scalar(ss[:, t:t + 1], ss[:, t:t + 1], 1.0 / D, EPS, ALU.mult, ALU.add
                                          ).then_inc(S("norm_mean"), 1)
                        if t:
                            evacs(t - 1)
                        at(dve, "root", t + 1)
                        dve.reciprocal(ss[:, t:t + 1], ss[:, t:t + 1]).then_inc(S("norm_rcp"), 1)
                        if t and to:
                            lows(t - 1)
                    evacs(nt - 1)
                    if to:
                        lows(nt - 1)

                @block.tensor
                def _(pe):
                    for t in range(nt):
                        at(pe, "xn", t + 1)
                        for b in range(2):
                            if t >= 4:
                                at(pe, "ev", 2 * (t - 4) + b + 1)
                            for j in range(4):
                                k = 4 * b + j
                                tr = pe.transpose(ps[:, (2 * t + b) % 8, j * P:(j + 1) * P],
                                                  xa[:, t % 3, k * P:(k + 1) * P], ident[:, :])
                            tr.then_inc(S("norm_t"), 1)

        def whole(p, w=512):
            return lambda k, x: tuple(h[:, k, x * w:(x + 1) * w] for h in p)

        def token_tiles(p):
            return lambda k, m: tuple(h[:, k, m * P:(m + 1) * P] for h in p)

        def rwkv():
            keep = ExitStack()
            kv = sb(keep, "kv", [P, 8, T + 1])
            pc = sb(keep, "pc", [P, 4, T // C])
            vecs = sb(keep, "rw_vecs", [P, 8, 4])
            mix = sb(keep, "rw_mix", [P, 13])
            hones = sb(keep, "hones", [P, P])
            rl = sb(keep, "rl", [P, 5, T + 1])
            lora = sb(keep, "lora", [P, AW])
            names = ["rwkv_w0", "rwkv_a0", "rwkv_k_k", "rwkv_k_a", None, "rwkv_ln_w", "rwkv_ln_b"]
            pairs = [(vecs[:, i, :], vec(A[n][0], 4)) for i, n in enumerate(names) if n]
            pairs += [(vecs[:, 4, :], vec(A["rwkv_r_k"][0].rearrange("h n -> (h n)"), 4)),
                      (mix[:, :], vec(A["rwkv_shift_mix"][0], 13)), (hones[:, :], A["c_hones"]),
                      (lora[0:64, :], A["rwkv_w_up"][0]), (lora[64:P, :], A["rwkv_a_up"][0])]
            load(pairs + [(gains[:, 0, :], vec(A["pre_norm_gain"][0])), (ident[:, :], A["c_ident"]),
                          (ones[:, :], A["c_ones"])])
            hpair = ExitStack()
            hp = pair(hpair, "h", [P, KD, T])
            norm_T(x_rows, NT, gains[:, 0, :], None, hp, dst=hT, tag="n1")

            def place_of(c):
                return rl[:, c, :] if c < 4 else rl[:, 4, :] if c == 12 else kv[:, c - 4, :]

            def keep_h(gp):
                gp.dma_start(h_d, hT[:, :, :]).then_inc(S("h_out"), 16)
                gp.wait_ge(S("h_out"), 16)
            gemm([dict(w=wcols(w_in, OFF_RWKV, OFF_RWKV + 1664), mode="T", act=whole(hp), tiles=2,
                       evac=lambda kind, eng, src, m, x: copy(
                           kind, eng, place_of(m)[:, 1 + x * 512:513 + x * 512], src))], ring=3, pool=keep_h)
            hpair.close()
            ar = sb(keep, "ar", [P, 4, NT, 2, P])
            bt = sb(keep, "bt", [P, 4, T])
            bonus = sb(keep, "bonus", [P, 4, T])
            ozr = sb(keep, "ozr", [P, 4, T])

            with ExitStack() as st:
                diff = sb(st, "diff", [P, T])
                block = st.enter_context(nc.Block())

                @block.vector
                def _(dve):
                    link = Link(dve, "dve_link")
                    dve.memset(rl[:, :, 0:1], 0.0)
                    link(dve.memset(kv[:, :, 0:1], 0.0))
                    link(dve.tensor_scalar(vecs[:, 7, :], vecs[:, 3, :], -1.0, 1.0, ALU.mult, ALU.add))
                    for c in range(13):
                        pr = place_of(c)
                        link(dve.tensor_tensor(diff[:, :], pr[:, 0:T], pr[:, 1:T + 1], ALU.subtract))
                        link(dve.scalar_tensor_tensor(pr[:, 1:T + 1], diff[:, :], mix[:, c:c + 1],
                                                      pr[:, 1:T + 1], ALU.mult, ALU.add))

            with ExitStack() as st:
                def t_(n):
                    return sb(st, "rw_" + n, [P, T])
                sig, a, cs, csm, pi, kk, w1, w2 = map(t_, ["sig", "a", "cs", "csm", "pi", "kk", "w1", "w2"])
                resets = sb(st, "resets", [P, T])
                load([(resets[:, :], A["c_resets"])])
                pr_, pp = sig, csm
                block = st.enter_context(nc.Block())
                two = lambda b: ps[:, b:b + 2, :].rearrange("p a b -> p (a b)")

                @block.tensor
                def _(pe):
                    pe.wait_ge(S("rw_tanh"), 1)
                    for c in range(4):
                        if c:
                            pe.wait_ge(S("rw_sig"), 2 * c)
                        for hf in range(2):
                            cols = slice(1 + hf * 512, 513 + hf * 512)
                            pe.matmul(ps[:, hf, :], lora[0:64, c * P:(c + 1) * P], rl[0:64, 4, cols],
                                      start=True, stop=True)
                            mm = pe.matmul(ps[:, 2 + hf, :], lora[64:P, c * P:(c + 1) * P], rl[64:P, 4, cols],
                                           start=True, stop=True)
                        mm.then_inc(S("rw_lora"), 1)
                        for name, src, b in (("rw_ksq", w1, 4), ("rw_rk", w2, 6)):
                            pe.wait_ge(S(name), c + 1)
                            for hf in range(2):
                                mm = pe.matmul(ps[:, b + hf, :], hones[:, :], src[:, hf * 512:(hf + 1) * 512],
                                               start=True, stop=True)
                            mm.then_inc(S(name + "_sum"), 1)

                @block.scalar
                def _(act):
                    act.activation(rl[0:64, 4, 1:T + 1], rl[0:64, 4, 1:T + 1], ACT.Tanh).then_inc(S("rw_tanh"), 1)
                    for c in range(4):
                        act.wait_ge(S("rw_lora"), c + 1)
                        if c:
                            act.wait_ge(S("rw_tile"), c)
                        act.activation(sig[:, :], two(0), ACT.Sigmoid, bias=vecs[:, 0, c:c + 1]).then_inc(S("rw_sig"), 1)
                        act.activation(a[:, :], two(2), ACT.Sigmoid, bias=vecs[:, 1, c:c + 1]).then_inc(S("rw_sig"), 1)
                        act.wait_ge(S("rw_cs"), c + 1)
                        act.activation(pr_[:, :], cs[:, :], ACT.Exp, scale=-DECAY).then_inc(S("rw_exp"), 1)
                        act.activation(pi[:, :], cs[:, :], ACT.Exp, scale=DECAY).then_inc(S("rw_exp"), 1)
                        act.activation(pp[:, :], csm[:, :], ACT.Exp, scale=-DECAY).then_inc(S("rw_exp"), 1)
                        act.wait_ge(S("rw_nrm"), c + 1)
                        act.activation(w1[:, :], w1[:, :], ACT.Sqrt).then_inc(S("rw_root"), 1)

                @block.vector
                def _(dve):
                    link = Link(dve, "dve_link")
                    for c in range(4):
                        k_ = kv[:, c, 1:T + 1]
                        v_ = kv[:, 4 + c, 1:T + 1]
                        r_ = rl[:, c, 1:T + 1]
                        by_tile = lambda ap: ap.rearrange("p (n t) -> p n t", t=P)
                        link(dve.tensor_scalar(kk[:, :], k_, vecs[:, 2, c:c + 1], None, ALU.mult))
                        dve.tensor_tensor(w1[:, :], kk[:, :], kk[:, :], ALU.mult).then_inc(S("rw_ksq"), 1)
                        dve.wait_ge(S("rw_sig"), 2 * c + 2)
                        link(dve.tensor_tensor_scan(cs[:, :], resets[:, :], sig[:, :], 0.0, ALU.mult, ALU.add))
                        dve.tensor_tensor(csm[:, :], cs[:, :], sig[:, :], ALU.subtract).then_inc(S("rw_cs"), 1)
                        dve.wait_ge(S("rw_ksq_sum"), c + 1)
                        dve.tensor_scalar(w1[:, :], two(4), 1e-24, None, ALU.max).then_inc(S("rw_nrm"), 1)
                        link(dve.tensor_scalar(w2[:, :], a[:, :], vecs[:, 3, c:c + 1], vecs[:, 7, c:c + 1],
                                               ALU.mult, ALU.add))
                        link(dve.tensor_tensor(k_, k_, w2[:, :], ALU.mult))
                        link(dve.scalar_tensor_tensor(w2[:, :], r_, vecs[:, 4, c:c + 1], k_, ALU.mult, ALU.mult))
                        dve.engine_nop().then_inc(S("rw_rk"), 1)
                        dve.wait_ge(S("rw_exp"), 3 * c + 3)
                        dve.tensor_tensor(by_tile(k_), by_tile(k_), by_tile(pi[:, :]), ALU.mult)
                        dve.tensor_tensor(ar[:, c, :, 1, :], by_tile(r_), by_tile(pr_[:, :]), ALU.mult)
                        dve.tensor_copy(pc[:, c, :], pr_[:, C - 1:T:C])
                        dve.wait_ge(S("rw_root"), c + 1)
                        link(dve.reciprocal(w1[:, :], w1[:, :]))
                        link(dve.tensor_tensor(kk[:, :], kk[:, :], w1[:, :], ALU.mult))
                        dve.scalar_tensor_tensor(ar[:, c, :, 0, :], by_tile(kk[:, :]), -1.0, by_tile(pp[:, :]),
                                                 ALU.mult, ALU.mult)
                        link(dve.tensor_tensor(w1[:, :], kk[:, :], a[:, :], ALU.mult))
                        dve.tensor_tensor(bt[:, c, :], w1[:, :], pi[:, :], ALU.mult)
                        dve.wait_ge(S("rw_rk_sum"), c + 1)
                        dve.tensor_tensor(bonus[:, c, :], two(6), v_, ALU.mult).then_inc(S("rw_tile"), 1)
                        dve.wait_ge(S("rw_tile"), c + 1)
            dump("ar", ar[:, :, :, :, :].rearrange("p a b c d -> p (a b c d)"))
            dump("bt", bt[:, :, :])
            dump("bonus", bonus[:, :, :])

            l_d = dram("rw_l", [NT * HEADS, P, P])
            w_d = dram("rw_w", [P, 4 * SUB * SUB])
            masks = sb(keep, "rw_masks", [P, 4, P])
            eye64 = sb(keep, "eye64", [P, C])
            load([(masks[:, 0, :], A["c_mask_off"]), (masks[:, 1, :], A["c_mask_ar"][:, P:2 * P]),
                  (masks[:, 2, :], A["c_mask_ar"][:, 0:P]), (masks[:, 3, :], A["c_mask_ar"][:, P:2 * P]),
                  (eye64[:, :], A["c_eye64"])])
            with ExitStack() as st:
                lbuf = sb(st, "lbuf", [P, 2, HEADS, P])
                lt = sb(st, "lt", [P, 4, SUB, SUB])
                wt = sb(st, "wt", [P, 4, SUB, SUB])
                tmp = sb(st, "wtmp", [P, 4 * SUB * SUB])
                block = st.enter_context(nc.Block())

                @block.tensor
                def _(pe):
                    for tt in range(NT):
                        if tt >= 4:
                            pe.wait_ge(S("rw_lev"), 2 * (tt - 3))
                        for h in range(HEADS):
                            rows = slice(64 * (h % 2), 64 * (h % 2) + 64)
                            mm = pe.matmul(ps[:, 2 * (tt % 4) + h % 2, (h // 2) * P:(h // 2 + 1) * P],
                                           bt[rows, h // 2, tt * P:(tt + 1) * P], ar[rows, h // 2, tt, 0, :],
                                           start=True, stop=True)
                        mm.then_inc(S("rw_lmm"), 1)

                @block.vector
                def _(dve):
                    link = Link(dve, "dve_link")
                    for tt in range(NT):
                        dve.wait_ge(S("rw_lmm"), tt + 1)
                        if tt >= 2:
                            dve.wait_ge(S(f"rw_ldump{tt % 2}"), 16 * (tt // 2))
                        for par in range(2):
                            dve.tensor_tensor(lbuf[:, tt % 2, par::2, :],
                                              ps[:, 2 * (tt % 4) + par, :].rearrange("p (h t) -> p h t", t=P),
                                              masks[:, 2:3, :].to_broadcast([P, 4, P]),
                                              ALU.mult).then_inc(S("rw_lev"), 1)
                    dve.wait_ge(S("rw_lin"), 16 * 9)
                    for t in range(1, SUB):
                        v = tmp[:, 0:4 * t * t].rearrange("p (b j s) -> p b j s", b=4, j=t)
                        coef = lt[:, :, 0:t, t:t + 1].rearrange("p b s o -> p b o s").to_broadcast([P, 4, t, t])
                        if t == 1:
                            link(dve.tensor_copy(wt[:, :, 0, 1], lt[:, :, 0, 1]))
                            continue
                        link(dve.tensor_tensor(v, wt[:, :, 0:t, 0:t], coef, ALU.mult))
                        link(dve.tensor_reduce(wt[:, :, 0:t, t], v, X, ALU.add))
                    dve.engine_nop().then_inc(S("rw_inv"), 1)

                @block.sync
                def _(sp):
                    sp.dma_start(wt[:, :, :, :].rearrange("p a b c -> p (a b c)"), A["c_eye16"]).then_inc(S("rw_lin"), 16)
                    for tt in range(NT):
                        sp.wait_ge(S("rw_lev"), 2 * tt + 2)
                        sp.dma_start(l_d[tt * HEADS:(tt + 1) * HEADS].rearrange("h s t -> s h t"),
                                     lbuf[:, tt % 2, :, :]).then_inc(S(f"rw_ldump{tt % 2}"), 16)
                    for b in range(2):
                        sp.wait_ge(S(f"rw_ldump{b}"), 16 * NT // 2)
                    for half in range(2):
                        for blk in range(4):
                            o = half * 64 + blk * SUB
                            sp.dma_start(lt[half * 64:half * 64 + 64, blk, :, :],
                                         l_d[:, o:o + SUB, o:o + SUB]).then_inc(S("rw_lin"), 16)
                    sp.wait_ge(S("rw_inv"), 1)
                    sp.dma_start(w_d, wt[:, :, :, :].rearrange("p a b c -> p (a b c)")).then_inc(S("rw_wout"), 16)
                    sp.wait_ge(S("rw_wout"), 16)

            with ExitStack() as st:
                scratch = rl[:, :, :].rearrange("p a b -> p (a b)")
                ti = scratch[:, 0:2048].rearrange("p (a h t) -> p a h t", a=2, t=P)
                m = scratch[:, 2048:4096].rearrange("p (h a t) -> p h a t", h=4, t=P)
                rhs = scratch[:, 4096:4608].rearrange("p (h c) -> p h c", h=4)
                tb = sb(st, "rw_tb", [P, 4, C])
                tkv = sb(st, "rw_tkv", [P, 2, 4, C])
                ft = sb(st, "rw_ft", [P, 4, P])
                z = sb(st, "rw_z", [P, 4, P])
                xb = sb(st, "rw_x", [P, 2, 4, P])
                gb = sb(st, "rw_gb", [P, 2, 2, C])
                hb = sb(st, "rw_hb", [P, 2, 2, C])
                qb = sb(st, "rw_qb", [P, 2, P])
                yi = sb(st, "rw_yi", [P, 2, P])
                state = sb(st, "rw_state", [P, 3, 4, C])
                s1 = sb(st, "rw_s1", [P, 2, C])
                gw = sb(st, "gate_w", [P, 3, KD, P])
                go = sb(st, "gate_out", [P, 2, 512])
                w_v = w_d.rearrange("(x u) (b s t) -> x b s u t", x=2, b=4, s=SUB)
                block = st.enter_context(nc.Block())
                rounds = [(tt, rd) for tt in range(NT) for rd in range(2)]
                GATES = 24
                assert 2 * GATES == 3 * len(rounds)

                @block.sync
                def _(sp):
                    def blocks(tt):
                        for half in range(2):
                            for blk in range(4):
                                o = half * 64 + blk * SUB
                                sp.dma_start(ti[o:o + SUB, tt % 2, :, o:o + SUB],
                                             w_v[half, blk, :, tt * HEADS:(tt + 1) * HEADS, :]
                                             ).then_inc(S(f"rw_ti{tt % 2}"), 16)

                    def gate_weights(m):
                        off = (OFF_ZR + m * P, OFF_Z + (m - 4) * P, OFF_MERGE + (m - 8) * P)[min(m // 4, 2)]
                        sp.dma_start(gw[:, m % 3], wcols(w_in, off, off + P)).then_inc(S(f"gate_w{m % 3}"), 16)

                    sp.wait_ge(S("rw_zeroed"), 2)
                    blocks(0)
                    for m in range(3):
                        gate_weights(m)
                    for r in range(len(rounds)):
                        if r % 2 == 0 and r // 2 + 1 < NT:
                            if r:
                                sp.wait_ge(S("rw_ymm"), r)
                            blocks(r // 2 + 1)
                        for n in range(3 * r, 3 * r + 3):
                            m, hf = divmod(n, 2)
                            sp.wait_ge(S("gate_ev"), n + 1)
                            sp.dma_start(gates_d[:, m, hf * 512:(hf + 1) * 512], go[:, n % 2, :]
                                         ).then_inc(S(f"gate_out{n % 2}"), 16)
                            if hf == 1 and m + 3 < GATES:
                                gate_weights(m + 3)
                    for x in range(2):
                        sp.wait_ge(S(f"gate_out{x}"), 16 * GATES)

                @block.tensor
                def _(pe):
                    queue = [(n, k) for n in range(2 * GATES) for k in range(KD)]

                    def gate_products(count):
                        for _i in range(count):
                            n, k = queue.pop(0)
                            m, hf = divmod(n, 2)
                            if k == 0:
                                pe.wait_ge(S(f"gate_w{m % 3}"), 16 * (m // 3 + 1))
                                if n:
                                    pe.wait_ge(S("gate_ev"), n)
                            mm = pe.matmul(ps[:, 7, :], gw[:, m % 3, k, :], hT[:, k, hf * 512:(hf + 1) * 512],
                                           start=(k == 0), stop=(k == KD - 1))
                            if k == KD - 1:
                                mm.then_inc(S("gate_mm"), 1)

                    for r, (tt, rd) in enumerate(rounds):
                        tok = slice(tt * P, (tt + 1) * P)
                        pe.wait_ge(S("rw_y"), r) if r else None
                        for cc in range(2):
                            c = 2 * rd + cc
                            pe.transpose(ps[:, 0, cc * P:(cc + 1) * P], ar[:, c, tt, 0, :], ident[:, :])
                            pe.transpose(ps[:, 0, 256 + cc * P:256 + (cc + 1) * P], bt[:, c, tok], ident[:, :])
                            pe.transpose(ps[:, 1, cc * P:(cc + 1) * P],
                                         kv[:, c, 1 + tt * P:1 + (tt + 1) * P], ident[:, :])
                            tr = pe.transpose(ps[:, 1, 256 + cc * P:256 + (cc + 1) * P],
                                              kv[:, 4 + c, 1 + tt * P:1 + (tt + 1) * P], ident[:, :])
                        tr.then_inc(S("rw_tr"), 1)
                        for hh in range(4):
                            c, rows = 2 * rd + hh // 2, slice(64 * (hh % 2), 64 * (hh % 2) + 64)
                            b_, k_ = bt[rows, c, tok], kv[rows, c, 1 + tt * P:1 + (tt + 1) * P]
                            pe.matmul(ps[:, 2 + hh, 0:P], ar[rows, c, tt, 0, :], b_, start=True, stop=True)
                            pe.matmul(ps[:, 2 + hh, P:2 * P], b_, ar[rows, c, tt, 1, :], start=True, stop=True)
                            mm = pe.matmul(ps[:, 2 + hh, 2 * P:4 * P], k_,
                                           ar[rows, c, tt, :, :].rearrange("p a b -> p (a b)"),
                                           start=True, stop=True)
                            mm.then_inc(S("rw_mat"), 1)
                        gate_products(3)
                        pe.wait_ge(S("rw_tok"), 3 * r + 3)
                        pe.wait_ge(S("rw_m"), 4 * r + 4)
                        pe.wait_ge(S(f"rw_ti{tt % 2}"), 128 * (tt // 2 + 1))
                        for hh in range(4):
                            pe.matmul(ps[:, 6, hh * C:(hh + 1) * C], m[:, hh, 2, :], tkv[:, 1, hh, :],
                                      start=True, stop=True)
                            mm = pe.matmul(ps[:, 2, hh * P:(hh + 1) * P], m[:, hh, 0, :], ti[:, tt % 2, 4 * rd + hh, :],
                                           start=True, stop=True)
                        mm.then_inc(S("rw_kav"), 1)
                        gate_products(3)
                        pe.wait_ge(S("rw_kf"), 2 * r + 2)
                        for hh in range(4):
                            mm = pe.matmul(ps[:, 0, hh * P:(hh + 1) * P], ti[:, tt % 2, 4 * rd + hh, :], rhs[:, hh, :],
                                           start=True, stop=True)
                        mm.then_inc(S("rw_zmm"), 1)
                        gate_products(2)
                        for i in range(3):
                            pe.wait_ge(S("rw_x"), 4 * r + i + 1)
                            src = z if i == 0 else xb[:, (i - 1) % 2]
                            for hh in range(4):
                                mm = pe.matmul(ps[:, 1 + i, hh * P:(hh + 1) * P], ft[:, hh, :], src[:, hh, :],
                                               start=True, stop=True)
                            mm.then_inc(S("rw_xmm"), 1)
                            gate_products(2 if i == 2 else 3)
                        pe.wait_ge(S("rw_x"), 4 * r + 4)
                        xf = xb[:, 0]
                        for hh in range(4):
                            cc, o = hh // 2, 64 * (hh % 2)
                            out_ = slice(o, o + 64)
                            for half in range(2):
                                t_ = slice(64 * half, 64 * half + 64)
                                pe.matmul(ps[out_, 4 + half, cc * C:(cc + 1) * C], xf[t_, hh, 0:C], tb[t_, hh, :],
                                          start=True, stop=True)
                                h_ = ps[out_, 4 + half, 128 + cc * C:128 + (cc + 1) * C]
                                pe.matmul(h_, tb[t_, hh, :], xf[t_, hh, C:2 * C], start=True, stop=False)
                                pe.matmul(h_, tkv[t_, 0, hh, :], tkv[t_, 1, hh, :], start=False, stop=True)
                            pe.matmul(ps[out_, 6, cc * P:(cc + 1) * P], xf[:, hh, 0:C], m[:, hh, 1, :],
                                      start=True, stop=True)
                            y_ = ps[out_, 1, 256 + cc * P:256 + (cc + 1) * P]
                            pe.matmul(y_, xf[:, hh, C:2 * C], m[:, hh, 1, :], start=True, stop=False)
                            mm = pe.matmul(y_, tkv[:, 1, hh, :], m[:, hh, 3, :], start=False, stop=True)
                        mm.then_inc(S("rw_gmm"), 1)
                        gate_products(3)
                        pe.wait_ge(S("rw_gq"), 3 * r + 3)
                        pe.wait_ge(S("rw_zeroed"), 2)
                        for half in range(2):
                            n = 2 * tt + half
                            if half:
                                pe.wait_ge(S("rw_st"), 2 * r + 1)
                            for hh in range(4):
                                cc, o = hh // 2, 64 * (hh % 2)
                                o = slice(o, o + 64)
                                mm = pe.matmul(ps[o, 2 + half, cc * C:(cc + 1) * C], gb[o, half, cc, :],
                                               state[o, n % 3, 2 * rd + cc, :], start=True, stop=True)
                            mm.then_inc(S("rw_cmm"), 1)
                            gate_products(3 if half == 0 else 0)
                            for hh in range(4):
                                cc, o = hh // 2, 64 * (hh % 2)
                                o = slice(o, o + 64)
                                mm = pe.matmul(ps[o, 0, cc * P + half * C:cc * P + half * C + C],
                                               state[o, n % 3, 2 * rd + cc, :], qb[o, cc, half * C:(half + 1) * C],
                                               start=True, stop=True)
                        mm.then_inc(S("rw_ymm"), 1)
                        gate_products(2)

                @block.scalar
                def _(act):
                    def gate_out(n):
                        act.wait_ge(S("gate_mm"), n + 1)
                        if n >= 2:
                            act.wait_ge(S(f"gate_out{n % 2}"), 16 * (n // 2))
                        act.activation(go[:, n % 2, :], ps[:, 7, :], ACT.Silu if n < 16 else ACT.Sigmoid
                                       ).then_inc(S("gate_ev"), 1)

                    for r, (tt, rd) in enumerate(rounds):
                        act.wait_ge(S("rw_tr"), r + 1)
                        act.activation(rhs[:, :, 0:C], ps[:, 0, 0:256].rearrange("p (h c) -> p h c", c=C),
                                       ACT.Copy).then_inc(S("rw_tok"), 1)
                        act.activation(tb[:, :, :].rearrange("p h c -> p (h c)"), ps[:, 0, 256:512],
                                       ACT.Copy).then_inc(S("rw_tok"), 1)
                        act.activation(tkv[:, :, :, :].rearrange("p a h c -> p (a h c)"), ps[:, 1, :],
                                       ACT.Copy).then_inc(S("rw_tok"), 1)
                        act.wait_ge(S("rw_kav"), r + 1)
                        act.activation(rhs[:, :, C:2 * C], ps[:, 6, 0:256].rearrange("p (h c) -> p h c", c=C),
                                       ACT.Copy).then_inc(S("rw_kf"), 1)
                        act.activation(ft[:, :, :].rearrange("p h t -> p (h t)"), ps[:, 2, :],
                                       ACT.Copy).then_inc(S("rw_kf"), 1)
                        gate_out(3 * r)
                        gate_out(3 * r + 1)
                        act.wait_ge(S("rw_gmm"), r + 1)
                        act.activation(yi[:, :, :].rearrange("p a t -> p (a t)"), ps[:, 1, 256:512],
                                       ACT.Copy).then_inc(S("rw_yi"), 1)
                        gate_out(3 * r + 2)

                @block.vector
                def _(dve):
                    link = Link(dve, "dve_link")
                    dve.memset(ti[:, :, :, :], 0.0).then_inc(S("rw_zeroed"), 1)
                    dve.memset(state[:, 0, :, :], 0.0).then_inc(S("rw_zeroed"), 1)
                    for r, (tt, rd) in enumerate(rounds):
                        for hh in range(4):
                            dve.wait_ge(S("rw_mat"), 4 * r + hh + 1)
                            dve.tensor_tensor(m[:, hh, :, :].rearrange("p a t -> p (a t)"), ps[:, 2 + hh, :],
                                              masks[:, :, :].rearrange("p a t -> p (a t)"),
                                              ALU.mult).then_inc(S("rw_m"), 1)
                        dve.wait_ge(S("rw_zmm"), r + 1)
                        flat = lambda ap: ap.rearrange("p h t -> p (h t)")
                        dve.tensor_copy(flat(z[:, :, :]), ps[:, 0, :]).then_inc(S("rw_x"), 1)
                        dve.wait_ge(S("rw_x"), 4 * r + 1)
                        for i in range(3):
                            dve.wait_ge(S("rw_xmm"), 3 * r + i + 1)
                            dve.tensor_tensor(flat(xb[:, i % 2]), ps[:, 1 + i, :], flat(z[:, :, :]),
                                              ALU.add).then_inc(S("rw_x"), 1)
                        dve.wait_ge(S("rw_gmm"), r + 1)
                        dve.tensor_tensor(gb[:, :, :, :], ps[:, 4:6, 0:P].rearrange("p a (c k) -> p a c k", k=C),
                                          eye64[:, :].unsqueeze(1).unsqueeze(1).to_broadcast([P, 2, 2, C]),
                                          ALU.add).then_inc(S("rw_gq"), 1)
                        dve.tensor_copy(hb[:, :, :, :].rearrange("p a c k -> p a (c k)"),
                                        ps[:, 4:6, P:2 * P]).then_inc(S("rw_gq"), 1)
                        dve.tensor_tensor(qb[:, :, :], ps[:, 6, 0:256].rearrange("p (c t) -> p c t", t=P),
                                          ar[:, 2 * rd:2 * rd + 2, tt, 1, :], ALU.add).then_inc(S("rw_gq"), 1)
                        dve.wait_ge(S("rw_gq"), 3 * r + 3)
                        for half in range(2):
                            n = 2 * tt + half
                            dve.wait_ge(S("rw_cmm"), 2 * r + half + 1)
                            link(dve.tensor_tensor(s1[:, :, :], ps[:, 2 + half, 0:P].rearrange("p (c k) -> p c k", k=C),
                                                   hb[:, half, :, :], ALU.add))
                            dve.tensor_tensor(state[:, (n + 1) % 3, 2 * rd:2 * rd + 2, :], s1[:, :, :],
                                              pc[:, 2 * rd:2 * rd + 2, n:n + 1].to_broadcast([P, 2, C]),
                                              ALU.mult).then_inc(S("rw_st"), 1)
                        dve.wait_ge(S("rw_ymm"), r + 1)
                        dve.wait_ge(S("rw_yi"), r + 1)
                        dve.tensor_tensor(ozr[:, 2 * rd:2 * rd + 2, tt * P:(tt + 1) * P],
                                          ps[:, 0, 0:256].rearrange("p (c t) -> p c t", t=P), yi[:, :, :],
                                          ALU.add).then_inc(S("rw_y"), 1)
            dump("y", ozr[:, :, :])

            with ExitStack() as st:
                sq = sb(st, "gn_sq", [P, 4, T])
                rs = sb(st, "gn_rs", [P, 4, T])
                block = st.enter_context(nc.Block())
                two = lambda b: ps[:, b:b + 2, :].rearrange("p a b -> p (a b)")

                @block.tensor
                def _(pe):
                    for i, src in enumerate((ozr, sq)):
                        if i:
                            pe.wait_ge(S("gn_sq"), 4)
                        for c in range(4):
                            for hf in range(2):
                                mm = pe.matmul(ps[:, 2 * c + hf, :], hones[:, :], src[:, c, hf * 512:(hf + 1) * 512],
                                               start=True, stop=True)
                            mm.then_inc(S("gn_sum"), 1)

                @block.scalar
                def _(act):
                    for c in range(4):
                        act.wait_ge(S("gn_c"), c + 1)
                        act.activation(sq[:, c, :], ozr[:, c, :], ACT.Square).then_inc(S("gn_sq"), 1)
                    act.wait_ge(S("gn_v"), 4)
                    act.activation(rs[:, :, :], rs[:, :, :], ACT.Sqrt).then_inc(S("gn_root"), 1)

                @block.vector
                def _(dve):
                    link = Link(dve, "dve_link")
                    for c in range(4):
                        dve.wait_ge(S("gn_sum"), c + 1)
                        dve.scalar_tensor_tensor(ozr[:, c, :], two(2 * c), -1.0 / HD, ozr[:, c, :],
                                                 ALU.mult, ALU.add).then_inc(S("gn_c"), 1)
                    for c in range(4):
                        dve.wait_ge(S("gn_sum"), 5 + c)
                        dve.tensor_scalar(rs[:, c, :], two(2 * c), 1.0 / HD, GN_EPS, ALU.mult, ALU.add
                                          ).then_inc(S("gn_v"), 1)
                    dve.wait_ge(S("gn_root"), 1)
                    link(dve.reciprocal(rs[:, :, :], rs[:, :, :]))
                    for c in range(4):
                        link(dve.tensor_tensor(ozr[:, c, :], ozr[:, c, :], rs[:, c, :], ALU.mult))
                        link(dve.tensor_scalar(ozr[:, c, :], ozr[:, c, :], vecs[:, 5, c:c + 1], vecs[:, 6, c:c + 1],
                                               ALU.mult, ALU.add))
                        link(dve.tensor_tensor(ozr[:, c, :], ozr[:, c, :], bonus[:, c, :], ALU.add))
            dump("ozr", ozr[:, :, :])
            with nc.Block() as block:
                @block.sync
                def _(sp):
                    sp.dma_start(orw_d, ozr[:, :, :]).then_inc(S("rw_o_out"), 16)
                    sp.wait_ge(S("rw_o_out"), 16)
            keep.close()

        def bias_lines():
            with ExitStack() as st:
                tab = sb(st, "rel_tab", [33, 24])
                hot = sb(st, "hot", [33, 3, 384])
                line = sb(st, "line", [HEADS, 3, 384])
                load([(tab[0:32, :], A["rel_bias"]), (hot[:, :, :], A["c_hot"])])
                block = st.enter_context(nc.Block())

                @block.vector
                def _(dve):
                    dve.memset(tab[32:33, :], MASKED).then_inc(S("at_tab"), 1)
                    dve.wait_ge(S("at_line_mm"), 3)
                    dve.tensor_copy(line[:, :, :], ps[0:HEADS, 0:3, 0:384]).then_inc(S("at_line"), 1)

                @block.tensor
                def _(pe):
                    pe.wait_ge(S("at_tab"), 1)
                    for g in range(3):
                        pe.matmul(ps[0:HEADS, g, 0:384], tab[:, g * HEADS:(g + 1) * HEADS], hot[:, g, :],
                                  start=True, stop=True).then_inc(S("at_line_mm"), 1)

                @block.sync
                def _(sp):
                    sp.wait_ge(S("at_line"), 1)
                    sp.dma_start(line_d.rearrange("g h y -> h g y"), line[:, :, :]).then_inc(S("at_line_out"), 16)
                    sp.wait_ge(S("at_line_out"), 16)
                    for g in range(3):
                        sp.dma_start(lines_d[g], bass.AP(tensor=line_d.tensor, offset=g * HEADS * 384,
                                                         ap=[[384, HEADS], [0, P], [1, 384]])
                                     ).then_inc(S("at_lines"), 16)

        def attention(keep):
            ag_d = dram("attn_groups", [3, T, 528])
            REC = 528
            hs = ExitStack()
            hp = pair(hs, "h2", [P, KD, T])
            qz = sb(hs, "qz", [P, 2, 4, T])
            kk = sb(hs, "kk", [P, 4, T])
            v = sb(hs, "v", [P, NT, AW])
            cv = sb(hs, "cv", [P, KD, 2])
            bm = sb(hs, "bm", [P, 6, KD])
            mw = sb(hs, "mod_w", [P, 2, KD, 256])
            MODS = 6 * D // 256

            def mod_weights(eng, s_):
                if s_ >= 2:
                    eng.wait_ge(S("mod_mm"), s_ - 1)
                eng.dma_start(mw[:, s_ % 2], wcols(A["w_mod_2"][0], 256 * s_, 256 * s_ + 256)
                              ).then_inc(S(f"mod_w{s_ % 2}"), 16)

            def mod_products(pe, s_):
                if s_ == 0:
                    pe.wait_ge(S("mod_c"), 1)
                pe.wait_ge(S(f"mod_w{s_ % 2}"), 16 * (s_ // 2 + 1))
                if s_:
                    pe.wait_ge(S("mod_ev"), s_)
                for c in range(2):
                    for k in range(KD):
                        mm = pe.matmul(ps[:, 7, 2 * c:2 * c + 2], mw[:, s_ % 2, k, c * P:(c + 1) * P], cv[:, k, :],
                                       start=(k == 0), stop=(k == KD - 1))
                mm.then_inc(S("mod_mm"), 1)

            def mod_out(dve, s_):
                part, c = divmod(2 * s_, KD)
                dve.wait_ge(S("mod_mm"), s_ + 1)
                dve.tensor_tensor(modv[:, part, c:c + 2, :], ps[:, 7, 0:4].rearrange("p (c v) -> p c v", v=2),
                                  bm[:, part, c:c + 2].unsqueeze(2).to_broadcast([P, 2, 2]), ALU.add
                                  ).then_inc(S("mod_ev"), 1)

            load([(cv[:, :, 0], vec(A["c_2"][0])), (cv[:, :, 1], vec(A["c_ctx_2"][0])),
                  (bm[:, :, :], A["b_mod_2"][0].rearrange("(s k p) -> p s k", p=P, s=6)),
                  (gains[:, 7, :], vec(A["norm1_g_2"][0])), (gains[:, 8, :], vec(A["norm2_g_2"][0]))])
            with ExitStack() as st:
                raw = sb(st, "h_raw", [P, 4, T])
                block = st.enter_context(nc.Block())

                @block.sync
                def _(sp):
                    for k in range(KD):
                        if k >= 4:
                            sp.wait_ge(S("h_hi"), k - 3)
                            sp.wait_ge(S("h_lo"), k - 3)
                        sp.dma_start(raw[:, k % 4, :], h_d[:, k, :]).then_inc(S(f"h_in{k % 4}"), 16)

                @block.scalar
                def _(act):
                    act.activation(cv[:, :, :], cv[:, :, :], ACT.Silu).then_inc(S("mod_c"), 1)
                    for k in range(KD):
                        act.wait_ge(S(f"h_in{k % 4}"), 16 * (k // 4 + 1))
                        high(act, hp[0][:, k, :], raw[:, k % 4, :]).then_inc(S("h_hi"), 1)

                @block.vector
                def _(dve):
                    for k in range(KD):
                        dve.wait_ge(S("h_hi"), k + 1)
                        low(dve, hp[1][:, k, :], raw[:, k % 4, :], hp[0][:, k, :]).then_inc(S("h_lo"), 1)

                @block.gpsimd
                def _(gp):
                    mod_weights(gp, 0)
                    mod_weights(gp, 1)
                    gp.memset(qz[64:P, 0, :, :], 0.0)
                    gp.memset(qz[0:64, 1, :, :], 0.0)

            for g, dil in enumerate(DILATIONS):
                step = stride_of(dil)
                length = T // step
                off = [(which * 3 + g) * AW for which in range(3)]

                def spread(src, step=step):
                    return src.rearrange("p (i r) -> p i r", r=step)

                def places(dst, x, step=step):
                    w = 512 // step
                    return dst.rearrange("p (r i) -> p i r", r=step)[:, x * w:(x + 1) * w, :]

                def put_q(kind, eng, src, m, x):
                    copy(kind, eng, places(qz[0:64, 0, m, :], x), spread(src[0:64, :]))
                    return copy(kind, eng, places(qz[64:P, 1, m, :], x), spread(src[64:P, :]))

                def put_k(kind, eng, src, m, x):
                    return copy(kind, eng, places(kk[:, m, :], x), spread(src))

                def v_tokens(k, m, length=length, step=step):
                    r, i0 = divmod(m * P, length)
                    return tuple(h[:, k, :].rearrange("p (i r) -> p r i", r=step)[:, r, i0:i0 + P] for h in hp)

                def mods(gp, g=g):
                    for s_ in range(8 * g + 2, min(8 * g + 10, MODS)):
                        mod_weights(gp, s_)
                gemm([dict(w=wcols(w_in, off[0], off[0] + AW), mode="T", act=whole(hp), tiles=2, evac=put_q),
                      dict(w=wcols(w_in, off[1], off[1] + AW), mode="T", act=whole(hp), tiles=2, evac=put_k),
                      dict(w=wcols(w_in, off[2], off[2] + AW), mode="N", act=v_tokens, tiles=NT,
                           evac=lambda kind, eng, src, m, x: copy(kind, eng, v[:, m, :], src))],
                     ring=5, banks=7, pool=mods,
                     side={"at": {3 * i + 2: 8 * g + i for i in range(8)}, "pe": mod_products, "dve": mod_out})
                with ExitStack() as gst:
                    bias = sb(gst, f"bias{g}", [P, 2, 4, 2 * P])
                    sbuf = sb(gst, f"sc{g}", [P, 2, 2, 4, 2 * P])
                    pt = sb(gst, f"pt{g}", [P, 2, 2, 2, 4, P])
                    og = sb(gst, f"og{g}", [P, 3, REC])
                    nkey = [2 if (j * P) % length and length > P else 1 for j in range(NT)]
                    ngrp = [2 * n for n in nkey]
                    gsum = [sum(ngrp[:j]) for j in range(NT + 1)]
                    block = gst.enter_context(nc.Block())
                    counts = {"sc": NT, "sb": NT, "exp": NT, "tr": gsum[NT], "pt0": gsum[NT] // 2, "pt1": gsum[NT] // 2,
                              "pv": NT, "og": NT, "nm": NT, "bias": 32}
                    counts.update({f"out{x}": 16 * len(range(x, NT, 3)) for x in range(3)})
                    sn = {n: S(f"at_{n}") for n in counts}
                    bs = {n: base(f"at_{n}", c) for n, c in counts.items()}
                    gv = ag_d[g].rearrange("(i r) c -> r i c", r=step)

                    @block.tensor
                    def _(pe):
                        def scores(j):
                            if j:
                                pe.wait_ge(sn["sb"], bs["sb"] + j)
                            k0 = (j + 1 - nkey[j]) * P
                            for h in range(HEADS):
                                w = nkey[j] * P
                                bank, o = 2 * (h % 2) + (h // 2) // 2, ((h // 2) % 2) * 256 + 256 - w
                                mm = pe.matmul(ps[:, bank, o:o + w], qz[:, h % 2, h // 2, j * P:(j + 1) * P],
                                               kk[:, h // 2, k0:k0 + w], start=True, stop=True)
                            mm.then_inc(sn["sc"], 1)

                        def output(j):
                            for x in range(2):
                                pe.wait_ge(sn[f"pt{x}"], bs[f"pt{x}"] + gsum[j + 1] // 2)
                            if j:
                                pe.wait_ge(sn["og"], bs["og"] + j)
                            for h in range(HEADS):
                                for kb in range(nkey[j]):
                                    mm = pe.matmul(ps[:, 7, h * HD:(h + 1) * HD], pt[:, j % 2, kb, h % 2, h // 2, :],
                                                   v[:, j + 1 - nkey[j] + kb, h * HD:(h + 1) * HD],
                                                   start=(kb == 0), stop=(kb == nkey[j] - 1))
                            mm.then_inc(sn["pv"], 1)

                        scores(0)
                        for j in range(NT):
                            if j + 1 < NT:
                                scores(j + 1)
                            if j:
                                output(j - 1)
                            pe.wait_ge(sn["exp"], bs["exp"] + j + 1)
                            for n in range(ngrp[j]):
                                kb, par = n // 2, n % 2
                                w = gsum[j] + n
                                if w >= 3:
                                    pe.wait_ge(sn[f"pt{(w - 3) % 2}"], bs[f"pt{(w - 3) % 2}"] + (w - 3) // 2 + 1)
                                o = (2 - nkey[j] + kb) * P
                                for hh in range(4):
                                    tr = pe.transpose(ps[:, 4 + w % 3, hh * P:(hh + 1) * P],
                                                      sbuf[:, j % 2, par, hh, o:o + P], ident[:, :])
                                tr.then_inc(sn["tr"], 1)
                        output(NT - 1)

                    @block.vector
                    def _(dve):
                        link = Link(dve, "dve_link")

                        def soft(j):
                            w = 2 * P - nkey[j] * P
                            if j == 0:
                                dve.wait_ge(sn["bias"], bs["bias"] + 32)
                            dve.wait_ge(sn["sc"], bs["sc"] + j + 1)
                            if j >= 2:
                                dve.wait_ge(sn["tr"], bs["tr"] + gsum[j - 1])
                            for par in range(2):
                                ins = dve.scalar_tensor_tensor(
                                    sbuf[:, j % 2, par, :, w:], ps[:, 2 * par:2 * par + 2, :].rearrange(
                                        "p a (b k) -> p (a b) k", b=2)[:, :, w:], 0.125,
                                    bias[:, par, :, w:], ALU.mult, ALU.add)
                                if par == 0:
                                    link(ins)
                                else:
                                    ins.then_inc(sn["sb"], 1)
                            dve.wait_ge(sn["sb"], bs["sb"] + j + 1)
                            if j >= 3:
                                dve.wait_ge(sn[f"out{j % 3}"], bs[f"out{j % 3}"] + 16 * (j // 3))
                            dve.tensor_reduce(og[:, j % 3, 520:528].rearrange("p (hh two) -> p two hh", two=2),
                                              sbuf[:, j % 2, :, :, w:], X, ALU.max, negate=True
                                              ).then_inc(sn["nm"], 1)

                        soft(0)
                        for j in range(NT):
                            if j + 1 < NT:
                                soft(j + 1)
                            for n in range(1, ngrp[j], 2):
                                w = gsum[j] + n
                                dve.wait_ge(sn["tr"], bs["tr"] + w + 1)
                                if j >= 2:
                                    dve.wait_ge(sn["pv"], bs["pv"] + j - 1)
                                dve.tensor_copy(pt[:, j % 2, n // 2, n % 2, :, :].rearrange("p a b -> p (a b)"),
                                                ps[:, 4 + w % 3, :]).then_inc(sn["pt1"], 1)

                    @block.scalar
                    def _(act):
                        def numerators(j):
                            act.wait_ge(sn["pv"], bs["pv"] + j + 1)
                            act.activation(og[:, j % 3, 0:512], ps[:, 7, :], ACT.Copy).then_inc(sn["og"], 1)

                        for j in range(NT):
                            w0 = 2 * P - nkey[j] * P
                            act.wait_ge(sn["nm"], bs["nm"] + j + 1)
                            for h in range(HEADS):
                                part = sbuf[:, j % 2, h % 2, h // 2, w0:]
                                e = act.activation(part, part, ACT.Exp, bias=og[:, j % 3, 520 + h:521 + h],
                                                   accum_out=og[:, j % 3, 512 + h:513 + h])
                            e.then_inc(sn["exp"], 1)
                            if j:
                                numerators(j - 1)
                            for n in range(0, ngrp[j], 2):
                                w = gsum[j] + n
                                act.wait_ge(sn["tr"], bs["tr"] + w + 1)
                                if j >= 2:
                                    act.wait_ge(sn["pv"], bs["pv"] + j - 1)
                                act.activation(pt[:, j % 2, n // 2, n % 2, :, :].rearrange("p a b -> p (a b)"),
                                               ps[:, 4 + w % 3, :], ACT.Copy).then_inc(sn["pt0"], 1)
                        numerators(NT - 1)

                    @block.sync
                    def _(sp):
                        sp.wait_ge(S("at_lines"), 48)
                        for par in range(2):
                            sp.dma_start(bias[:, par, :, :],
                                         bass.AP(tensor=lines_d.tensor, offset=(g * HEADS + par) * P * 384 + 127,
                                                 ap=[[383, P], [2 * P * 384, 4], [1, 2 * P]])).then_inc(sn["bias"], 16)
                        for j in range(NT):
                            sp.wait_ge(sn["og"], bs["og"] + j + 1)
                            r, i0 = divmod(j * P, length)
                            sp.dma_start(gv[r, i0:i0 + P, :], og[:, j % 3, :]).then_inc(sn[f"out{j % 3}"], 16)
                        for x in range(3):
                            sp.wait_ge(sn[f"out{x}"], bs[f"out{x}"] + 16 * len(range(x, NT, 3)))
            hs.close()

            merged = pair(keep, "merged", [P, KD, T])
            o_stack = ExitStack()
            oa = pair(o_stack, "oa", [P, 4, T])
            orw = pair(o_stack, "orw", [P, 4, T])
            with ExitStack() as st:
                dm = sb(st, "cdm", [P, NT, 3, 16])
                ga = sb(st, "cg", [P, 3, 3, 512])
                mn = sb(st, "cmn", [P, NT, HEADS])
                wg = sb(st, "cwg", [P, NT, 3, HEADS])
                wd = sb(st, "cwd", [P, NT, 3, HEADS])
                zg = sb(st, "czg", [P, 3, 8, P])
                ob = sb(st, "cob", [P, 3, 4, P])
                og = sb(st, "cog", [P, 2, 2, 4, P])
                block = st.enter_context(nc.Block())

                @block.sync
                def _(sp):
                    for g in range(3):
                        sp.dma_start(dm[:, :, g, :], ag_d[g].rearrange("(t p) c -> p t c", p=P)[:, :, 512:528]
                                     ).then_inc(S("cm_dm"), 16)
                    for tt in range(NT):
                        tok = slice(tt * P, (tt + 1) * P)
                        if tt >= 3:
                            sp.wait_ge(S("cm_ev"), 2 * (tt - 2))
                        sp.dma_start(ga[:, tt % 3, :, :], ag_d[:, tok, 0:512].rearrange("g p c -> p g c")
                                     ).then_inc(S(f"cm_in{tt % 3}"), 16)
                        sp.dma_start(zg[:, tt % 3, :, :], gates_d[:, 0:8, tok]).then_inc(S(f"cm_in{tt % 3}"), 16)
                        sp.dma_start(ob[:, tt % 3, :, :], orw_d[:, :, tok]).then_inc(S(f"cm_in{tt % 3}"), 16)

                @block.scalar
                def _(act):
                    act.wait_ge(S("cm_dif"), 3)
                    act.activation(wg[:, :, :, :], wg[:, :, :, :], ACT.Exp).then_inc(S("cm_w"), 1)
                    for tt in range(NT):
                        tok = slice(tt * P, (tt + 1) * P)
                        for n, o in enumerate((oa, orw)):
                            act.wait_ge(S("cm_ev"), 2 * tt + n + 1)
                            high(act, o[0][:, :, tok], og[:, tt % 2, n, :, :]).then_inc(S("cm_hi"), 1)

                @block.vector
                def _(dve):
                    link = Link(dve, "dve_link")
                    nm = lambda g: dm[:, :, g, 8:16]
                    dve.wait_ge(S("cm_dm"), 48)
                    link(dve.tensor_tensor(mn[:, :, :], nm(0), nm(1), ALU.min))
                    link(dve.tensor_tensor(mn[:, :, :], mn[:, :, :], nm(2), ALU.min))
                    for g in range(3):
                        dve.tensor_tensor(wg[:, :, g, :], mn[:, :, :], nm(g), ALU.subtract).then_inc(S("cm_dif"), 1)
                    dve.wait_ge(S("cm_w"), 1)
                    link(dve.tensor_tensor(wd[:, :, :, :], wg[:, :, :, :], dm[:, :, :, 0:8], ALU.mult))
                    link(dve.tensor_tensor(mn[:, :, :], wd[:, :, 0, :], wd[:, :, 1, :], ALU.add))
                    link(dve.tensor_tensor(mn[:, :, :], mn[:, :, :], wd[:, :, 2, :], ALU.add))
                    link(dve.reciprocal(mn[:, :, :], mn[:, :, :]))
                    link(dve.tensor_tensor(wg[:, :, :, :], wg[:, :, :, :],
                                           mn[:, :, :].unsqueeze(2).to_broadcast([P, NT, 3, HEADS]), ALU.mult))

                    def lows(tt):
                        tok = slice(tt * P, (tt + 1) * P)
                        for n, o in enumerate((oa, orw)):
                            dve.wait_ge(S("cm_hi"), 2 * tt + n + 1)
                            low(dve, o[1][:, :, tok], og[:, tt % 2, n, :, :], o[0][:, :, tok]).then_inc(S("cm_lo"), 1)

                    def gated(tt):
                        dve.wait_ge(S("cm_tr"), tt + 1)
                        if tt >= 2:
                            dve.wait_ge(S("cm_lo"), 2 * (tt - 1))
                        dve.tensor_tensor(og[:, tt % 2, 0, :, :], ps[:, tt % 8, :].rearrange("p (c t) -> p c t", t=P),
                                          zg[:, tt % 3, 4:8, :], ALU.mult).then_inc(S("cm_ev"), 1)
                        dve.tensor_tensor(og[:, tt % 2, 1, :, :], ob[:, tt % 3, :, :],
                                          zg[:, tt % 3, 0:4, :], ALU.mult).then_inc(S("cm_ev"), 1)
                    for tt in range(NT):
                        dve.wait_ge(S(f"cm_in{tt % 3}"), 48 * (tt // 3 + 1))
                        num = ga[:, tt % 3, :, :].rearrange("p g (h c) -> p g h c", c=HD)
                        link(dve.tensor_tensor(num, num, wg[:, tt, :, :].unsqueeze(3).to_broadcast([P, 3, HEADS, HD]),
                                               ALU.mult))
                        o = ga[:, tt % 3, 0, :]
                        link(dve.tensor_tensor(o, o, ga[:, tt % 3, 1, :], ALU.add))
                        dve.tensor_tensor(o, o, ga[:, tt % 3, 2, :], ALU.add).then_inc(S("cm_o"), 1)
                        if tt:
                            gated(tt - 1)
                        if tt >= 2:
                            lows(tt - 2)
                    gated(NT - 1)
                    lows(NT - 2)
                    lows(NT - 1)

                @block.tensor
                def _(pe):
                    for tt in range(NT):
                        pe.wait_ge(S("cm_o"), tt + 1)
                        for c in range(4):
                            tr = pe.transpose(ps[:, tt % 8, c * P:(c + 1) * P], ga[:, tt % 3, 0, c * P:(c + 1) * P],
                                              ident[:, :])
                        tr.then_inc(S("cm_tr"), 1)
            return merged, oa, orw, o_stack

        def merge(merged, gates, wa, wb, oa, ob, tag):
            with ExitStack() as st:
                gt = sb(st, "mg_gates" + tag, [P, 2, 2, T])
                ta = sb(st, "mg_a" + tag, [P, 4, 512])
                tm = sb(st, "mg_m" + tag, [P, 2, 512])
                b = {n: base("mg_" + n, c) for n, c in (("g0", 128), ("g1", 128), ("hi", 2 * KD), ("lo", 2 * KD), ("used", KD))}

                def gate_loads(gp):
                    for m in range(KD):
                        if m >= 2:
                            gp.wait_ge(S("mg_used"), b["used"] + m - 1)
                        for i in range(2):
                            gp.dma_start(gt[:, m % 2, i, :], gates[:, KD * i + m, :]).then_inc(S(f"mg_g{m % 2}"), 16)

                link = [None]

                def lows(dve, m, x):
                    dve.wait_ge(S("mg_hi"), b["hi"] + 2 * m + x + 1)
                    cut_ = (slice(None), m, slice(x * 512, (x + 1) * 512))
                    low(dve, merged[1][cut_], tm[:, x, :], merged[0][cut_]).then_inc(S("mg_lo"), 1)

                def jobs(m):
                    def up_a(kind, dve, src, _m, x):
                        if x == 0:
                            dve.wait_ge(S(f"mg_g{m % 2}"), b[f"g{m % 2}"] + 32 * (m // 2 + 1))
                        return dve.tensor_tensor(ta[:, 2 * (m % 2) + x, :], src, gt[:, m % 2, 0, x * 512:(x + 1) * 512], ALU.mult)

                    def lows_before(dve, _m, x):
                        if m:
                            lows(dve, m - 1, x)

                    def up_b(kind, dve, src, _m, x):
                        if link[0] is None:
                            link[0] = Link(dve, "dve_link")
                        if m:
                            dve.wait_ge(S("mg_lo"), b["lo"] + 2 * (m - 1) + x + 1)
                        link[0](dve.tensor_tensor(tm[:, x, :], src, gt[:, m % 2, 1, x * 512:(x + 1) * 512], ALU.mult))
                        return dve.tensor_tensor(tm[:, x, :], tm[:, x, :], ta[:, 2 * (m % 2) + x, :], ALU.add)

                    def highs(act, _m, x, summed):
                        act.wait_ge(*summed)
                        high(act, merged[0][:, m, x * 512:(x + 1) * 512], tm[:, x, :]).then_inc(S("mg_hi"), 1)

                    def after_b(dve, _m, x):
                        if x:
                            dve.engine_nop().then_inc(S("mg_used"), 1)
                            if m == KD - 1:
                                lows(dve, m, 0)
                                lows(dve, m, 1)
                    cols = slice(m * P, (m + 1) * P)
                    return [dict(w=wcols(wa, 0, D)[:, :, cols], mode="T", act=whole(oa), tiles=2, on="dve", evac=up_a,
                                 dve_step=lows_before),
                            dict(w=wcols(wb, 0, D)[:, :, cols], mode="T", act=whole(ob), tiles=2, on="dve", evac=up_b,
                                 act_step=highs, dve_step=after_b)]
                gemm([j for m in range(KD) for j in jobs(m)], ring=3, pool=gate_loads)

        def row(ap):
            return bass.AP(tensor=ap.tensor, offset=ap.offset, ap=[[0, P], [1, D]])

        def merge_first():
            keep = ExitStack()
            merged, oa, orw, o_stack = attention(keep)
            merge(merged, gates_d[:, 8:24, :], A["w_up_attn"][0], A["w_up_rwkv"][0], oa, orw, "1")
            o_stack.close()
            retire("rw_", "gate_", "gn_", "at_", "cm_", "h_")
            with ExitStack() as st:
                rows = sb(st, "rows1", [P, NT, D])
                xr = sb(st, "x_res", [P, NT, D])
                pg = sb(st, "post_gain", [P, D])

                def residual(gp):
                    gp.dma_start(xr[:, :, :], x_rows.rearrange("(t p) d -> p t d", p=P)).then_inc(S("pn_in"), 16)
                    gp.dma_start(pg[:, :], row(A["post_norm_gain"][0])).then_inc(S("pn_in"), 16)
                gemm([dict(w=wcols(A["w_out"][0], 512 * i, 512 * i + 512), mode="N", act=token_tiles(merged), tiles=NT,
                           evac=lambda kind, eng, src, m, x, i=i: copy(kind, eng, rows[:, m, i * 512:(i + 1) * 512], src))
                      for i in range(2)], pool=residual)
                sq = sb(st, "pn_sq", [P, D])
                ss = sb(st, "pn_ss", [P, NT])
                block = st.enter_context(nc.Block())

                @block.scalar
                def _(act):
                    for t in range(NT):
                        if t:
                            act.wait_ge(S("pn_ss"), t)
                        act.activation(sq[:, :], rows[:, t, :], ACT.Square, accum_out=ss[:, t:t + 1]).then_inc(S("pn_ss"), 1)
                    act.wait_ge(S("pn_mean"), 1)
                    act.activation(ss[:, :], ss[:, :], ACT.Sqrt).then_inc(S("pn_root"), 1)

                @block.vector
                def _(dve):
                    link = Link(dve, "dve_link")
                    dve.wait_ge(S("pn_ss"), NT)
                    dve.tensor_scalar(ss[:, :], ss[:, :], 1.0 / D, EPS, ALU.mult, ALU.add).then_inc(S("pn_mean"), 1)
                    dve.wait_ge(S("pn_root"), 1)
                    link(dve.reciprocal(ss[:, :], ss[:, :]))
                    dve.wait_ge(S("pn_in"), 32)
                    for t in range(NT):
                        link(dve.scalar_tensor_tensor(rows[:, t, :], rows[:, t, :], ss[:, t:t + 1], pg[:, :],
                                                      ALU.mult, ALU.mult))
                        dve.tensor_tensor(xr[:, t, :], xr[:, t, :], rows[:, t, :], ALU.add).then_inc(S("pn_x"), 1)

                @block.sync
                def _(sp):
                    for t in range(NT):
                        sp.wait_ge(S("pn_x"), t + 1)
                        sp.dma_start(x1_d[t * P:(t + 1) * P, :], xr[:, t, :]).then_inc(S("pn_out"), 16)
                    sp.wait_ge(S("pn_out"), 16 * NT)
            keep.close()

        def chan_norm(buf, to, kt, slices, gain, width, tag):
            n_tok = buf.shape[2]
            with ExitStack() as st:
                sq = sb(st, f"cn_sq{tag}", [P, kt, n_tok])
                rs = sb(st, f"cn_rs{tag}", [P, n_tok])
                b = {n: base(f"cn_{n}", c) for n, c in (("sq", 1), ("mm", 1), ("mean", len(slices)), ("root", 1),
                                                       ("x", kt), ("hi", kt))}
                block = st.enter_context(nc.Block())

                @block.scalar
                def _(act):
                    act.activation(sq[:, :, :], buf[:, :, :], ACT.Square).then_inc(S("cn_sq"), 1)
                    act.wait_ge(S("cn_mean"), b["mean"] + len(slices))
                    act.activation(rs[:, :], rs[:, :], ACT.Sqrt).then_inc(S("cn_root"), 1)
                    for k in range(kt):
                        act.wait_ge(S("cn_x"), b["x"] + k + 1)
                        high(act, to[0][:, k, :], buf[:, k, :]).then_inc(S("cn_hi"), 1)

                @block.tensor
                def _(pe):
                    pe.wait_ge(S("cn_sq"), b["sq"] + 1)
                    for n, (o, w) in enumerate(slices):
                        for k in range(kt):
                            mm = pe.matmul(ps[:, n, 0:w], ones[:, :], sq[:, k, o:o + w], start=(k == 0), stop=(k == kt - 1))
                    mm.then_inc(S("cn_mm"), 1)

                @block.vector
                def _(dve):
                    link = Link(dve, "dve_link")
                    dve.wait_ge(S("cn_mm"), b["mm"] + 1)
                    for n, (o, w) in enumerate(slices):
                        dve.tensor_scalar(rs[:, o:o + w], ps[:, n, 0:w], 1.0 / width, EPS, ALU.mult, ALU.add
                                          ).then_inc(S("cn_mean"), 1)
                    dve.wait_ge(S("cn_root"), b["root"] + 1)
                    link(dve.reciprocal(rs[:, :], rs[:, :]))
                    for k in range(kt):
                        dve.scalar_tensor_tensor(buf[:, k, :], buf[:, k, :], gain[:, k:k + 1], rs[:, :], ALU.mult, ALU.mult
                                                 ).then_inc(S("cn_x"), 1)
                    for k in range(kt):
                        dve.wait_ge(S("cn_hi"), b["hi"] + k + 1)
                        low(dve, to[1][:, k, :], buf[:, k, :], to[0][:, k, :])

        def head_norm_rope(buf, nt, gain_row, rope_tiles, tag):
            with ExitStack() as st:
                ss = sb(st, f"hn_ss{tag}", [P, nt, HEADS])
                sq = sb(st, f"hn_sq{tag}", [P, 2, HEADS, QKD])
                t1 = sb(st, f"hn_t1{tag}", [P, HEADS, ROPE])
                t2 = sb(st, f"hn_t2{tag}", [P, HEADS, ROPE])
                rope = sb(st, f"hn_rope{tag}", [P, NT, 2, ROPE])
                load([(rope[:, :, :, :].rearrange("p t a c -> p t (a c)"),
                       A["c_rope"].rearrange("(t p) a c -> p t (a c)", p=P))])
                b = {n: base(f"hn_{n}", c) for n, c in (("sq", nt), ("ss", nt), ("root", 1), ("mean", 1))}
                block = st.enter_context(nc.Block())

                @block.scalar
                def _(act):
                    for t in range(nt):
                        if t >= 2:
                            act.wait_ge(S("hn_ss"), b["ss"] + t - 1)
                        act.activation(sq[:, t % 2, :, :], buf[:, t, :, :], ACT.Square).then_inc(S("hn_sq"), 1)
                    act.wait_ge(S("hn_mean"), b["mean"] + 1)
                    act.activation(ss[:, :, :], ss[:, :, :], ACT.Sqrt).then_inc(S("hn_root"), 1)

                @block.vector
                def _(dve):
                    link = Link(dve, "dve_link")
                    for t in range(nt):
                        dve.wait_ge(S("hn_sq"), b["sq"] + t + 1)
                        dve.tensor_reduce(ss[:, t, :], sq[:, t % 2, :, :], X, ALU.add).then_inc(S("hn_ss"), 1)
                    dve.wait_ge(S("hn_ss"), b["ss"] + nt)
                    dve.tensor_scalar(ss[:, :, :], ss[:, :, :], 1.0 / QKD, EPS, ALU.mult, ALU.add).then_inc(S("hn_mean"), 1)
                    dve.wait_ge(S("hn_root"), b["root"] + 1)
                    link(dve.reciprocal(ss[:, :, :], ss[:, :, :]))
                    for t in range(nt):
                        link(dve.tensor_tensor(buf[:, t, :, :], buf[:, t, :, :],
                                               ss[:, t, :].unsqueeze(2).to_broadcast([P, HEADS, QKD]), ALU.mult))
                        link(dve.tensor_tensor(buf[:, t, :, :], buf[:, t, :, :],
                                               gain_row.unsqueeze(1).to_broadcast([P, HEADS, QKD]), ALU.mult))
                        if t < rope_tiles:
                            xr = buf[:, t, :, NOPE:QKD]
                            tab = lambda i: rope[:, t, i, :].unsqueeze(1).to_broadcast([P, HEADS, ROPE])
                            halves = lambda ap, s: ap.rearrange("p h (a s e) -> p h a s e", a=2, s=2)[:, :, :, s, :]
                            dve.tensor_tensor(t1[:, :, :], xr, tab(0), ALU.mult)
                            dve.tensor_copy(halves(t2[:, :, :], 0), halves(xr, 1))
                            link(dve.tensor_copy(halves(t2[:, :, :], 1), halves(xr, 0)))
                            link(dve.tensor_tensor(t2[:, :, :], t2[:, :, :], tab(1), ALU.mult))
                            link(dve.tensor_tensor(xr, t1[:, :, :], t2[:, :, :], ALU.add))

        def second():
            w_in2 = A["w_in_2"][0]
            with nc.Block() as block:
                @block.vector
                def _(dve):
                    for dst, g, s, v in ((1, 7, 1, 0), (3, 7, 1, 1), (5, 8, 4, 0)):
                        dve.scalar_tensor_tensor(gains[:, dst, :], modv[:, s, :, v], 1.0, gains[:, g, :], ALU.add, ALU.mult)
                    for dst, s, v in ((2, 0, 0), (4, 0, 1), (6, 3, 0)):
                        dve.tensor_copy(gains[:, dst, :], modv[:, s, :, v])

                @block.sync
                def _(sp):
                    with nc.allow_non_contiguous_dma("per-channel vectors"):
                        for i, s in enumerate((2, 5)):
                            sp.dma_start(vec(res_gates_d[i]), modv[:, s, :, 0]).then_inc(S("mod_out"), 16)
                    sp.wait_ge(S("mod_out"), 32)
            mix = ExitStack()
            fT = sb(mix, "fT", [P, 4, T])
            low_rank = ExitStack()
            cq = sb(low_rank, "cq", [P, 3, T])
            ckv = sb(low_rank, "ckv", [P, 2, NKEY])
            kpe = sb(low_rank, "kpe", [P, NKT, ROPE])
            with ExitStack() as st:
                hA = pair(st, "hA", [P, KD, NKEY])
                go = sb(st, "go2", [P, 4, 512])
                norm_T(x1_d, NT, gains[:, 1, :], gains[:, 2, :], tuple(h[:, :, 0:T] for h in hA), tag="n2")
                norm_T(A["ctx_2"][0], NTC, gains[:, 3, :], gains[:, 4, :], tuple(h[:, :, T:NKEY] for h in hA), tag="n3")

                def gate(kind, act, src, m, x):
                    n = 2 * m + x
                    if n >= 4:
                        act.wait_ge(S(f"g2_out{n % 4}"), 16 * (n // 4))
                    return act.activation(go[:, n % 4, :], src, ACT.Sigmoid)

                def gate_out(act, m, x, done):
                    n = 2 * m + x
                    act.wait_ge(*done)
                    act.dma_start(gates2_d[:, m, x * 512:(x + 1) * 512], go[:, n % 4, :]).then_inc(S(f"g2_out{n % 4}"), 16)
                    if n == 31:
                        for i in range(4):
                            act.wait_ge(S(f"g2_out{i}"), 16 * 8)

                latent = tuple(h[:, :, 0:T] for h in hA)
                put = lambda dst: lambda kind, eng, src, m, x: copy(
                    kind, eng, dst[:, m, x * 512:min((x + 1) * 512, dst.shape[2])],
                    src[:, 0:min(512, dst.shape[2] - x * 512)])
                gemm([dict(w=wcols(w_in2, 0, QL), mode="T", act=whole(latent), tiles=2, evac=put(cq)),
                      dict(w=wcols(w_in2, QL, QL + KVL), mode="T", tiles=3, evac=put(ckv),
                           act=lambda k, x: tuple(h[:, k, x * 512:min((x + 1) * 512, NKEY)] for h in hA)),
                      dict(w=wcols(w_in2, QL + KVL, OFF_F), mode="N", act=token_tiles(hA), tiles=NKT,
                           evac=lambda kind, eng, src, m, x: copy(kind, eng, kpe[:, m, :], src[:, 0:ROPE])),
                      dict(w=wcols(w_in2, OFF_F, OFF_F + 512), mode="T", act=whole(latent), tiles=2, evac=put(fT)),
                      dict(w=wcols(w_in2, OFF_GA, OFF_GA + 2 * D), mode="T", act=whole(latent), tiles=2, evac=gate,
                           on="act", act_step=gate_out)])

            with ExitStack() as st:
                foT = fT
                dc = sb(st, "dft_ch", [P, 2 * P])
                dp = sb(st, "dft_pos", [P, 4, 4, 512])
                ab = sb(st, "dft_ab", [P, NT, 4, 2, P])
                fold = sb(st, "dft_fold", [P, 4, 2, 4, 2, P])
                load([(dc[:, :], A["c_dft_ch"]), (dp[:, :, :, :].rearrange("p t a k -> p t (a k)"),
                                                  A["c_dft_pos"].rearrange("(t p) a b k -> p t (a b k)", p=P))])
                block = st.enter_context(nc.Block())

                @block.tensor
                def _(pe):
                    for tt in range(NT):
                        if tt >= 4:
                            pe.wait_ge(S("ft_ab"), 2 * (tt - 3))
                        for g in range(4):
                            mm = pe.matmul(ps[:, 2 * (tt % 4) + g // 2, (g % 2) * 256:(g % 2 + 1) * 256],
                                           fT[:, g, tt * P:(tt + 1) * P], dc[:, :], start=True, stop=True)
                        mm.then_inc(S("ft_mm"), 1)
                    pe.wait_ge(S("ft_fold"), 8)
                    for n, (g, par) in enumerate([(g, par) for g in range(4) for par in range(2)]):
                        for pt_ in range(4):
                            for x in range(2):
                                mm = pe.matmul(ps[:, n, :], fold[:, pt_, par, g, x, :], dp[:, pt_, 2 * par + x, :],
                                               start=(pt_ + x == 0), stop=(pt_ + x == 4))
                        mm.then_inc(S("ft_out"), 1)

                @block.scalar
                def _(act):
                    for tt in range(NT):
                        act.wait_ge(S("ft_mm"), tt + 1)
                        for x in range(2):
                            act.activation(ab[:, tt, 2 * x:2 * x + 2, :, :].rearrange("p g x c -> p (g x c)"),
                                           ps[:, 2 * (tt % 4) + x, :], ACT.Copy).then_inc(S("ft_ab"), 1)

                @block.vector
                def _(dve):
                    flat = lambda ap: ap.rearrange("p g x c -> p (g x c)")
                    dve.wait_ge(S("ft_ab"), 2 * NT)
                    for tt in range(4):
                        for par, op in ((0, ALU.add), (1, ALU.subtract)):
                            dve.tensor_tensor(flat(fold[:, tt, par]), flat(ab[:, tt]), flat(ab[:, tt + 4]), op
                                              ).then_inc(S("ft_fold"), 1)
                    for n in range(8):
                        g, par = divmod(n, 2)
                        dve.wait_ge(S("ft_out"), n + 1)
                        dve.tensor_copy(foT[:, g, par::2], ps[:, n, :]).then_inc(S("ft_done"), 1)

                @block.sync
                def _(sp):
                    sp.wait_ge(S("ft_done"), 8)
                    sp.dma_start(four_d, foT[:, :, :]).then_inc(S("ft_stored"), 16)
                    sp.wait_ge(S("ft_stored"), 16)

            kv_slices = [(0, 512), (512, 512), (1024, 256)]
            mla = ExitStack()
            q = sb(mla, "mla_q", [P, NT, HEADS, QKD])
            kb = sb(mla, "mla_k", [P, NKT, HEADS, QKD])
            vb = sb(mla, "mla_v", [P, NKT, HEADS, VD])
            rowg = sb(mla, "mla_rowg", [P, 2, QKD])
            with ExitStack() as st:
                gv = sb(st, "mla_gv", [P, 5])
                rowv = lambda ap: bass.AP(tensor=ap.tensor, offset=ap.offset, ap=[[0, P], [1, QKD]])
                load([(gv[:, 0:3], vec(A["q_a_norm_g_2"][0], 3)), (gv[:, 3:5], vec(A["kv_a_norm_g_2"][0], 2)),
                      (rowg[:, 0, :], rowv(A["q_norm_g_2"][0])), (rowg[:, 1, :], rowv(A["k_norm_g_2"][0]))])
                cqp = pair(st, "cqp", [P, 3, T])
                ckvp = pair(st, "ckvp", [P, 2, NKEY])
                chan_norm(cq, cqp, 3, [(0, 512), (512, 512)], gv[:, 0:3], QL, "q")
                chan_norm(ckv, ckvp, 2, kv_slices, gv[:, 3:5], KVL, "kv")
                wq = A["w_q_up_2"][0]
                qf = q[:, :, :, :].rearrange("p t h c -> p t (h c)")

                def split_kv(kind, eng, src, m, ci):
                    s4 = src.rearrange("p (h c) -> p h c", c=P)
                    copy(kind, eng, kb[:, m, 4 * ci:4 * ci + 4, 0:NOPE], s4[:, :, 0:NOPE])
                    return copy(kind, eng, vb[:, m, 4 * ci:4 * ci + 4, :], s4[:, :, NOPE:])
                gemm([dict(w=wcols(wq, 384 * i, 384 * i + 384), mode="N", act=token_tiles(cqp), tiles=NT,
                           evac=lambda kind, eng, src, m, x, i=i: copy(
                               kind, eng, qf[:, m, i * 384:(i + 1) * 384], src[:, 0:384])) for i in range(2)]
                     + [dict(w=wcols(A["w_kv_up_2"][0], 512 * i, 512 * i + 512), mode="N", act=token_tiles(ckvp), tiles=NKT,
                             evac=lambda kind, eng, src, m, x, i=i: split_kv(kind, eng, src, m, i)) for i in range(2)],
                     ring=4)
                with nc.Block() as block:
                    @block.vector
                    def _(dve):
                        for t in range(NKT):
                            dve.tensor_copy(kb[:, t, :, NOPE:QKD],
                                            kpe[:, t, :].unsqueeze(1).to_broadcast([P, HEADS, ROPE]))
                head_norm_rope(q, NT, rowg[:, 0, :], NT, "q")
                head_norm_rope(kb, NKT, rowg[:, 1, :], NT, "k")
            dump("q", q[:, :, :, :].rearrange("p t h c -> p (t h c)"))
            dump("k", kb[:, :, :, :].rearrange("p t h c -> p (t h c)"))
            SC = QKD ** -0.5
            with ExitStack() as st:
                qT = sb(st, "qT", [QKD, 2, T])
                kT = sb(st, "kT", [QKD, 2, NKEY])
                pr = sb(st, "mla_p", [P, 2, NKEY])
                pT = sb(st, "mla_pT", [P, 2, NKT, P])
                nm = sb(st, "mla_nm", [P, HEADS * NT])
                den = sb(st, "mla_den", [P, HEADS * NT])
                ao = fT[:, :, :].rearrange("p c t -> p (c t)").rearrange("p (t c) -> p t c", c=512)
                block = st.enter_context(nc.Block())
                its = [(h, t) for h in range(HEADS) for t in range(NT)]
                GR = [(0, 4), (4, 4), (8, 2)]

                N = len(its)
                s3 = lambda n: ps[:, 3 * (n % 2):3 * (n % 2) + 3, :].rearrange("p a b -> p (a b)")[:, 0:NKEY]
                out_bank = lambda n: ps[:, 3 * ((n + 1) % 2) + 2, 256:256 + VD]

                def head_group(h, i):
                    src, dst, t0, n_ = (q, qT, 4 * i, NT) if i < 2 else (kb, kT, 4 * (i - 2), NKT)
                    return src, t0, min(4, n_ - t0), dst

                def next_head(n):
                    h, t = its[n]
                    return (h + 1, t - 1) if 1 <= t <= 5 and h + 1 < HEADS else None

                @block.tensor
                def _(pe):
                    def head(h, i):
                        src, t0, w, _d = head_group(h, i)
                        n = 5 * h + i
                        if n:
                            pe.wait_ge(S("ml_hev"), n)
                        for j in range(w):
                            tr = pe.transpose(ps[0:QKD, 7, j * P:(j + 1) * P], src[:, t0 + j, h, :], ident[:, :])
                        tr.then_inc(S("ml_htr"), 1)

                    def scores(n):
                        h, t = its[n]
                        if t == 0:
                            pe.wait_ge(S("ml_hev"), 5 * h + 5)
                        if n >= 2:
                            pe.wait_ge(S("ml_e"), n - 1)
                        for i in range(3):
                            w = 512 if i < 2 else 256
                            if i == 2 and n >= 3:
                                pe.wait_ge(S("ml_o"), n - 2)
                            mm = pe.matmul(ps[:, 3 * (n % 2) + i, 0:w], qT[:, h % 2, t * P:(t + 1) * P],
                                           kT[:, h % 2, i * 512:i * 512 + w], start=True, stop=True)
                        mm.then_inc(S("ml_s"), 1)

                    def transposes(n, i):
                        g0, w = GR[i]
                        for j in range(w):
                            tr = pe.transpose(ps[:, 6 + i % 2, j * P:(j + 1) * P],
                                              pr[:, n % 2, (g0 + j) * P:(g0 + j + 1) * P], ident[:, :])
                        tr.then_inc(S("ml_t"), 1)

                    def output(n):
                        h = its[n][0]
                        pe.wait_ge(S("ml_pd"), n + 1)
                        pe.wait_ge(S("ml_pa"), 2 * n + 2)
                        for k in range(NKT):
                            mm = pe.matmul(out_bank(n), pT[:, n % 2, k, :], vb[:, k, h, :],
                                           start=(k == 0), stop=(k == NKT - 1))
                        mm.then_inc(S("ml_pv"), 1)

                    for i in range(5):
                        head(0, i)
                    scores(0)
                    for n in range(N):
                        if n + 1 < N:
                            scores(n + 1)
                        pe.wait_ge(S("ml_e"), n + 1)
                        if n:
                            pe.wait_ge(S("ml_pa"), 2 * n)
                            pe.wait_ge(S("ml_pd"), n)
                        if n and next_head(n - 1):
                            hh, i = next_head(n - 1)
                            pe.wait_ge(S("ml_hev"), 5 * hh + i + 1)
                        transposes(n, 0)
                        transposes(n, 1)
                        if n:
                            output(n - 1)
                        pe.wait_ge(S("ml_pa"), 2 * n + 1)
                        transposes(n, 2)
                        if next_head(n):
                            pe.wait_ge(S("ml_pd"), n + 1)
                            head(*next_head(n))
                    output(N - 1)

                @block.scalar
                def _(act):
                    def exponentials(n):
                        act.wait_ge(S("ml_m"), n + 1)
                        if n >= 2:
                            act.wait_ge(S("ml_t"), 3 * (n - 1))
                        act.activation(pr[:, n % 2, :], s3(n), ACT.Exp, bias=nm[:, n:n + 1], scale=SC,
                                       accum_out=den[:, n:n + 1]).then_inc(S("ml_e"), 1)

                    def probs(n, i):
                        g0, w = GR[i]
                        act.wait_ge(S("ml_t"), 3 * n + i + 1)
                        if i == 0 and n >= 2:
                            act.wait_ge(S("ml_pv"), n - 1)
                        act.activation(pT[:, n % 2, g0:g0 + w, :].rearrange("p k t -> p (k t)"), ps[:, 6, 0:w * P],
                                       ACT.Copy).then_inc(S("ml_pa"), 1)

                    exponentials(0)
                    for n in range(N):
                        probs(n, 0)
                        if n + 1 < N:
                            exponentials(n + 1)
                        probs(n, 2)

                @block.vector
                def _(dve):
                    link = Link(dve, "dve_link")

                    def head(h, i):
                        _s, t0, w, dst = head_group(h, i)
                        dve.wait_ge(S("ml_htr"), 5 * h + i + 1)
                        dve.tensor_copy(dst[:, h % 2, t0 * P:(t0 + w) * P], ps[0:QKD, 7, 0:w * P]
                                        ).then_inc(S("ml_hev"), 1)

                    def row_max(n):
                        dve.wait_ge(S("ml_s"), n + 1)
                        link(dve.tensor_reduce(nm[:, n:n + 1], s3(n), X, ALU.max))
                        dve.tensor_scalar(nm[:, n:n + 1], nm[:, n:n + 1], -SC, None, ALU.mult).then_inc(S("ml_m"), 1)

                    def output(n):
                        h, t = its[n]
                        dve.wait_ge(S("ml_e"), n + 1)
                        link(dve.reciprocal(den[:, n:n + 1], den[:, n:n + 1]))
                        dve.wait_ge(S("ml_pv"), n + 1)
                        dve.tensor_scalar(ao[:, t, h * VD:(h + 1) * VD], out_bank(n), den[:, n:n + 1], None, ALU.mult
                                          ).then_inc(S("ml_o"), 1)

                    for i in range(5):
                        head(0, i)
                    row_max(0)
                    for n in range(N):
                        if n + 1 < N:
                            row_max(n + 1)
                        dve.wait_ge(S("ml_t"), 3 * n + 2)
                        if n >= 2:
                            dve.wait_ge(S("ml_pv"), n - 1)
                        dve.tensor_copy(pT[:, n % 2, 4:8, :].rearrange("p k t -> p (k t)"), ps[:, 7, :]
                                        ).then_inc(S("ml_pd"), 1)
                        if n:
                            output(n - 1)
                        if next_head(n):
                            head(*next_head(n))
                    output(N - 1)
            mla.close()
            low_rank.close()

            merged = pair(mix, "merged2", [P, KD, T])
            with ExitStack() as st:
                oa = pair(st, "oa2", [P, 4, T])
                of = pair(st, "of2", [P, 4, T])
                with ExitStack() as s2:
                    fr = sb(s2, "four_raw", [P, 4, T])
                    block = s2.enter_context(nc.Block())

                    @block.sync
                    def _(sp):
                        for c in range(4):
                            sp.dma_start(fr[:, c, :], four_d[:, c, :]).then_inc(S(f"m2_in{c}"), 16)

                    @block.tensor
                    def _(pe):
                        for t in range(NT):
                            for c in range(4):
                                tr = pe.transpose(ps[:, t, c * P:(c + 1) * P], ao[:, t, c * P:(c + 1) * P], ident[:, :])
                            tr.then_inc(S("m2_tr"), 1)

                    @block.scalar
                    def _(act):
                        for t in range(NT):
                            act.wait_ge(S("m2_tr"), t + 1)
                            high(act, oa[0][:, :, t * P:(t + 1) * P], ps[:, t, :].rearrange("p (c x) -> p c x", x=P)
                                 ).then_inc(S("m2_hi"), 1)
                        for c in range(4):
                            act.wait_ge(S(f"m2_in{c}"), 16)
                            high(act, of[0][:, c, :], fr[:, c, :]).then_inc(S("m2_hi"), 1)

                    @block.vector
                    def _(dve):
                        for t in range(NT):
                            tok = slice(t * P, (t + 1) * P)
                            dve.wait_ge(S("m2_hi"), t + 1)
                            low(dve, oa[1][:, :, tok], ps[:, t, :].rearrange("p (c x) -> p c x", x=P), oa[0][:, :, tok])
                        for c in range(4):
                            dve.wait_ge(S("m2_hi"), NT + c + 1)
                            low(dve, of[1][:, c, :], fr[:, c, :], of[0][:, c, :])
                merge(merged, gates2_d, A["w_o_attn_2"][0], A["w_fourier_2"][0], oa, of, "2")
            with ExitStack() as st:
                g1r = sb(st, "g1r", [P, D])
                x2 = sb(st, "x2_sum", [P, NT, D])

                def rows_io(gp):
                    gp.dma_start(g1r[:, :], row(res_gates_d[0])).then_inc(S("r2_in"), 16)
                    gp.dma_start(x2[:, :, :], x1_d.rearrange("(t p) d -> p t d", p=P)).then_inc(S("r2_in"), 16)
                    for t in range(NT):
                        gp.wait_ge(S("r2_x"), t + 1)
                        gp.dma_start(x2_d[t * P:(t + 1) * P, :], x2[:, t, :]).then_inc(S("r2_out"), 16)
                    gp.wait_ge(S("r2_out"), 16 * NT)

                link = [None]
                prod = sb(st, "g1_prod", [P, 512])

                def add(kind, dve, src, m, i):
                    cols = slice(i * 512, (i + 1) * 512)
                    if link[0] is None:
                        link[0] = Link(dve, "dve_link")
                        dve.wait_ge(S("r2_in"), 32)
                    link[0](dve.tensor_tensor(prod[:, :], src, g1r[:, cols], ALU.mult))
                    link[0](dve.tensor_tensor(x2[:, m, cols], x2[:, m, cols], prod[:, :], ALU.add))
                    if i == 1:
                        dve.engine_nop().then_inc(S("r2_x"), 1)
                    return dve.engine_nop()
                gemm([dict(w=wcols(A["w_out_2"][0], 512 * i, 512 * i + 512), mode="N", act=token_tiles(merged), tiles=NT,
                           on="dve", evac=lambda kind, eng, src, m, x, i=i: add(kind, eng, src, m, i))
                      for i in range(2)], pool=rows_io)
            mix.close()

            xn_d = dram("xn_rows", [T, D])
            y_d = dram("y_rows", [T, D])
            moe = ExitStack()
            slot = sb(moe, "slot", [P, NT, NE])
            tg = sb(moe, "tg", [P, NT, NE, 2])
            sel = sb(moe, "sel", [P, NE, 2])
            idx = sb(moe, "idx", [P, NE], U32)
            iota = sb(moe, "iota", [P, CAP])
            with ExitStack() as st:
                h2T = sb(st, "h2T", [P, KD, T])
                norm_T(x2_d, NT, gains[:, 5, :], gains[:, 6, :], None, dst=h2T, rows_out=xn_d, tag="n4")
                wr = sb(st, "wr", [P, KD, NE])
                tok = sb(st, "tok", [P, NT])
                lg = sb(st, "lg", [P, NT, NE])
                m1 = sb(st, "lg_m", [P, NT])
                affT = sb(st, "affT", [NE, T])
                work = sb(st, "work", [NE, T])
                one = sb(st, "one", [NE, T])
                m8 = sb(st, "m8", [NE, 8])
                zero = sb(st, "zero", [P, D])
                oh = sb(st, "oh", [P, 4, CAP])
                load([(wr[:, :, :], A["w_router_2"][0].rearrange("(k p) e -> p k e", p=P)), (tok[:, :], A["c_tok"]),
                      (iota[:, :], A["c_slot"])])
                block = st.enter_context(nc.Block())

                @block.tensor
                def _(pe):
                    for t in range(NT):
                        for k in range(KD):
                            mm = pe.matmul(ps[:, 0, t * NE:(t + 1) * NE], h2T[:, k, t * P:(t + 1) * P], wr[:, k, :],
                                           start=(k == 0), stop=(k == KD - 1))
                    mm.then_inc(S("ro_l"), 1)
                    pe.wait_ge(S("ro_a"), 1)
                    for t in range(NT):
                        tr = pe.transpose(ps[0:NE, 1 + t // 4, (t % 4) * P:(t % 4 + 1) * P], lg[:, t, :], ident[:, :])
                    tr.then_inc(S("ro_t"), 1)
                    pe.wait_ge(S("ro_s"), 1)
                    for t in range(NT):
                        tr = pe.transpose(ps[:, 3, t * NE:(t + 1) * NE], work[:, t * P:(t + 1) * P], ident[0:NE, 0:NE])
                    tr.then_inc(S("ro_st"), 1)
                    for n in range(NE * NT):
                        e, t = divmod(n, NT)
                        pe.wait_ge(S("ro_oh"), n + 1)
                        pe.matmul(ps[:, 4, 2 * e:2 * e + 2], oh[:, n % 4, :], tg[:, t, e, :],
                                  start=(t == 0), stop=(t == NT - 1)).then_inc(S("ro_sel"), 1)

                @block.scalar
                def _(act):
                    act.wait_ge(S("ro_m"), 1)
                    act.activation(lg[:, :, :], lg[:, :, :], ACT.Exp).then_inc(S("ro_e"), 1)

                @block.sync
                def _(sp):
                    sp.wait_ge(S("ro_zero"), 1)
                    for t in range(NT):
                        sp.dma_start(y_d[t * P:(t + 1) * P, :], zero[:, :]).then_inc(S("ro_y0"), 16)
                    sp.wait_ge(S("ro_y0"), 16 * NT)

                @block.vector
                def _(dve):
                    link = Link(dve, "dve_link")
                    dve.memset(zero[:, :], 0.0).then_inc(S("ro_zero"), 1)
                    link(dve.memset(one[:, :], 1.0))
                    dve.wait_ge(S("ro_l"), 1)
                    lgp = ps[:, 0, 0:NT * NE].rearrange("p (t e) -> p t e", e=NE)
                    wide = lambda ap: ap.unsqueeze(2).to_broadcast([P, NT, NE])
                    link(dve.tensor_reduce(m1[:, :], lgp, X, ALU.max))
                    dve.tensor_tensor(lg[:, :, :], lgp, wide(m1[:, :]), ALU.subtract).then_inc(S("ro_m"), 1)
                    dve.wait_ge(S("ro_e"), 1)
                    link(dve.tensor_reduce(m1[:, :], lg[:, :, :], X, ALU.add))
                    link(dve.reciprocal(m1[:, :], m1[:, :]))
                    dve.tensor_tensor(lg[:, :, :], lg[:, :, :], wide(m1[:, :]), ALU.mult).then_inc(S("ro_a"), 1)
                    dve.wait_ge(S("ro_a"), 1)
                    dve.tensor_copy(tg[:, :, :, 1], lg[:, :, :])
                    dve.tensor_copy(tg[:, :, :, 0], wide(tok[:, :]))
                    dve.wait_ge(S("ro_t"), 1)
                    for dst in (affT, work):
                        ins = dve.tensor_copy(dst[:, :].rearrange("p (a b) -> p a b", a=2), ps[0:NE, 1:3, :])
                    link(ins)
                    for _i in range(CAP // 8):
                        link(dve.max(m8[:, :], work[:, :]))
                        link(dve.match_replace(work[:, :], m8[:, :], work[:, :], -1.0))
                    link(dve.tensor_scalar(work[:, :], work[:, :], 0.0, None, ALU.is_lt))
                    link(dve.tensor_tensor_scan(affT[:, :], one[:, :], work[:, :], 0.0, ALU.mult, ALU.add))
                    link(dve.tensor_tensor(work[:, :], affT[:, :], work[:, :], ALU.mult))
                    dve.tensor_scalar(work[:, :], work[:, :], -1.0, None, ALU.add).then_inc(S("ro_s"), 1)
                    dve.wait_ge(S("ro_st"), 1)
                    link(dve.tensor_copy(slot[:, :, :].rearrange("p t e -> p (t e)"), ps[:, 3, 0:NT * NE]))
                    for n in range(NE * NT):
                        e, t = divmod(n, NT)
                        if n >= 4:
                            dve.wait_ge(S("ro_sel"), n - 3)
                        dve.tensor_scalar(oh[:, n % 4, :], iota[:, :], slot[:, t, e:e + 1], None, ALU.is_equal
                                          ).then_inc(S("ro_oh"), 1)
                    dve.wait_ge(S("ro_sel"), NE * NT)
                    link(dve.tensor_copy(sel[:, :, :].rearrange("p e x -> p (e x)"), ps[:, 4, 0:2 * NE]))
                    dve.tensor_copy(idx[:, :], sel[:, :, 0])
            dump("sel", sel[:, :, :].rearrange("p e x -> p (e x)"))

            with ExitStack() as st:
                wg = sb(st, "wg", [P, 2, KD, DE])
                wu = sb(st, "wu", [P, 2, KD, DE])
                wd = sb(st, "wd", [P, 2, 4, D])
                xe = sb(st, "xe", [P, 2, D])
                xeT = sb(st, "xeT", [P, KD, P])
                ag = sb(st, "ag", [P, DE])
                au = sb(st, "au", [P, DE])
                aT = sb(st, "aT", [P, 4, P])
                ye = sb(st, "ye", [P, 2, D])
                block = st.enter_context(nc.Block())

                @block.sync
                def _(sp):
                    for e in range(NE):
                        if e >= 2:
                            sp.wait_ge(S("mo_gu"), e - 1)
                        sp.dma_start(wg[:, e % 2], A["w_e_gate_2"][0, e].rearrange("(k p) f -> p k f", p=P)
                                     ).then_inc(S(f"mo_w{e % 2}"), 16)
                        sp.dma_start(wu[:, e % 2], A["w_e_up_2"][0, e].rearrange("(k p) f -> p k f", p=P)
                                     ).then_inc(S(f"mo_w{e % 2}"), 16)
                        if e >= 2:
                            sp.wait_ge(S("mo_d"), e - 1)
                        sp.dma_start(wd[:, e % 2], A["w_e_down_2"][0, e].rearrange("(k p) n -> p k n", p=P)
                                     ).then_inc(S(f"mo_wd{e % 2}"), 16)

                @block.gpsimd
                def _(pool):
                    def gather(e):
                        if e >= 2:
                            pool.wait_ge(S("mo_xt"), e - 1)
                        pool.indirect_dma_start(xe[:, e % 2, :], None, xn_d,
                                                bass.IndirectOffsetOnAxis(ap=idx[:, e:e + 1], axis=0),
                                                ).then_inc(S(f"mo_x{e % 2}"), 16)
                    gather(0)
                    for e in range(NE):
                        if e + 1 < NE:
                            gather(e + 1)
                        pool.wait_ge(S("mo_ye"), 2 * e + 2)
                        if e:
                            pool.wait_ge(S("mo_y"), 16 * e)
                        pool.indirect_dma_start(y_d, bass.IndirectOffsetOnAxis(ap=idx[:, e:e + 1], axis=0),
                                                ye[:, e % 2, :], None, compute_op=ALU.add).then_inc(S("mo_y"), 16)
                    pool.wait_ge(S("mo_y"), 16 * NE)

                @block.tensor
                def _(pe):
                    def xT(e):
                        pe.wait_ge(S(f"mo_x{e % 2}"), 16 * (e // 2 + 1))
                        if e:
                            pe.wait_ge(S("mo_xev"), 8 * e)
                        for k in range(KD):
                            tr = pe.transpose(ps[:, k // 4, (k % 4) * P:(k % 4 + 1) * P], xe[:, e % 2, k * P:(k + 1) * P],
                                              ident[:, :])
                        tr.then_inc(S("mo_xt"), 1)
                    xT(0)
                    for e in range(NE):
                        pe.wait_ge(S("mo_xev"), 8 * e + 8)
                        pe.wait_ge(S(f"mo_w{e % 2}"), 32 * (e // 2 + 1))
                        if e:
                            pe.wait_ge(S("mo_h"), e)
                        for w, b in ((wg, 2), (wu, 3)):
                            for k in range(KD):
                                mm = pe.matmul(ps[:, b, :], xeT[:, k, :], w[:, e % 2, k, :], start=(k == 0), stop=(k == KD - 1))
                            mm.then_inc(S("mo_a"), 1)
                        mm = pe.transpose(ps[:, 7, 0:P], ident[:, :], ident[:, :])
                        mm.then_inc(S("mo_gu"), 1)
                        if e + 1 < NE:
                            xT(e + 1)
                        pe.wait_ge(S("mo_h"), e + 1)
                        for f in range(4):
                            tr = pe.transpose(ps[:, 4, f * P:(f + 1) * P], au[:, f * P:(f + 1) * P], ident[:, :])
                        tr.then_inc(S("mo_ht"), 1)
                        pe.wait_ge(S("mo_hev"), e + 1)
                        pe.wait_ge(S(f"mo_wd{e % 2}"), 16 * (e // 2 + 1))
                        if e:
                            pe.wait_ge(S("mo_ye"), 2 * e)
                        for c in range(2):
                            for f in range(4):
                                mm = pe.matmul(ps[:, 5 + c, :], aT[:, f, :], wd[:, e % 2, f, c * 512:(c + 1) * 512],
                                               start=(f == 0), stop=(f == 3))
                        mm.then_inc(S("mo_d"), 1)

                @block.scalar
                def _(act):
                    for e in range(NE):
                        act.wait_ge(S("mo_a"), 2 * e + 1)
                        if e:
                            act.wait_ge(S("mo_h"), e)
                        act.activation(ag[:, :], ps[:, 2, :], ACT.Silu).then_inc(S("mo_s"), 1)
                        act.wait_ge(S("mo_ht"), e + 1)
                        if e:
                            act.wait_ge(S("mo_d"), e)
                        act.activation(aT[:, :, :].rearrange("p f t -> p (f t)"), ps[:, 4, :], ACT.Copy
                                       ).then_inc(S("mo_hev"), 1)
                        act.wait_ge(S("mo_d"), e + 1)
                        if e >= 2:
                            act.wait_ge(S("mo_y"), 16 * (e - 1))
                        for c in range(2):
                            act.activation(ye[:, e % 2, c * 512:(c + 1) * 512], ps[:, 5 + c, :], ACT.Copy,
                                           scale=sel[:, e, 1:2]).then_inc(S("mo_ye"), 1)

                @block.vector
                def _(dve):
                    def xev(e):
                        dve.wait_ge(S("mo_xt"), e + 1)
                        if e:
                            dve.wait_ge(S("mo_a"), 2 * e)
                        for k in range(KD):
                            dve.tensor_scalar(xeT[:, k, :], ps[:, k // 4, (k % 4) * P:(k % 4 + 1) * P],
                                              gains[:, 5, k:k + 1], gains[:, 6, k:k + 1], ALU.mult, ALU.add
                                              ).then_inc(S("mo_xev"), 1)
                    xev(0)
                    for e in range(NE):
                        dve.wait_ge(S("mo_s"), e + 1)
                        dve.wait_ge(S("mo_a"), 2 * e + 2)
                        if e:
                            dve.wait_ge(S("mo_ht"), e)
                        dve.tensor_tensor(au[:, :], ps[:, 3, :], ag[:, :], ALU.mult).then_inc(S("mo_h"), 1)
                        if e + 1 < NE:
                            xev(e + 1)
            moe.close()

            with ExitStack() as st:
                xf = sb(st, "xf", [P, NT, D])
                yf = sb(st, "yf", [P, NT, D])
                g2r = sb(st, "g2r", [P, D])
                block = st.enter_context(nc.Block())

                @block.sync
                def _(sp):
                    sp.dma_start(g2r[:, :], row(res_gates_d[1])).then_inc(S("fi_g"), 16)
                    for t in range(NT):
                        sp.dma_start(yf[:, t, :], y_d[t * P:(t + 1) * P, :]).then_inc(S(f"fi_in{t % 4}"), 16)
                        sp.dma_start(xf[:, t, :], x2_d[t * P:(t + 1) * P, :]).then_inc(S(f"fi_in{t % 4}"), 16)
                    for t in range(NT):
                        sp.wait_ge(S("fi_x"), t + 1)
                        sp.dma_start(out[0, t * P:(t + 1) * P, :], xf[:, t, :]).then_inc(S("fi_out"), 16)
                    sp.wait_ge(S("fi_out"), 16 * NT)

                @block.vector
                def _(dve):
                    link = Link(dve, "dve_link")
                    dve.wait_ge(S("fi_g"), 16)
                    for q_ in range(4):
                        dve.wait_ge(S(f"fi_in{q_}"), 64)
                    for t in range(NT):
                        link(dve.tensor_tensor(yf[:, t, :], yf[:, t, :], g2r[:, :], ALU.mult))
                        dve.tensor_tensor(xf[:, t, :], xf[:, t, :], yf[:, t, :], ALU.add).then_inc(S("fi_x"), 1)

        w_in = A["w_in"][0]
        x_rows = A["x"][0]
        x1_d = dram("x1_rows", [T, D])
        x2_d = dram("x2_rows", [T, D])
        h_d = dram("h", [P, KD, T])
        orw_d = dram("o_rwkv", [P, 4, T])
        four_d = dram("fourier", [P, 4, T])
        gates_d = dram("gates", [P, 24, T])
        gates2_d = dram("gates2", [P, 16, T])
        res_gates_d = dram("res_gates", [2, D])
        line_d = dram("bias_line", [3, HEADS, 384])
        lines_d = dram("bias_lines", [3, HEADS, P, 384])
        h_stack = ExitStack()
        hT = sb(h_stack, "hT", [P, KD, T])
        bias_lines()
        rwkv()
        h_stack.close()
        merge_first()
        if debug is not None and "x1_in" in debug:
            with nc.Block() as block:
                @block.sync
                def _(sp):
                    sp.dma_start(x1_d, A["x1_in"]).then_inc(S("dbgx"), 16)
                    sp.wait_ge(S("dbgx"), 16)
        if debug is None or debug.get("second", 1):
            second()
        dump("end", ident[:, :])


def kernel(**inputs):
    import numpy as _np
    import concourse.bacc as _bacc
    from concourse import mybir as _mybir
    from concourse.bass_utils import run_bass_kernel_spmd as _run

    nc = _bacc.Bacc("TRN2", target_bir_lowering=False, num_devices=1)
    arrays, aps = {}, {}
    for name, a in list(inputs.items()) + list(constants().items()):
        a = _np.ascontiguousarray(a)
        if name == "c_ctx_2":
            a = a.reshape(1, -1)
        arrays[name] = a
        aps[name] = nc.dram_tensor(name, a.shape, _mybir.dt.from_np(a.dtype), kind="ExternalInput").ap()
    out = nc.dram_tensor("out_0", (1, T, D), F32, kind="ExternalOutput").ap()
    build(nc, aps, out)
    r = _run(nc, [arrays], core_ids=[0])
    return r.results[0]["out_0"]
```

```python
import math
from contextlib import ExitStack

import numpy as np

import concourse.bass as bass
from concourse import mybir

F32 = mybir.dt.float32
F32R = mybir.dt.float32r
BF16 = mybir.dt.bfloat16
U32 = mybir.dt.uint32
ALU = mybir.AluOpType
ACT = mybir.ActivationFunctionType
X = mybir.AxisListType.X

P = 128
T = 1024
NT = T // P
D = 1024
KD = D // P
HEADS = 8
HD = 64
AW = HEADS * HD
DILATIONS = (1, 4, 16)
STEPS = 128
MASKED = -1e30
QKV = 9 * AW
OFF_Z = QKV
OFF_RWKV = OFF_Z + AW
OFF_ZR = OFF_RWKV + 3 * AW + 128
OFF_MERGE = OFF_ZR + AW
C = 64
SUB = 16
DECAY = math.exp(-0.5)
GN_EPS = 64e-5
EPS = 1e-6
CTX = 256
NTC = CTX // P
QKD, NOPE, ROPE, VD = 96, 64, 32, 64
QL, KVL = 384, 256
OFF_F = QL + KVL + ROPE
OFF_GA = OFF_F + 512
NE, DE, CAP = 16, 512, 128
NKEY = T + CTX
NKT = NKEY // P


def bucket(dist):
    d = np.maximum(np.asarray(dist), 0)
    ratio = np.log(np.maximum(d, 1).astype(np.float32) / 16) / np.float32(math.log(2048 / 16))
    large = np.minimum(16 + (ratio * 16).astype(np.int32), 31)
    return np.where(d < 16, d, large).astype(np.int32)


def stride_of(dil):
    return min(dil, T // P)


def constants():
    f = np.float32
    i = np.arange(P)
    c = {"c_ident": np.eye(P, dtype=f)}
    c["c_hones"] = (i[:, None] // HD == i[None] // HD).astype(f)
    c["c_ones"] = np.ones((P, P), f)
    c["c_resets"] = np.tile((np.arange(T) % C != 0).astype(f), (P, 1))
    same = i[:, None] // C == i[None] // C
    c["c_mask_ar"] = np.concatenate([same & (i[:, None] < i[None]), same & (i[:, None] <= i[None])], 1).astype(f)
    c["c_mask_off"] = (same & (i[:, None] > i[None]) & (i[:, None] // SUB != i[None] // SUB)).astype(f)
    c["c_eye64"] = np.tile(np.eye(C, dtype=f), (2, 1))
    y = np.arange(383)
    rel = 255 - y
    hot = np.zeros((33, 3, 384), f)
    for g, dil in enumerate(DILATIONS):
        step = stride_of(dil)
        valid = (rel >= 0) & (rel * step <= STEPS * dil) & (rel * step % dil == 0)
        b = bucket(np.maximum(rel, 0) * step)
        for n in range(383):
            hot[b[n] if valid[n] else 32, g, n] = 1
    c["c_hot"] = hot
    c["c_eye16"] = np.tile(np.eye(SUB, dtype=f).reshape(1, 1, -1), (P, 4, 1)).reshape(P, -1)
    a = 2 * np.pi * np.outer(i, i) / P
    c["c_dft_ch"] = np.concatenate([np.cos(a), np.sin(a)], 1).astype(f)
    p = np.arange(T // 2)[:, None]
    s = 1 / math.sqrt(T * P)
    pos = np.zeros((T // 2, 2, 2, T // 2), np.float64)
    for par in range(2):
        k = 2 * np.arange(T // 2)[None] + par
        a = 2 * np.pi * ((p * k) % T) / T
        pos[:, par, 0] = np.cos(a) * s
        pos[:, par, 1] = -np.sin(a) * s
    c["c_dft_pos"] = pos.astype(f)
    inv = (1.0 / (np.float32(10000.0) ** (np.arange(8, dtype=f) / 8))).astype(f)
    t = np.arange(T)
    ang = [np.concatenate([q.astype(f)[:, None] * inv] * 2, 1) for q in (t // 64, t % 64)]
    sign = np.concatenate([-np.ones(8), np.ones(8)]).astype(f)
    c["c_rope"] = np.stack([np.concatenate([np.cos(x) for x in ang], 1),
                            np.concatenate([np.sin(x) * sign for x in ang], 1)], 1).astype(f)
    c["c_slot"] = np.tile(np.arange(CAP, dtype=f), (P, 1))
    c["c_tok"] = np.stack([np.tile(np.arange(NT)[None] * P, (P, 1)), np.tile(i[:, None], (1, NT))], 2).astype(f)
    return c


def build(nc, A, out, debug=None):
    ctx = ExitStack()
    sems = {}
    used = {}

    def S(name):
        if name not in sems:
            sems[name] = nc.alloc_semaphore(name=name)
        return sems[name]

    def retire(*prefixes):
        over = [n for n in sems if n.startswith(prefixes)]
        nc.clear_and_free_semaphores([sems.pop(n) for n in over])
        for n in over:
            used.pop(n, None)
        with nc.Block() as block:
            @block.gpsimd
            def _(gp):
                gp.engine_nop()

    def sb(stack, name, shape, dt=F32):
        return stack.enter_context(nc.sbuf_tensor(name, shape, dt))

    def dram(name, shape, dt=F32):
        return nc.dram_tensor(name, shape, dt, kind="Internal").ap()

    def dump(name, ap):
        if debug is None or name not in debug:
            return
        with nc.Block() as block:
            @block.sync
            def _(sp):
                s = S("dbg")
                debug[name]["n"] = debug["_"] = debug.get("_", 0) + 16
                sp.dma_start(debug[name]["ap"], ap).then_inc(s, 16)
                sp.wait_ge(s, debug["_"])

    class Link:

        def __init__(self, eng, name):
            self.eng, self.sem = eng, S(name)
            self.n = Link.last.get(name, 0)
            self.name = name

        def __call__(self, ins):
            self.n += 1
            Link.last[self.name] = self.n
            ins.then_inc(self.sem, 1)
            self.eng.wait_ge(self.sem, self.n)

    Link.last = {}

    def base(name, count):
        b = used.get(name, 0)
        used[name] = b + count
        return b

    with ctx:
        ps = ctx.enter_context(nc.psum_tensor("ps", [P, 8, 512], F32))
        S("fi_out")
        ident = sb(ctx, "ident", [P, P])
        ones = sb(ctx, "ones", [P, P])
        gains = sb(ctx, "gains", [P, 9, 8])
        modv = sb(ctx, "modv", [P, 6, KD, 2])

        def load(pairs):
            with nc.Block() as block:
                @block.sync
                def _(sp):
                    b = base("loaded", 16 * len(pairs))
                    for dst, src in pairs:
                        with nc.allow_non_contiguous_dma("per-channel vectors"):
                            sp.dma_start(dst, src).then_inc(S("loaded"), 16)
                    sp.wait_ge(S("loaded"), b + 16 * len(pairs))

        def start_load(name, pairs):
            b = base(name, 16 * len(pairs))
            with nc.Block() as block:
                @block.sync
                def _(sp):
                    for dst, src in pairs:
                        sp.dma_start(dst, src).then_inc(S(name), 16)
            return b + 16 * len(pairs)

        def vec(ap, n=KD):
            return ap.rearrange("(k p) -> p k", p=P)


        def pair(stack, name, shape):
            return sb(stack, name + "_hi", shape, F32R), sb(stack, name + "_lo", shape, F32R)

        def high(act, dst, src):
            return act.activation(dst, src, ACT.Copy)

        def low(dve, dst, src, hi):
            return dve.tensor_tensor(dst, src, hi.bitcast(F32), ALU.subtract)

        def products(pe, out, a, b, first, last):
            pe.matmul(out, a[1], b[0], start=first, stop=False)
            pe.matmul(out, a[0], b[1], start=False, stop=False)
            return pe.matmul(out, a[0], b[0], start=False, stop=last)

        SPLIT = 1024

        def gemm(jobs, ring=6, raws=2, banks=8, side=None, pool=None):
            pieces, groups = [], []
            for job in jobs:
                w = job["w"]
                kt, cols = w.shape[1], w.shape[2]
                first = len(pieces)
                if job["mode"] == "T":
                    for m in range(cols // P):
                        pieces.append((w[:, :, m * P:(m + 1) * P], kt, P))
                        groups += [(job, m, x, [(first + m, k, k) for k in range(kt)]) for x in range(job["tiles"])]
                else:
                    per = min(kt, SPLIT // cols)
                    for k in range(0, kt, per):
                        pieces.append((w[:, k:min(k + per, kt), :], min(per, kt - k), cols))
                    groups += [(job, m, 0, [(first + k // per, k % per, k) for k in range(kt)])
                               for m in range(job["tiles"])]
            NP, NG = len(pieces), len(groups)
            last_use = [max(n for n, g in enumerate(groups) if any(u[0] == i for u in g[3])) for i in range(NP)]
            on_act = []
            for job, m, x, _u in groups:
                on = job.get("on", "alt")
                on_act.append(len(on_act) % 2 == 0 if on == "alt" else on == "act")
            place = [sum(a == on_act[n] for a in on_act[:n + 1]) for n in range(NG)]
            order = [("split", i) for i in range(min(ring, NP))]
            for n in range(NG):
                order.append(("evac", n))
                order += [("split", i) for i in range(ring, NP) if last_use[i - ring] == n]
            braw = [base(f"gemm_raw{b}", 16 * len(range(b, NP, raws))) for b in range(raws)]
            bhi, blo, bmm = base("gemm_hi", NP), base("gemm_lo", NP), base("gemm_mm", NG)
            bev = [base("gemm_ev0", sum(on_act)), base("gemm_ev1", NG - sum(on_act))]
            ev = lambda n: (S("gemm_ev0" if on_act[n] else "gemm_ev1"), bev[not on_act[n]] + place[n])
            with ExitStack() as st:
                raw = sb(st, f"raw{bmm}", [P, raws, SPLIT])
                whi, wlo = pair(st, f"w{bmm}", [P, ring, SPLIT])
                view = lambda ap, i: ap[:, 0:pieces[i][1] * pieces[i][2]]
                block = st.enter_context(nc.Block())

                @block.sync
                def _(sp):
                    for i, (w, kn, cols) in enumerate(pieces):
                        if i >= raws:
                            sp.wait_ge(S("gemm_hi"), bhi + i - raws + 1)
                            sp.wait_ge(S("gemm_lo"), blo + i - raws + 1)
                        sp.dma_start(raw[:, i % raws, 0:kn * cols].rearrange("p (k n) -> p k n", k=kn), w
                                     ).then_inc(S(f"gemm_raw{i % raws}"), 16)

                if pool is not None:
                    @block.gpsimd
                    def _(gp):
                        pool(gp, ev)

                @block.tensor
                def _(pe):
                    if side is not None and "first" in side:
                        side["first"]("pe", pe)
                    ready = -1
                    for n, (job, m, x, uses) in enumerate(groups):
                        if m == 0 and x == 0 and job.get("ready"):
                            for name, value in job["ready"]:
                                pe.wait_ge(S(name), value)
                        if n >= banks:
                            pe.wait_ge(*ev(n - banks))
                        for i, at, k in uses:
                            if i > ready:
                                pe.wait_ge(S("gemm_hi"), bhi + i + 1)
                                pe.wait_ge(S("gemm_lo"), blo + i + 1)
                                ready = i
                            cols = pieces[i][2]
                            w = (whi[:, i % ring, at * cols:(at + 1) * cols], wlo[:, i % ring, at * cols:(at + 1) * cols])
                            first, last = k == uses[0][2], k == uses[-1][2]
                            if job["mode"] == "T":
                                a = job["act"](k, x)
                                mm = products(pe, ps[:, n % banks, 0:a[0].shape[-1]], w, a, first, last)
                            else:
                                mm = products(pe, ps[:, n % banks, 0:cols], job["act"](k, m), w, first, last)
                        mm.then_inc(S("gemm_mm"), 1)
                        if side is not None and n in side["at"]:
                            side["pe"](pe, side["at"][n])

                @block.scalar
                def _(act):
                    if side is not None and "first" in side:
                        side["first"]("act", act)
                    for what, n in order:
                        if what == "split":
                            act.wait_ge(S(f"gemm_raw{n % raws}"), braw[n % raws] + 16 * (n // raws + 1))
                            if n >= ring:
                                act.wait_ge(S("gemm_mm"), bmm + last_use[n - ring] + 1)
                            high(act, view(whi[:, n % ring, :], n), view(raw[:, n % raws, :], n)).then_inc(S("gemm_hi"), 1)
                        else:
                            job, m, x, _u = groups[n]
                            if on_act[n]:
                                act.wait_ge(S("gemm_mm"), bmm + n + 1)
                                job["evac"]("act", act, ps[:, n % banks, :], m, x).then_inc(S("gemm_ev0"), 1)
                            if "act_step" in job:
                                job["act_step"](act, m, x, ev(n))
                            if side is not None and n in side["at"] and "act" in side:
                                side["act"](act, side["at"][n])

                @block.vector
                def _(dve):
                    if side is not None and "first" in side:
                        side["first"]("dve", dve)
                    for what, n in order:
                        if what == "split":
                            dve.wait_ge(S("gemm_hi"), bhi + n + 1)
                            low(dve, view(wlo[:, n % ring, :], n), view(raw[:, n % raws, :], n),
                                view(whi[:, n % ring, :], n)).then_inc(S("gemm_lo"), 1)
                        else:
                            job, m, x, _u = groups[n]
                            if not on_act[n]:
                                dve.wait_ge(S("gemm_mm"), bmm + n + 1)
                                job["evac"]("dve", dve, ps[:, n % banks, :], m, x).then_inc(S("gemm_ev1"), 1)
                            if "dve_step" in job:
                                job["dve_step"](dve, m, x, ev(n))
                            if side is not None and n in side["at"]:
                                side["dve"](dve, side["at"][n])

        def copy(kind, eng, dst, src):
            if kind == "act":
                return eng.activation(dst, src, ACT.Copy)
            return eng.tensor_copy(dst, src)

        def wcols(w, a, b):
            return w[:, a:b].rearrange("(k p) n -> p k n", p=P)

        def norm_T(src, nt, gain, shift, to, dst=None, rows_out=None, banks=8, after=None, tag="n"):
            with ExitStack() as st:
                xa = sb(st, f"{tag}_x", [P, 3, D])
                sq = sb(st, f"{tag}_sq", [P, D])
                ss = sb(st, f"{tag}_ss", [P, nt])
                tmp = sb(st, f"{tag}_tmp", [P, 4, 4, P]) if dst is None else None
                place = lambda t, b: (tmp[:, (2 * t + b) % 4] if dst is None else
                                      dst[:, 4 * b:4 * b + 4, t * P:(t + 1) * P])
                names = {"x0": 16 * len(range(0, nt, 3)), "x1": 16 * len(range(1, nt, 3)), "x2": 16 * len(range(2, nt, 3)),
                         "ss": nt, "mean": nt, "root": nt, "rcp": nt, "xn": nt, "t": 2 * nt, "ev": 2 * nt,
                         "hi": 2 * nt if to else 0, "lo": 2 * nt if to else 0, "out": 16 * nt if rows_out is not None else 0}
                b0 = {n: base("norm_" + n, c) for n, c in names.items()}
                at = lambda eng, n, v: eng.wait_ge(S("norm_" + n), b0[n] + v)
                block = st.enter_context(nc.Block())

                @block.sync
                def _(sp):
                    for t in range(nt):
                        if t >= 3:
                            at(sp, "t", 2 * (t - 2))
                            if rows_out is not None:
                                at(sp, "out", 16 * (t - 2))
                        sp.dma_start(xa[:, t % 3, :], src[t * P:(t + 1) * P, :]).then_inc(S(f"norm_x{t % 3}"), 16)

                if rows_out is not None:
                    @block.gpsimd
                    def _(gp):
                        for t in range(nt):
                            at(gp, "xn", t + 1)
                            gp.dma_start(rows_out[t * P:(t + 1) * P, :], xa[:, t % 3, :]).then_inc(S("norm_out"), 16)
                            at(gp, "out", 16 * (t + 1))

                @block.scalar
                def _(act):
                    def squares(t):
                        at(act, f"x{t % 3}", 16 * (t // 3 + 1))
                        if t:
                            at(act, "ss", t)
                        act.activation(sq[:, :], xa[:, t % 3, :], ACT.Square, accum_out=ss[:, t:t + 1]
                                       ).then_inc(S("norm_ss"), 1)

                    def highs(t):
                        for b in range(2):
                            at(act, "ev", 2 * t + b + 1)
                            high(act, to[0][:, 4 * b:4 * b + 4, t * P:(t + 1) * P], place(t, b)).then_inc(S("norm_hi"), 1)

                    def root(t):
                        at(act, "mean", t + 1)
                        act.activation(ss[:, t:t + 1], ss[:, t:t + 1], ACT.Sqrt).then_inc(S("norm_root"), 1)
                    squares(0)
                    root(0)
                    squares(1)
                    for t in range(nt):
                        at(act, "rcp", t + 1)
                        act.activation(xa[:, t % 3, :], xa[:, t % 3, :], ACT.Copy, scale=ss[:, t:t + 1]
                                       ).then_inc(S("norm_xn"), 1)
                        if t + 1 < nt:
                            root(t + 1)
                        if t + 2 < nt:
                            squares(t + 2)
                        if t and to:
                            highs(t - 1)
                    if to:
                        highs(nt - 1)

                @block.vector
                def _(dve):
                    link = Link(dve, "dve_link")
                    wide = lambda v, b: v[:, 4 * b:4 * b + 4].unsqueeze(2).to_broadcast([P, 4, P])

                    def evacs(t):
                        if t >= 2 and dst is None:
                            at(dve, "lo", 2 * (t - 1))
                        for b in range(2):
                            at(dve, "t", 2 * t + b + 1)
                            src_ = ps[:, (2 * t + b) % banks, :].rearrange("p (k t) -> p k t", t=P)
                            ins = dve.tensor_tensor(place(t, b), src_, wide(gain, b), ALU.mult)
                            if shift is not None:
                                link(ins)
                                ins = dve.tensor_tensor(place(t, b), place(t, b), wide(shift, b), ALU.add)
                            ins.then_inc(S("norm_ev"), 1)

                    def lows(t):
                        for b in range(2):
                            at(dve, "hi", 2 * t + b + 1)
                            cut_ = (slice(None), slice(4 * b, 4 * b + 4), slice(t * P, (t + 1) * P))
                            low(dve, to[1][cut_], place(t, b), to[0][cut_]).then_inc(S("norm_lo"), 1)

                    def mean(t):
                        at(dve, "ss", t + 1)
                        dve.tensor_scalar(ss[:, t:t + 1], ss[:, t:t + 1], 1.0 / D, EPS, ALU.mult, ALU.add
                                          ).then_inc(S("norm_mean"), 1)
                    mean(0)
                    for t in range(nt):
                        at(dve, "root", t + 1)
                        dve.reciprocal(ss[:, t:t + 1], ss[:, t:t + 1]).then_inc(S("norm_rcp"), 1)
                        if t + 1 < nt:
                            mean(t + 1)
                        if t:
                            evacs(t - 1)
                            if to:
                                lows(t - 1)
                    evacs(nt - 1)
                    if to:
                        lows(nt - 1)

                @block.tensor
                def _(pe):
                    for t in range(nt):
                        at(pe, "xn", t + 1)
                        for b in range(2):
                            if 2 * t + b >= banks:
                                at(pe, "ev", 2 * t + b - banks + 1)
                            for j in range(4):
                                k = 4 * b + j
                                tr = pe.transpose(ps[:, (2 * t + b) % banks, j * P:(j + 1) * P],
                                                  xa[:, t % 3, k * P:(k + 1) * P], ident[:, :])
                            tr.then_inc(S("norm_t"), 1)
                        if after is not None and t:
                            at(pe, "ev", 2 * t)
                            after(pe, t - 1)
                    if after is not None:
                        at(pe, "ev", 2 * nt)
                        after(pe, nt - 1)

        def whole(p, w=512):
            return lambda k, x: tuple(h[:, k, x * w:(x + 1) * w] for h in p)

        def token_tiles(p):
            return lambda k, m: tuple(h[:, k, m * P:(m + 1) * P] for h in p)

        def rwkv():
            keep = ExitStack()
            kv = sb(keep, "kv", [P, 8, T + 1])
            pc = sb(keep, "pc", [P, 4, T // C])
            vecs = sb(keep, "rw_vecs", [P, 8, 4])
            mix = sb(keep, "rw_mix", [P, 13])
            hones = sb(keep, "hones", [P, P])
            rl = sb(keep, "rl", [P, 5, T + 1])
            lora = sb(keep, "lora", [P, AW])
            names = ["rwkv_w0", "rwkv_a0", "rwkv_k_k", "rwkv_k_a", None, "rwkv_ln_w", "rwkv_ln_b"]
            pairs = [(vecs[:, i, :], vec(A[n][0], 4)) for i, n in enumerate(names) if n]
            pairs += [(vecs[:, 4, :], vec(A["rwkv_r_k"][0].rearrange("h n -> (h n)"), 4)),
                      (mix[:, :], vec(A["rwkv_shift_mix"][0], 13)), (hones[:, :], A["c_hones"]),
                      (lora[0:64, :], A["rwkv_w_up"][0]), (lora[64:P, :], A["rwkv_a_up"][0])]
            load(pairs + [(gains[:, 0, :], vec(A["pre_norm_gain"][0])), (ident[:, :], A["c_ident"]),
                          (ones[:, :], A["c_ones"])])
            hpair = ExitStack()
            hp = pair(hpair, "h", [P, KD, T])
            norm_T(x_rows, NT, gains[:, 0, :], None, hp, dst=hT, tag="n1")

            def place_of(c):
                return rl[:, c, :] if c < 4 else rl[:, 4, :] if c == 12 else kv[:, c - 4, :]

            def keep_h(gp, ev):
                gp.dma_start(h_d, hT[:, :, :]).then_inc(S("h_out"), 16)
                gp.wait_ge(S("h_out"), 16)
            diff = sb(hpair, "diff", [P, T])
            link = [None]

            def shift(dve, m, x, done):
                if link[0] is None:
                    link[0] = Link(dve, "dve_link")
                    dve.memset(rl[:, :, 0:1], 0.0)
                    link[0](dve.memset(kv[:, :, 0:1], 0.0))
                    link[0](dve.tensor_scalar(vecs[:, 7, :], vecs[:, 3, :], -1.0, 1.0, ALU.mult, ALU.add))
                if x:
                    pr = place_of(m)
                    dve.wait_ge(*done)
                    link[0](dve.tensor_tensor(diff[:, :], pr[:, 0:T], pr[:, 1:T + 1], ALU.subtract))
                    link[0](dve.scalar_tensor_tensor(pr[:, 1:T + 1], diff[:, :], mix[:, m:m + 1],
                                                     pr[:, 1:T + 1], ALU.mult, ALU.add))
            gemm([dict(w=wcols(w_in, OFF_RWKV, OFF_RWKV + 1664), mode="T", act=whole(hp), tiles=2, on="act",
                       evac=lambda kind, eng, src, m, x: copy(
                           kind, eng, place_of(m)[:, 1 + x * 512:513 + x * 512], src), dve_step=shift)],
                 ring=3, pool=keep_h)
            hpair.close()
            ar = sb(keep, "ar", [P, 4, NT, 2, P])
            bt = sb(keep, "bt", [P, 4, T])
            bonus = sb(keep, "bonus", [P, 4, T])
            ozr = sb(keep, "ozr", [P, 4, T])

            with ExitStack() as st:
                def t_(n):
                    return sb(st, "rw_" + n, [P, T])
                sig, a, cs, csm, pi, kk, w1, w2 = map(t_, ["sig", "a", "cs", "csm", "pi", "kk", "w1", "w2"])
                resets = sb(st, "resets", [P, T])
                load([(resets[:, :], A["c_resets"])])
                pr_, pp = sig, csm
                block = st.enter_context(nc.Block())
                two = lambda b: ps[:, b:b + 2, :].rearrange("p a b -> p (a b)")

                @block.tensor
                def _(pe):
                    pe.wait_ge(S("rw_tanh"), 1)
                    for c in range(4):
                        if c:
                            pe.wait_ge(S("rw_sig"), 2 * c)
                        for hf in range(2):
                            cols = slice(1 + hf * 512, 513 + hf * 512)
                            pe.matmul(ps[:, hf, :], lora[0:64, c * P:(c + 1) * P], rl[0:64, 4, cols],
                                      start=True, stop=True)
                            mm = pe.matmul(ps[:, 2 + hf, :], lora[64:P, c * P:(c + 1) * P], rl[64:P, 4, cols],
                                           start=True, stop=True)
                        mm.then_inc(S("rw_lora"), 1)
                        for name, src, b in (("rw_ksq", w1, 4), ("rw_rk", w2, 6)):
                            pe.wait_ge(S(name), c + 1)
                            for hf in range(2):
                                mm = pe.matmul(ps[:, b + hf, :], hones[:, :], src[:, hf * 512:(hf + 1) * 512],
                                               start=True, stop=True)
                            mm.then_inc(S(name + "_sum"), 1)

                @block.scalar
                def _(act):
                    act.activation(rl[0:64, 4, 1:T + 1], rl[0:64, 4, 1:T + 1], ACT.Tanh).then_inc(S("rw_tanh"), 1)
                    for c in range(4):
                        act.wait_ge(S("rw_lora"), c + 1)
                        if c:
                            act.wait_ge(S("rw_tile"), c)
                        act.activation(sig[:, :], two(0), ACT.Sigmoid, bias=vecs[:, 0, c:c + 1]).then_inc(S("rw_sig"), 1)
                        act.activation(a[:, :], two(2), ACT.Sigmoid, bias=vecs[:, 1, c:c + 1]).then_inc(S("rw_sig"), 1)
                        act.wait_ge(S("rw_cs"), c + 1)
                        act.activation(pr_[:, :], cs[:, :], ACT.Exp, scale=-DECAY).then_inc(S("rw_exp"), 1)
                        act.activation(pi[:, :], cs[:, :], ACT.Exp, scale=DECAY).then_inc(S("rw_exp"), 1)
                        act.activation(pp[:, :], csm[:, :], ACT.Exp, scale=-DECAY).then_inc(S("rw_exp"), 1)
                        act.wait_ge(S("rw_nrm"), c + 1)
                        act.activation(w1[:, :], w1[:, :], ACT.Sqrt).then_inc(S("rw_root"), 1)

                @block.vector
                def _(dve):
                    link = Link(dve, "dve_link")
                    for c in range(4):
                        k_ = kv[:, c, 1:T + 1]
                        v_ = kv[:, 4 + c, 1:T + 1]
                        r_ = rl[:, c, 1:T + 1]
                        by_tile = lambda ap: ap.rearrange("p (n t) -> p n t", t=P)
                        link(dve.tensor_scalar(kk[:, :], k_, vecs[:, 2, c:c + 1], None, ALU.mult))
                        dve.tensor_tensor(w1[:, :], kk[:, :], kk[:, :], ALU.mult).then_inc(S("rw_ksq"), 1)
                        dve.wait_ge(S("rw_sig"), 2 * c + 2)
                        link(dve.tensor_tensor_scan(cs[:, :], resets[:, :], sig[:, :], 0.0, ALU.mult, ALU.add))
                        dve.tensor_tensor(csm[:, :], cs[:, :], sig[:, :], ALU.subtract).then_inc(S("rw_cs"), 1)
                        dve.wait_ge(S("rw_ksq_sum"), c + 1)
                        dve.tensor_scalar(w1[:, :], two(4), 1e-24, None, ALU.max).then_inc(S("rw_nrm"), 1)
                        link(dve.tensor_scalar(w2[:, :], a[:, :], vecs[:, 3, c:c + 1], vecs[:, 7, c:c + 1],
                                               ALU.mult, ALU.add))
                        link(dve.tensor_tensor(k_, k_, w2[:, :], ALU.mult))
                        link(dve.scalar_tensor_tensor(w2[:, :], r_, vecs[:, 4, c:c + 1], k_, ALU.mult, ALU.mult))
                        dve.engine_nop().then_inc(S("rw_rk"), 1)
                        dve.wait_ge(S("rw_exp"), 3 * c + 3)
                        dve.tensor_tensor(by_tile(k_), by_tile(k_), by_tile(pi[:, :]), ALU.mult)
                        dve.tensor_tensor(ar[:, c, :, 1, :], by_tile(r_), by_tile(pr_[:, :]), ALU.mult)
                        dve.tensor_copy(pc[:, c, :], pr_[:, C - 1:T:C])
                        dve.wait_ge(S("rw_root"), c + 1)
                        link(dve.reciprocal(w1[:, :], w1[:, :]))
                        link(dve.tensor_tensor(kk[:, :], kk[:, :], w1[:, :], ALU.mult))
                        dve.scalar_tensor_tensor(ar[:, c, :, 0, :], by_tile(kk[:, :]), -1.0, by_tile(pp[:, :]),
                                                 ALU.mult, ALU.mult)
                        link(dve.tensor_tensor(w1[:, :], kk[:, :], a[:, :], ALU.mult))
                        dve.tensor_tensor(bt[:, c, :], w1[:, :], pi[:, :], ALU.mult)
                        dve.wait_ge(S("rw_rk_sum"), c + 1)
                        dve.tensor_tensor(bonus[:, c, :], two(6), v_, ALU.mult).then_inc(S("rw_tile"), 1)
                        dve.wait_ge(S("rw_tile"), c + 1)
            dump("ar", ar[:, :, :, :, :].rearrange("p a b c d -> p (a b c d)"))
            dump("bt", bt[:, :, :])
            dump("bonus", bonus[:, :, :])

            l_d = dram("rw_l", [NT * HEADS, P, P])
            w_d = dram("rw_w", [P, 4 * SUB * SUB])
            masks = sb(keep, "rw_masks", [P, 4, P])
            eye64 = sb(keep, "eye64", [P, C])
            load([(masks[:, 0, :], A["c_mask_off"]), (masks[:, 1, :], A["c_mask_ar"][:, P:2 * P]),
                  (masks[:, 2, :], A["c_mask_ar"][:, 0:P]), (masks[:, 3, :], A["c_mask_ar"][:, P:2 * P]),
                  (eye64[:, :], A["c_eye64"])])
            with ExitStack() as st:
                lbuf = sb(st, "lbuf", [P, 2, HEADS, P])
                lt = sb(st, "lt", [P, 4, SUB, SUB])
                wt = sb(st, "wt", [P, 4, SUB, SUB])
                tmp = sb(st, "wtmp", [P, 4 * SUB * SUB])
                block = st.enter_context(nc.Block())

                @block.tensor
                def _(pe):
                    for tt in range(NT):
                        if tt >= 4:
                            pe.wait_ge(S("rw_lev"), 2 * (tt - 3))
                        for h in range(HEADS):
                            rows = slice(64 * (h % 2), 64 * (h % 2) + 64)
                            mm = pe.matmul(ps[:, 2 * (tt % 4) + h % 2, (h // 2) * P:(h // 2 + 1) * P],
                                           bt[rows, h // 2, tt * P:(tt + 1) * P], ar[rows, h // 2, tt, 0, :],
                                           start=True, stop=True)
                        mm.then_inc(S("rw_lmm"), 1)

                @block.vector
                def _(dve):
                    link = Link(dve, "dve_link")
                    for tt in range(NT):
                        dve.wait_ge(S("rw_lmm"), tt + 1)
                        if tt >= 2:
                            dve.wait_ge(S(f"rw_ldump{tt % 2}"), 16 * (tt // 2))
                        for par in range(2):
                            dve.tensor_tensor(lbuf[:, tt % 2, par::2, :],
                                              ps[:, 2 * (tt % 4) + par, :].rearrange("p (h t) -> p h t", t=P),
                                              masks[:, 2:3, :].to_broadcast([P, 4, P]),
                                              ALU.mult).then_inc(S("rw_lev"), 1)
                    dve.wait_ge(S("rw_lin"), 16 * 9)
                    for t in range(1, SUB):
                        v = tmp[:, 0:4 * t * t].rearrange("p (b j s) -> p b j s", b=4, j=t)
                        coef = lt[:, :, 0:t, t:t + 1].rearrange("p b s o -> p b o s").to_broadcast([P, 4, t, t])
                        if t == 1:
                            link(dve.tensor_copy(wt[:, :, 0, 1], lt[:, :, 0, 1]))
                            continue
                        link(dve.tensor_tensor(v, wt[:, :, 0:t, 0:t], coef, ALU.mult))
                        link(dve.tensor_reduce(wt[:, :, 0:t, t], v, X, ALU.add))
                    dve.engine_nop().then_inc(S("rw_inv"), 1)

                @block.sync
                def _(sp):
                    sp.dma_start(wt[:, :, :, :].rearrange("p a b c -> p (a b c)"), A["c_eye16"]).then_inc(S("rw_lin"), 16)
                    for tt in range(NT):
                        sp.wait_ge(S("rw_lev"), 2 * tt + 2)
                        sp.dma_start(l_d[tt * HEADS:(tt + 1) * HEADS].rearrange("h s t -> s h t"),
                                     lbuf[:, tt % 2, :, :]).then_inc(S(f"rw_ldump{tt % 2}"), 16)
                    for b in range(2):
                        sp.wait_ge(S(f"rw_ldump{b}"), 16 * NT // 2)
                    for half in range(2):
                        for blk in range(4):
                            o = half * 64 + blk * SUB
                            sp.dma_start(lt[half * 64:half * 64 + 64, blk, :, :],
                                         l_d[:, o:o + SUB, o:o + SUB]).then_inc(S("rw_lin"), 16)
                    sp.wait_ge(S("rw_inv"), 1)
                    sp.dma_start(w_d, wt[:, :, :, :].rearrange("p a b c -> p (a b c)")).then_inc(S("rw_wout"), 16)
                    sp.wait_ge(S("rw_wout"), 16)

            with ExitStack() as st:
                scratch = rl[:, :, :].rearrange("p a b -> p (a b)")
                ti = scratch[:, 0:2048].rearrange("p (a h t) -> p a h t", a=2, t=P)
                m = scratch[:, 2048:4096].rearrange("p (h a t) -> p h a t", h=4, t=P)
                rhs = scratch[:, 4096:4608].rearrange("p (h c) -> p h c", h=4)
                tb = sb(st, "rw_tb", [P, 4, C])
                tkv = sb(st, "rw_tkv", [P, 2, 4, C])
                ft = sb(st, "rw_ft", [P, 4, P])
                z = sb(st, "rw_z", [P, 4, P])
                xb = sb(st, "rw_x", [P, 2, 4, P])
                gb = sb(st, "rw_gb", [P, 2, 2, C])
                hb = sb(st, "rw_hb", [P, 2, 2, C])
                qb = sb(st, "rw_qb", [P, 2, P])
                yi = sb(st, "rw_yi", [P, 2, P])
                state = sb(st, "rw_state", [P, 3, 4, C])
                s1 = sb(st, "rw_s1", [P, 2, C])
                gw = sb(st, "gate_w", [P, 3, KD, P])
                go = sb(st, "gate_out", [P, 2, 512])
                w_v = w_d.rearrange("(x u) (b s t) -> x b s u t", x=2, b=4, s=SUB)
                block = st.enter_context(nc.Block())
                rounds = [(tt, rd) for tt in range(NT) for rd in range(2)]
                GATES = 24
                assert 2 * GATES == 3 * len(rounds)

                @block.sync
                def _(sp):
                    def blocks(tt):
                        for half in range(2):
                            for blk in range(4):
                                o = half * 64 + blk * SUB
                                sp.dma_start(ti[o:o + SUB, tt % 2, :, o:o + SUB],
                                             w_v[half, blk, :, tt * HEADS:(tt + 1) * HEADS, :]
                                             ).then_inc(S(f"rw_ti{tt % 2}"), 16)

                    def gate_weights(m):
                        off = (OFF_ZR + m * P, OFF_Z + (m - 4) * P, OFF_MERGE + (m - 8) * P)[min(m // 4, 2)]
                        sp.dma_start(gw[:, m % 3], wcols(w_in, off, off + P)).then_inc(S(f"gate_w{m % 3}"), 16)

                    sp.wait_ge(S("rw_zeroed"), 2)
                    blocks(0)
                    for m in range(3):
                        gate_weights(m)
                    for r in range(len(rounds)):
                        if r % 2 == 0 and r // 2 + 1 < NT:
                            if r:
                                sp.wait_ge(S("rw_ymm"), r)
                            blocks(r // 2 + 1)
                        for n in range(3 * r, 3 * r + 3):
                            m, hf = divmod(n, 2)
                            sp.wait_ge(S("gate_ev"), n + 1)
                            sp.dma_start(gates_d[:, m, hf * 512:(hf + 1) * 512], go[:, n % 2, :]
                                         ).then_inc(S(f"gate_out{n % 2}"), 16)
                            if hf == 1 and m + 3 < GATES:
                                gate_weights(m + 3)
                    for x in range(2):
                        sp.wait_ge(S(f"gate_out{x}"), 16 * GATES)

                @block.tensor
                def _(pe):
                    queue = [(n, k) for n in range(2 * GATES) for k in range(KD)]

                    def gate_products(count):
                        for _i in range(count):
                            n, k = queue.pop(0)
                            m, hf = divmod(n, 2)
                            if k == 0:
                                pe.wait_ge(S(f"gate_w{m % 3}"), 16 * (m // 3 + 1))
                                if n:
                                    pe.wait_ge(S("gate_ev"), n)
                            mm = pe.matmul(ps[:, 7, :], gw[:, m % 3, k, :], hT[:, k, hf * 512:(hf + 1) * 512],
                                           start=(k == 0), stop=(k == KD - 1))
                            if k == KD - 1:
                                mm.then_inc(S("gate_mm"), 1)

                    for r, (tt, rd) in enumerate(rounds):
                        tok = slice(tt * P, (tt + 1) * P)
                        pe.wait_ge(S("rw_y"), r) if r else None
                        for cc in range(2):
                            c = 2 * rd + cc
                            pe.transpose(ps[:, 0, cc * P:(cc + 1) * P], ar[:, c, tt, 0, :], ident[:, :])
                            pe.transpose(ps[:, 0, 256 + cc * P:256 + (cc + 1) * P], bt[:, c, tok], ident[:, :])
                            pe.transpose(ps[:, 1, cc * P:(cc + 1) * P],
                                         kv[:, c, 1 + tt * P:1 + (tt + 1) * P], ident[:, :])
                            tr = pe.transpose(ps[:, 1, 256 + cc * P:256 + (cc + 1) * P],
                                              kv[:, 4 + c, 1 + tt * P:1 + (tt + 1) * P], ident[:, :])
                        tr.then_inc(S("rw_tr"), 1)
                        for hh in range(4):
                            c, rows = 2 * rd + hh // 2, slice(64 * (hh % 2), 64 * (hh % 2) + 64)
                            b_, k_ = bt[rows, c, tok], kv[rows, c, 1 + tt * P:1 + (tt + 1) * P]
                            pe.matmul(ps[:, 2 + hh, 0:P], ar[rows, c, tt, 0, :], b_, start=True, stop=True)
                            pe.matmul(ps[:, 2 + hh, P:2 * P], b_, ar[rows, c, tt, 1, :], start=True, stop=True)
                            mm = pe.matmul(ps[:, 2 + hh, 2 * P:4 * P], k_,
                                           ar[rows, c, tt, :, :].rearrange("p a b -> p (a b)"),
                                           start=True, stop=True)
                            mm.then_inc(S("rw_mat"), 1)
                        gate_products(3)
                        pe.wait_ge(S("rw_tok"), 3 * r + 3)
                        pe.wait_ge(S("rw_m"), 4 * r + 4)
                        pe.wait_ge(S(f"rw_ti{tt % 2}"), 128 * (tt // 2 + 1))
                        for hh in range(4):
                            pe.matmul(ps[:, 6, hh * C:(hh + 1) * C], m[:, hh, 2, :], tkv[:, 1, hh, :],
                                      start=True, stop=True)
                            mm = pe.matmul(ps[:, 2, hh * P:(hh + 1) * P], m[:, hh, 0, :], ti[:, tt % 2, 4 * rd + hh, :],
                                           start=True, stop=True)
                        mm.then_inc(S("rw_kav"), 1)
                        gate_products(3)
                        pe.wait_ge(S("rw_kf"), 2 * r + 2)
                        for hh in range(4):
                            mm = pe.matmul(ps[:, 0, hh * P:(hh + 1) * P], ti[:, tt % 2, 4 * rd + hh, :], rhs[:, hh, :],
                                           start=True, stop=True)
                        mm.then_inc(S("rw_zmm"), 1)
                        gate_products(2)
                        for i in range(3):
                            pe.wait_ge(S("rw_x"), 4 * r + i + 1)
                            src = z if i == 0 else xb[:, (i - 1) % 2]
                            for hh in range(4):
                                mm = pe.matmul(ps[:, 1 + i, hh * P:(hh + 1) * P], ft[:, hh, :], src[:, hh, :],
                                               start=True, stop=True)
                            mm.then_inc(S("rw_xmm"), 1)
                            gate_products(2 if i == 2 else 3)
                        pe.wait_ge(S("rw_x"), 4 * r + 4)
                        xf = xb[:, 0]
                        for hh in range(4):
                            cc, o = hh // 2, 64 * (hh % 2)
                            out_ = slice(o, o + 64)
                            for half in range(2):
                                t_ = slice(64 * half, 64 * half + 64)
                                pe.matmul(ps[out_, 4 + half, cc * C:(cc + 1) * C], xf[t_, hh, 0:C], tb[t_, hh, :],
                                          start=True, stop=True)
                                h_ = ps[out_, 4 + half, 128 + cc * C:128 + (cc + 1) * C]
                                pe.matmul(h_, tb[t_, hh, :], xf[t_, hh, C:2 * C], start=True, stop=False)
                                pe.matmul(h_, tkv[t_, 0, hh, :], tkv[t_, 1, hh, :], start=False, stop=True)
                            pe.matmul(ps[out_, 6, cc * P:(cc + 1) * P], xf[:, hh, 0:C], m[:, hh, 1, :],
                                      start=True, stop=True)
                            y_ = ps[out_, 1, 256 + cc * P:256 + (cc + 1) * P]
                            pe.matmul(y_, xf[:, hh, C:2 * C], m[:, hh, 1, :], start=True, stop=False)
                            mm = pe.matmul(y_, tkv[:, 1, hh, :], m[:, hh, 3, :], start=False, stop=True)
                        mm.then_inc(S("rw_gmm"), 1)
                        gate_products(3)
                        pe.wait_ge(S("rw_gq"), 3 * r + 3)
                        pe.wait_ge(S("rw_zeroed"), 2)
                        for half in range(2):
                            n = 2 * tt + half
                            if half:
                                pe.wait_ge(S("rw_st"), 2 * r + 1)
                            for hh in range(4):
                                cc, o = hh // 2, 64 * (hh % 2)
                                o = slice(o, o + 64)
                                mm = pe.matmul(ps[o, 2 + half, cc * C:(cc + 1) * C], gb[o, half, cc, :],
                                               state[o, n % 3, 2 * rd + cc, :], start=True, stop=True)
                            mm.then_inc(S("rw_cmm"), 1)
                            gate_products(3 if half == 0 else 0)
                            for hh in range(4):
                                cc, o = hh // 2, 64 * (hh % 2)
                                o = slice(o, o + 64)
                                mm = pe.matmul(ps[o, 0, cc * P + half * C:cc * P + half * C + C],
                                               state[o, n % 3, 2 * rd + cc, :], qb[o, cc, half * C:(half + 1) * C],
                                               start=True, stop=True)
                        mm.then_inc(S("rw_ymm"), 1)
                        gate_products(2)

                @block.scalar
                def _(act):
                    def gate_out(n):
                        act.wait_ge(S("gate_mm"), n + 1)
                        if n >= 2:
                            act.wait_ge(S(f"gate_out{n % 2}"), 16 * (n // 2))
                        act.activation(go[:, n % 2, :], ps[:, 7, :], ACT.Silu if n < 16 else ACT.Sigmoid
                                       ).then_inc(S("gate_ev"), 1)

                    for r, (tt, rd) in enumerate(rounds):
                        act.wait_ge(S("rw_tr"), r + 1)
                        act.activation(rhs[:, :, 0:C], ps[:, 0, 0:256].rearrange("p (h c) -> p h c", c=C),
                                       ACT.Copy).then_inc(S("rw_tok"), 1)
                        act.activation(tb[:, :, :].rearrange("p h c -> p (h c)"), ps[:, 0, 256:512],
                                       ACT.Copy).then_inc(S("rw_tok"), 1)
                        act.activation(tkv[:, :, :, :].rearrange("p a h c -> p (a h c)"), ps[:, 1, :],
                                       ACT.Copy).then_inc(S("rw_tok"), 1)
                        act.wait_ge(S("rw_kav"), r + 1)
                        act.activation(rhs[:, :, C:2 * C], ps[:, 6, 0:256].rearrange("p (h c) -> p h c", c=C),
                                       ACT.Copy).then_inc(S("rw_kf"), 1)
                        act.activation(ft[:, :, :].rearrange("p h t -> p (h t)"), ps[:, 2, :],
                                       ACT.Copy).then_inc(S("rw_kf"), 1)
                        gate_out(3 * r)
                        gate_out(3 * r + 1)
                        act.wait_ge(S("rw_gmm"), r + 1)
                        act.activation(yi[:, :, :].rearrange("p a t -> p (a t)"), ps[:, 1, 256:512],
                                       ACT.Copy).then_inc(S("rw_yi"), 1)
                        gate_out(3 * r + 2)

                @block.vector
                def _(dve):
                    link = Link(dve, "dve_link")
                    dve.memset(ti[:, :, :, :], 0.0).then_inc(S("rw_zeroed"), 1)
                    dve.memset(state[:, 0, :, :], 0.0).then_inc(S("rw_zeroed"), 1)
                    for r, (tt, rd) in enumerate(rounds):
                        for hh in range(4):
                            dve.wait_ge(S("rw_mat"), 4 * r + hh + 1)
                            dve.tensor_tensor(m[:, hh, :, :].rearrange("p a t -> p (a t)"), ps[:, 2 + hh, :],
                                              masks[:, :, :].rearrange("p a t -> p (a t)"),
                                              ALU.mult).then_inc(S("rw_m"), 1)
                        dve.wait_ge(S("rw_zmm"), r + 1)
                        flat = lambda ap: ap.rearrange("p h t -> p (h t)")
                        dve.tensor_copy(flat(z[:, :, :]), ps[:, 0, :]).then_inc(S("rw_x"), 1)
                        dve.wait_ge(S("rw_x"), 4 * r + 1)
                        for i in range(3):
                            dve.wait_ge(S("rw_xmm"), 3 * r + i + 1)
                            dve.tensor_tensor(flat(xb[:, i % 2]), ps[:, 1 + i, :], flat(z[:, :, :]),
                                              ALU.add).then_inc(S("rw_x"), 1)
                        dve.wait_ge(S("rw_gmm"), r + 1)
                        dve.tensor_tensor(gb[:, :, :, :], ps[:, 4:6, 0:P].rearrange("p a (c k) -> p a c k", k=C),
                                          eye64[:, :].unsqueeze(1).unsqueeze(1).to_broadcast([P, 2, 2, C]),
                                          ALU.add).then_inc(S("rw_gq"), 1)
                        dve.tensor_copy(hb[:, :, :, :].rearrange("p a c k -> p a (c k)"),
                                        ps[:, 4:6, P:2 * P]).then_inc(S("rw_gq"), 1)
                        dve.tensor_tensor(qb[:, :, :], ps[:, 6, 0:256].rearrange("p (c t) -> p c t", t=P),
                                          ar[:, 2 * rd:2 * rd + 2, tt, 1, :], ALU.add).then_inc(S("rw_gq"), 1)
                        dve.wait_ge(S("rw_gq"), 3 * r + 3)
                        for half in range(2):
                            n = 2 * tt + half
                            dve.wait_ge(S("rw_cmm"), 2 * r + half + 1)
                            link(dve.tensor_tensor(s1[:, :, :], ps[:, 2 + half, 0:P].rearrange("p (c k) -> p c k", k=C),
                                                   hb[:, half, :, :], ALU.add))
                            dve.tensor_tensor(state[:, (n + 1) % 3, 2 * rd:2 * rd + 2, :], s1[:, :, :],
                                              pc[:, 2 * rd:2 * rd + 2, n:n + 1].to_broadcast([P, 2, C]),
                                              ALU.mult).then_inc(S("rw_st"), 1)
                        dve.wait_ge(S("rw_ymm"), r + 1)
                        dve.wait_ge(S("rw_yi"), r + 1)
                        dve.tensor_tensor(ozr[:, 2 * rd:2 * rd + 2, tt * P:(tt + 1) * P],
                                          ps[:, 0, 0:256].rearrange("p (c t) -> p c t", t=P), yi[:, :, :],
                                          ALU.add).then_inc(S("rw_y"), 1)
            dump("y", ozr[:, :, :])

            with ExitStack() as st:
                sq = sb(st, "gn_sq", [P, 4, T])
                rs = sb(st, "gn_rs", [P, 4, T])
                block = st.enter_context(nc.Block())
                two = lambda b: ps[:, b:b + 2, :].rearrange("p a b -> p (a b)")

                def finish(eng, link, tiles):
                    for c in tiles:
                        link(eng.tensor_tensor(ozr[:, c, :], ozr[:, c, :], rs[:, c, :], ALU.mult))
                        link(eng.tensor_scalar(ozr[:, c, :], ozr[:, c, :], vecs[:, 5, c:c + 1], vecs[:, 6, c:c + 1],
                                               ALU.mult, ALU.add))
                        eng.tensor_tensor(ozr[:, c, :], ozr[:, c, :], bonus[:, c, :], ALU.add).then_inc(S("gn_out"), 1)

                @block.tensor
                def _(pe):
                    for i, src in enumerate((ozr, sq)):
                        if i:
                            pe.wait_ge(S("gn_sq"), 4)
                        for c in range(4):
                            for hf in range(2):
                                mm = pe.matmul(ps[:, 2 * c + hf, :], hones[:, :], src[:, c, hf * 512:(hf + 1) * 512],
                                               start=True, stop=True)
                            mm.then_inc(S("gn_sum"), 1)

                @block.scalar
                def _(act):
                    for c in range(4):
                        act.wait_ge(S("gn_c"), c + 1)
                        act.activation(sq[:, c, :], ozr[:, c, :], ACT.Square).then_inc(S("gn_sq"), 1)
                    act.wait_ge(S("gn_v"), 4)
                    act.activation(rs[:, :, :], rs[:, :, :], ACT.Sqrt).then_inc(S("gn_root"), 1)

                @block.vector
                def _(dve):
                    link = Link(dve, "dve_link")
                    for c in range(4):
                        dve.wait_ge(S("gn_sum"), c + 1)
                        dve.scalar_tensor_tensor(ozr[:, c, :], two(2 * c), -1.0 / HD, ozr[:, c, :],
                                                 ALU.mult, ALU.add).then_inc(S("gn_c"), 1)
                    for c in range(4):
                        dve.wait_ge(S("gn_sum"), 5 + c)
                        dve.tensor_scalar(rs[:, c, :], two(2 * c), 1.0 / HD, GN_EPS, ALU.mult, ALU.add
                                          ).then_inc(S("gn_v"), 1)
                    dve.wait_ge(S("gn_root"), 1)
                    for c in (3, 2, 0, 1):
                        link(dve.reciprocal(rs[:, c, :], rs[:, c, :]))
                        dve.engine_nop().then_inc(S("gn_rcp"), 1)
                    finish(dve, link, (0, 1))

                @block.gpsimd
                def _(gp):
                    link = Link(gp, "pool_link")
                    gp.wait_ge(S("gn_rcp"), 2)
                    finish(gp, link, (3, 2))

                @block.sync
                def _(sp):
                    sp.wait_ge(S("gn_out"), 4)
                    sp.dma_start(orw_d, ozr[:, :, :]).then_inc(S("rw_o_out"), 16)
                    sp.wait_ge(S("rw_o_out"), 16)
            keep.close()

        def bias_lines():
            with ExitStack() as st:
                tab = sb(st, "rel_tab", [33, 24])
                hot = sb(st, "hot", [33, 3, 384])
                line = sb(st, "line", [HEADS, 3, 384])
                load([(tab[0:32, :], A["rel_bias"]), (hot[:, :, :], A["c_hot"])])
                block = st.enter_context(nc.Block())

                @block.vector
                def _(dve):
                    dve.memset(tab[32:33, :], MASKED).then_inc(S("at_tab"), 1)
                    dve.wait_ge(S("at_line_mm"), 3)
                    dve.tensor_copy(line[:, :, :], ps[0:HEADS, 0:3, 0:384]).then_inc(S("at_line"), 1)

                @block.tensor
                def _(pe):
                    pe.wait_ge(S("at_tab"), 1)
                    for g in range(3):
                        pe.matmul(ps[0:HEADS, g, 0:384], tab[:, g * HEADS:(g + 1) * HEADS], hot[:, g, :],
                                  start=True, stop=True).then_inc(S("at_line_mm"), 1)

                @block.sync
                def _(sp):
                    sp.wait_ge(S("at_line"), 1)
                    sp.dma_start(line_d.rearrange("g h y -> h g y"), line[:, :, :]).then_inc(S("at_line_out"), 16)
                    sp.wait_ge(S("at_line_out"), 16)
                    for g in range(3):
                        sp.dma_start(lines_d[g], bass.AP(tensor=line_d.tensor, offset=g * HEADS * 384,
                                                         ap=[[384, HEADS], [0, P], [1, 384]])
                                     ).then_inc(S("at_lines"), 16)

        def attention(keep):
            ag_d = dram("attn_groups", [3, T, 528])
            REC = 528
            hs = ExitStack()
            hp = pair(hs, "h2", [P, KD, T])
            qz = sb(hs, "qz", [P, 2, 4, T])
            kk = sb(hs, "kk", [P, 4, T])
            v = sb(hs, "v", [P, NT, AW])
            cv = sb(hs, "cv", [P, KD, 2])
            bm = sb(hs, "bm", [P, 6, KD])
            mw = sb(hs, "mod_w", [P, 2, KD, 256])
            MODS = 6 * D // 256

            def mod_weights(eng, s_):
                if s_ >= 2:
                    eng.wait_ge(S("mod_mm"), s_ - 1)
                eng.dma_start(mw[:, s_ % 2], wcols(A["w_mod_2"][0], 256 * s_, 256 * s_ + 256)
                              ).then_inc(S(f"mod_w{s_ % 2}"), 16)

            def mod_products(pe, s_):
                if s_ == 0:
                    pe.wait_ge(S("mod_c"), 1)
                pe.wait_ge(S(f"mod_w{s_ % 2}"), 16 * (s_ // 2 + 1))
                if s_:
                    pe.wait_ge(S("mod_ev"), s_)
                for c in range(2):
                    for k in range(KD):
                        mm = pe.matmul(ps[:, 7, 2 * c:2 * c + 2], mw[:, s_ % 2, k, c * P:(c + 1) * P], cv[:, k, :],
                                       start=(k == 0), stop=(k == KD - 1))
                mm.then_inc(S("mod_mm"), 1)

            def mod_out(dve, s_):
                part, c = divmod(2 * s_, KD)
                dve.wait_ge(S("mod_mm"), s_ + 1)
                dve.tensor_tensor(modv[:, part, c:c + 2, :], ps[:, 7, 0:4].rearrange("p (c v) -> p c v", v=2),
                                  bm[:, part, c:c + 2].unsqueeze(2).to_broadcast([P, 2, 2]), ALU.add
                                  ).then_inc(S("mod_ev"), 1)

            load([(cv[:, :, 0], vec(A["c_2"][0])), (cv[:, :, 1], vec(A["c_ctx_2"][0])),
                  (bm[:, :, :], A["b_mod_2"][0].rearrange("(s k p) -> p s k", p=P, s=6)),
                  (gains[:, 7, :], vec(A["norm1_g_2"][0])), (gains[:, 8, :], vec(A["norm2_g_2"][0]))])
            with ExitStack() as st:
                raw = sb(st, "h_raw", [P, 4, T])
                block = st.enter_context(nc.Block())

                @block.sync
                def _(sp):
                    for k in range(KD):
                        if k >= 4:
                            sp.wait_ge(S("h_hi"), k - 3)
                            sp.wait_ge(S("h_lo"), k - 3)
                        sp.dma_start(raw[:, k % 4, :], h_d[:, k, :]).then_inc(S(f"h_in{k % 4}"), 16)

                @block.scalar
                def _(act):
                    act.activation(cv[:, :, :], cv[:, :, :], ACT.Silu).then_inc(S("mod_c"), 1)
                    for k in range(KD):
                        act.wait_ge(S(f"h_in{k % 4}"), 16 * (k // 4 + 1))
                        high(act, hp[0][:, k, :], raw[:, k % 4, :]).then_inc(S("h_hi"), 1)

                @block.vector
                def _(dve):
                    for k in range(KD):
                        dve.wait_ge(S("h_hi"), k + 1)
                        low(dve, hp[1][:, k, :], raw[:, k % 4, :], hp[0][:, k, :]).then_inc(S("h_lo"), 1)

                @block.gpsimd
                def _(gp):
                    mod_weights(gp, 0)
                    mod_weights(gp, 1)
                    gp.memset(qz[64:P, 0, :, :], 0.0)
                    gp.memset(qz[0:64, 1, :, :], 0.0)

            for g, dil in enumerate(DILATIONS):
                step = stride_of(dil)
                length = T // step
                off = [(which * 3 + g) * AW for which in range(3)]

                def spread(src, step=step):
                    return src.rearrange("p (i r) -> p i r", r=step)

                def places(dst, x, step=step):
                    w = 512 // step
                    return dst.rearrange("p (r i) -> p i r", r=step)[:, x * w:(x + 1) * w, :]

                def put_q(kind, eng, src, m, x):
                    copy(kind, eng, places(qz[0:64, 0, m, :], x), spread(src[0:64, :]))
                    return copy(kind, eng, places(qz[64:P, 1, m, :], x), spread(src[64:P, :]))

                def put_k(kind, eng, src, m, x):
                    return copy(kind, eng, places(kk[:, m, :], x), spread(src))

                def v_tokens(k, m, length=length, step=step):
                    r, i0 = divmod(m * P, length)
                    return tuple(h[:, k, :].rearrange("p (i r) -> p r i", r=step)[:, r, i0:i0 + P] for h in hp)

                def mods(gp, ev, g=g):
                    for s_ in range(8 * g + 2, min(8 * g + 10, MODS)):
                        mod_weights(gp, s_)
                gemm([dict(w=wcols(w_in, off[0], off[0] + AW), mode="T", act=whole(hp), tiles=2, evac=put_q),
                      dict(w=wcols(w_in, off[1], off[1] + AW), mode="T", act=whole(hp), tiles=2, evac=put_k),
                      dict(w=wcols(w_in, off[2], off[2] + AW), mode="N", act=v_tokens, tiles=NT,
                           evac=lambda kind, eng, src, m, x: copy(kind, eng, v[:, m, :], src))],
                     ring=5, banks=7, pool=mods,
                     side={"at": {3 * i + 2: 8 * g + i for i in range(8)}, "pe": mod_products, "dve": mod_out})
                with ExitStack() as gst:
                    bias = sb(gst, f"bias{g}", [P, 2, 4, 2 * P])
                    sbuf = sb(gst, f"sc{g}", [P, 2, 2, 4, 2 * P])
                    pt = sb(gst, f"pt{g}", [P, 2, 2, 2, 4, P])
                    og = sb(gst, f"og{g}", [P, 3, REC])
                    nkey = [2 if (j * P) % length and length > P else 1 for j in range(NT)]
                    ngrp = [2 * n for n in nkey]
                    gsum = [sum(ngrp[:j]) for j in range(NT + 1)]
                    block = gst.enter_context(nc.Block())
                    counts = {"sc": NT, "sb": NT, "exp": NT, "tr": gsum[NT], "pt0": gsum[NT] // 2, "pt1": gsum[NT] // 2,
                              "pv": NT, "og": NT, "nm": NT, "bias": 32}
                    counts.update({f"out{x}": 16 * len(range(x, NT, 3)) for x in range(3)})
                    sn = {n: S(f"at_{n}") for n in counts}
                    bs = {n: base(f"at_{n}", c) for n, c in counts.items()}
                    gv = ag_d[g].rearrange("(i r) c -> r i c", r=step)

                    @block.tensor
                    def _(pe):
                        def scores(j):
                            if j:
                                pe.wait_ge(sn["sb"], bs["sb"] + j)
                            k0 = (j + 1 - nkey[j]) * P
                            for h in range(HEADS):
                                w = nkey[j] * P
                                bank, o = 2 * (h % 2) + (h // 2) // 2, ((h // 2) % 2) * 256 + 256 - w
                                mm = pe.matmul(ps[:, bank, o:o + w], qz[:, h % 2, h // 2, j * P:(j + 1) * P],
                                               kk[:, h // 2, k0:k0 + w], start=True, stop=True)
                            mm.then_inc(sn["sc"], 1)

                        def output(j):
                            for x in range(2):
                                pe.wait_ge(sn[f"pt{x}"], bs[f"pt{x}"] + gsum[j + 1] // 2)
                            if j:
                                pe.wait_ge(sn["og"], bs["og"] + j)
                            for h in range(HEADS):
                                for kb in range(nkey[j]):
                                    mm = pe.matmul(ps[:, 7, h * HD:(h + 1) * HD], pt[:, j % 2, kb, h % 2, h // 2, :],
                                                   v[:, j + 1 - nkey[j] + kb, h * HD:(h + 1) * HD],
                                                   start=(kb == 0), stop=(kb == nkey[j] - 1))
                            mm.then_inc(sn["pv"], 1)

                        scores(0)
                        for j in range(NT):
                            if j + 1 < NT:
                                scores(j + 1)
                            if j:
                                output(j - 1)
                            pe.wait_ge(sn["exp"], bs["exp"] + j + 1)
                            for n in range(ngrp[j]):
                                kb, par = n // 2, n % 2
                                w = gsum[j] + n
                                if w >= 3:
                                    pe.wait_ge(sn[f"pt{(w - 3) % 2}"], bs[f"pt{(w - 3) % 2}"] + (w - 3) // 2 + 1)
                                o = (2 - nkey[j] + kb) * P
                                for hh in range(4):
                                    tr = pe.transpose(ps[:, 4 + w % 3, hh * P:(hh + 1) * P],
                                                      sbuf[:, j % 2, par, hh, o:o + P], ident[:, :])
                                tr.then_inc(sn["tr"], 1)
                        output(NT - 1)

                    @block.vector
                    def _(dve):
                        link = Link(dve, "dve_link")

                        def soft(j):
                            w = 2 * P - nkey[j] * P
                            if j == 0:
                                dve.wait_ge(sn["bias"], bs["bias"] + 32)
                            dve.wait_ge(sn["sc"], bs["sc"] + j + 1)
                            if j >= 2:
                                dve.wait_ge(sn["tr"], bs["tr"] + gsum[j - 1])
                            for par in range(2):
                                ins = dve.scalar_tensor_tensor(
                                    sbuf[:, j % 2, par, :, w:], ps[:, 2 * par:2 * par + 2, :].rearrange(
                                        "p a (b k) -> p (a b) k", b=2)[:, :, w:], 0.125,
                                    bias[:, par, :, w:], ALU.mult, ALU.add)
                                if par == 0:
                                    link(ins)
                                else:
                                    ins.then_inc(sn["sb"], 1)
                            dve.wait_ge(sn["sb"], bs["sb"] + j + 1)
                            if j >= 3:
                                dve.wait_ge(sn[f"out{j % 3}"], bs[f"out{j % 3}"] + 16 * (j // 3))
                            dve.tensor_reduce(og[:, j % 3, 520:528].rearrange("p (hh two) -> p two hh", two=2),
                                              sbuf[:, j % 2, :, :, w:], X, ALU.max, negate=True
                                              ).then_inc(sn["nm"], 1)

                        soft(0)
                        for j in range(NT):
                            if j + 1 < NT:
                                soft(j + 1)
                            for n in range(1, ngrp[j], 2):
                                w = gsum[j] + n
                                dve.wait_ge(sn["tr"], bs["tr"] + w + 1)
                                if j >= 2:
                                    dve.wait_ge(sn["pv"], bs["pv"] + j - 1)
                                dve.tensor_copy(pt[:, j % 2, n // 2, n % 2, :, :].rearrange("p a b -> p (a b)"),
                                                ps[:, 4 + w % 3, :]).then_inc(sn["pt1"], 1)

                    @block.scalar
                    def _(act):
                        def numerators(j):
                            act.wait_ge(sn["pv"], bs["pv"] + j + 1)
                            act.activation(og[:, j % 3, 0:512], ps[:, 7, :], ACT.Copy).then_inc(sn["og"], 1)

                        for j in range(NT):
                            w0 = 2 * P - nkey[j] * P
                            act.wait_ge(sn["nm"], bs["nm"] + j + 1)
                            for h in range(HEADS):
                                part = sbuf[:, j % 2, h % 2, h // 2, w0:]
                                e = act.activation(part, part, ACT.Exp, bias=og[:, j % 3, 520 + h:521 + h],
                                                   accum_out=og[:, j % 3, 512 + h:513 + h])
                            e.then_inc(sn["exp"], 1)
                            if j:
                                numerators(j - 1)
                            for n in range(0, ngrp[j], 2):
                                w = gsum[j] + n
                                act.wait_ge(sn["tr"], bs["tr"] + w + 1)
                                if j >= 2:
                                    act.wait_ge(sn["pv"], bs["pv"] + j - 1)
                                act.activation(pt[:, j % 2, n // 2, n % 2, :, :].rearrange("p a b -> p (a b)"),
                                               ps[:, 4 + w % 3, :], ACT.Copy).then_inc(sn["pt0"], 1)
                        numerators(NT - 1)

                    @block.sync
                    def _(sp):
                        sp.wait_ge(S("at_lines"), 48)
                        for par in range(2):
                            sp.dma_start(bias[:, par, :, :],
                                         bass.AP(tensor=lines_d.tensor, offset=(g * HEADS + par) * P * 384 + 127,
                                                 ap=[[383, P], [2 * P * 384, 4], [1, 2 * P]])).then_inc(sn["bias"], 16)
                        for j in range(NT):
                            sp.wait_ge(sn["og"], bs["og"] + j + 1)
                            r, i0 = divmod(j * P, length)
                            sp.dma_start(gv[r, i0:i0 + P, :], og[:, j % 3, :]).then_inc(sn[f"out{j % 3}"], 16)
                        for x in range(3):
                            sp.wait_ge(sn[f"out{x}"], bs[f"out{x}"] + 16 * len(range(x, NT, 3)))
            hs.close()

            merged = pair(keep, "merged", [P, KD, T])
            o_stack = ExitStack()
            oa = pair(o_stack, "oa", [P, 4, T])
            orw = pair(o_stack, "orw", [P, 4, T])
            with ExitStack() as st:
                dm = sb(st, "cdm", [P, NT, 3, 16])
                ga = sb(st, "cg", [P, 3, 3, 512])
                mn = sb(st, "cmn", [P, NT, HEADS])
                wg = sb(st, "cwg", [P, NT, 3, HEADS])
                wd = sb(st, "cwd", [P, NT, 3, HEADS])
                zg = sb(st, "czg", [P, 3, 8, P])
                ob = sb(st, "cob", [P, 3, 4, P])
                og = sb(st, "cog", [P, 2, 2, 4, P])
                block = st.enter_context(nc.Block())

                @block.sync
                def _(sp):
                    for g in range(3):
                        sp.dma_start(dm[:, :, g, :], ag_d[g].rearrange("(t p) c -> p t c", p=P)[:, :, 512:528]
                                     ).then_inc(S("cm_dm"), 16)
                    for tt in range(NT):
                        tok = slice(tt * P, (tt + 1) * P)
                        if tt >= 3:
                            sp.wait_ge(S("cm_ev"), 2 * (tt - 2))
                        sp.dma_start(ga[:, tt % 3, :, :], ag_d[:, tok, 0:512].rearrange("g p c -> p g c")
                                     ).then_inc(S(f"cm_in{tt % 3}"), 16)
                        sp.dma_start(zg[:, tt % 3, :, :], gates_d[:, 0:8, tok]).then_inc(S(f"cm_in{tt % 3}"), 16)
                        sp.dma_start(ob[:, tt % 3, :, :], orw_d[:, :, tok]).then_inc(S(f"cm_in{tt % 3}"), 16)

                @block.scalar
                def _(act):
                    act.wait_ge(S("cm_dif"), 3)
                    act.activation(wg[:, :, :, :], wg[:, :, :, :], ACT.Exp).then_inc(S("cm_w"), 1)
                    for tt in range(NT):
                        tok = slice(tt * P, (tt + 1) * P)
                        for n, o in enumerate((oa, orw)):
                            act.wait_ge(S("cm_ev"), 2 * tt + n + 1)
                            high(act, o[0][:, :, tok], og[:, tt % 2, n, :, :]).then_inc(S("cm_hi"), 1)

                @block.vector
                def _(dve):
                    link = Link(dve, "dve_link")
                    nm = lambda g: dm[:, :, g, 8:16]
                    dve.wait_ge(S("cm_dm"), 48)
                    link(dve.tensor_tensor(mn[:, :, :], nm(0), nm(1), ALU.min))
                    link(dve.tensor_tensor(mn[:, :, :], mn[:, :, :], nm(2), ALU.min))
                    for g in range(3):
                        dve.tensor_tensor(wg[:, :, g, :], mn[:, :, :], nm(g), ALU.subtract).then_inc(S("cm_dif"), 1)
                    dve.wait_ge(S("cm_w"), 1)
                    link(dve.tensor_tensor(wd[:, :, :, :], wg[:, :, :, :], dm[:, :, :, 0:8], ALU.mult))
                    link(dve.tensor_tensor(mn[:, :, :], wd[:, :, 0, :], wd[:, :, 1, :], ALU.add))
                    link(dve.tensor_tensor(mn[:, :, :], mn[:, :, :], wd[:, :, 2, :], ALU.add))
                    link(dve.reciprocal(mn[:, :, :], mn[:, :, :]))
                    link(dve.tensor_tensor(wg[:, :, :, :], wg[:, :, :, :],
                                           mn[:, :, :].unsqueeze(2).to_broadcast([P, NT, 3, HEADS]), ALU.mult))

                    def lows(tt):
                        tok = slice(tt * P, (tt + 1) * P)
                        for n, o in enumerate((oa, orw)):
                            dve.wait_ge(S("cm_hi"), 2 * tt + n + 1)
                            low(dve, o[1][:, :, tok], og[:, tt % 2, n, :, :], o[0][:, :, tok]).then_inc(S("cm_lo"), 1)

                    def gated(tt):
                        dve.wait_ge(S("cm_tr"), tt + 1)
                        if tt >= 2:
                            dve.wait_ge(S("cm_lo"), 2 * (tt - 1))
                        dve.tensor_tensor(og[:, tt % 2, 0, :, :], ps[:, tt % 8, :].rearrange("p (c t) -> p c t", t=P),
                                          zg[:, tt % 3, 4:8, :], ALU.mult).then_inc(S("cm_ev"), 1)
                        dve.tensor_tensor(og[:, tt % 2, 1, :, :], ob[:, tt % 3, :, :],
                                          zg[:, tt % 3, 0:4, :], ALU.mult).then_inc(S("cm_ev"), 1)
                    for tt in range(NT):
                        dve.wait_ge(S(f"cm_in{tt % 3}"), 48 * (tt // 3 + 1))
                        num = ga[:, tt % 3, :, :].rearrange("p g (h c) -> p g h c", c=HD)
                        link(dve.tensor_tensor(num, num, wg[:, tt, :, :].unsqueeze(3).to_broadcast([P, 3, HEADS, HD]),
                                               ALU.mult))
                        o = ga[:, tt % 3, 0, :]
                        link(dve.tensor_tensor(o, o, ga[:, tt % 3, 1, :], ALU.add))
                        dve.tensor_tensor(o, o, ga[:, tt % 3, 2, :], ALU.add).then_inc(S("cm_o"), 1)
                        if tt:
                            gated(tt - 1)
                        if tt >= 2:
                            lows(tt - 2)
                    gated(NT - 1)
                    lows(NT - 2)
                    lows(NT - 1)

                @block.tensor
                def _(pe):
                    for tt in range(NT):
                        pe.wait_ge(S("cm_o"), tt + 1)
                        for c in range(4):
                            tr = pe.transpose(ps[:, tt % 8, c * P:(c + 1) * P], ga[:, tt % 3, 0, c * P:(c + 1) * P],
                                              ident[:, :])
                        tr.then_inc(S("cm_tr"), 1)
            return merged, oa, orw, o_stack

        def merge(merged, gates, wa, wb, oa, ob, tag):
            with ExitStack() as st:
                gt = sb(st, "mg_gates" + tag, [P, 2, 2, T])
                ta = sb(st, "mg_a" + tag, [P, 4, 512])
                tm = sb(st, "mg_m" + tag, [P, 2, 512])
                b = {n: base("mg_" + n, c) for n, c in (("g0", 128), ("g1", 128), ("hi", 2 * KD), ("lo", 2 * KD), ("used", KD))}

                def gate_loads(gp, ev):
                    for m in range(KD):
                        if m >= 2:
                            gp.wait_ge(S("mg_used"), b["used"] + m - 1)
                        for i in range(2):
                            gp.dma_start(gt[:, m % 2, i, :], gates[:, KD * i + m, :]).then_inc(S(f"mg_g{m % 2}"), 16)

                link = [None]

                def lows(dve, m, x):
                    dve.wait_ge(S("mg_hi"), b["hi"] + 2 * m + x + 1)
                    cut_ = (slice(None), m, slice(x * 512, (x + 1) * 512))
                    low(dve, merged[1][cut_], tm[:, x, :], merged[0][cut_]).then_inc(S("mg_lo"), 1)

                def jobs(m):
                    def up_a(kind, dve, src, _m, x):
                        if x == 0:
                            dve.wait_ge(S(f"mg_g{m % 2}"), b[f"g{m % 2}"] + 32 * (m // 2 + 1))
                        return dve.tensor_tensor(ta[:, 2 * (m % 2) + x, :], src, gt[:, m % 2, 0, x * 512:(x + 1) * 512], ALU.mult)

                    def lows_before(dve, _m, x, done):
                        if m:
                            lows(dve, m - 1, x)

                    def up_b(kind, dve, src, _m, x):
                        if link[0] is None:
                            link[0] = Link(dve, "dve_link")
                        if m:
                            dve.wait_ge(S("mg_lo"), b["lo"] + 2 * (m - 1) + x + 1)
                        link[0](dve.tensor_tensor(tm[:, x, :], src, gt[:, m % 2, 1, x * 512:(x + 1) * 512], ALU.mult))
                        return dve.tensor_tensor(tm[:, x, :], tm[:, x, :], ta[:, 2 * (m % 2) + x, :], ALU.add)

                    def highs(act, _m, x, summed):
                        act.wait_ge(*summed)
                        high(act, merged[0][:, m, x * 512:(x + 1) * 512], tm[:, x, :]).then_inc(S("mg_hi"), 1)

                    def after_b(dve, _m, x, done):
                        if x:
                            dve.engine_nop().then_inc(S("mg_used"), 1)
                            if m == KD - 1:
                                lows(dve, m, 0)
                                lows(dve, m, 1)
                    cols = slice(m * P, (m + 1) * P)
                    return [dict(w=wcols(wa, 0, D)[:, :, cols], mode="T", act=whole(oa), tiles=2, on="dve", evac=up_a,
                                 dve_step=lows_before),
                            dict(w=wcols(wb, 0, D)[:, :, cols], mode="T", act=whole(ob), tiles=2, on="dve", evac=up_b,
                                 act_step=highs, dve_step=after_b)]
                gemm([j for m in range(KD) for j in jobs(m)], ring=3, pool=gate_loads)

        def row(ap):
            return bass.AP(tensor=ap.tensor, offset=ap.offset, ap=[[0, P], [1, D]])

        def merge_first():
            keep = ExitStack()
            merged, oa, orw, o_stack = attention(keep)
            merge(merged, gates_d[:, 8:24, :], A["w_up_attn"][0], A["w_up_rwkv"][0], oa, orw, "1")
            o_stack.close()
            retire("rw_", "gate_", "gn_", "at_", "cm_", "h_")
            with ExitStack() as st:
                rows = sb(st, "rows1", [P, NT, D])
                xr = sb(st, "x_res", [P, NT, D])
                pg = sb(st, "post_gain", [P, D])
                sq = sb(st, "pn_sq", [P, D])
                ss = sb(st, "pn_ss", [P, NT])
                link = [None]

                def rows_io(gp, ev):
                    gp.dma_start(pg[:, :], row(A["post_norm_gain"][0])).then_inc(S("pn_in"), 16)
                    gp.dma_start(xr[:, :, :], x_rows.rearrange("(t p) d -> p t d", p=P)).then_inc(S("pn_in"), 16)
                    for t in range(NT):
                        gp.wait_ge(S("pn_x"), t + 1)
                        gp.dma_start(x1_d[t * P:(t + 1) * P, :], xr[:, t, :]).then_inc(S("pn_out"), 16)
                    gp.wait_ge(S("pn_out"), 16 * NT)

                def root(act, t):
                    act.wait_ge(S("pn_mean"), t + 1)
                    act.activation(ss[:, t:t + 1], ss[:, t:t + 1], ACT.Sqrt).then_inc(S("pn_root"), 1)

                def squares(act, t, x, done):
                    act.wait_ge(*done)
                    if t:
                        act.wait_ge(S("pn_ss"), t)
                    act.activation(sq[:, :], rows[:, t, :], ACT.Square, accum_out=ss[:, t:t + 1]).then_inc(S("pn_ss"), 1)
                    if t:
                        root(act, t - 1)
                    if t == NT - 1:
                        root(act, t)

                def normed(dve, t):
                    dve.wait_ge(S("pn_root"), t + 1)
                    link[0](dve.reciprocal(ss[:, t:t + 1], ss[:, t:t + 1]))
                    link[0](dve.scalar_tensor_tensor(rows[:, t, :], rows[:, t, :], ss[:, t:t + 1], pg[:, :],
                                                     ALU.mult, ALU.mult))
                    dve.tensor_tensor(xr[:, t, :], xr[:, t, :], rows[:, t, :], ALU.add).then_inc(S("pn_x"), 1)

                def residual(dve, t, x, done):
                    if link[0] is None:
                        link[0] = Link(dve, "dve_link")
                        dve.wait_ge(S("pn_in"), 32)
                    dve.wait_ge(S("pn_ss"), t + 1)
                    dve.tensor_scalar(ss[:, t:t + 1], ss[:, t:t + 1], 1.0 / D, EPS, ALU.mult, ALU.add
                                      ).then_inc(S("pn_mean"), 1)
                    if t:
                        normed(dve, t - 1)
                    if t == NT - 1:
                        normed(dve, t)
                jobs = [dict(w=wcols(A["w_out"][0], 512 * i, 512 * i + 512), mode="N", act=token_tiles(merged), tiles=NT,
                             on="act", evac=lambda kind, eng, src, m, x, i=i: copy(
                                 kind, eng, rows[:, m, i * 512:(i + 1) * 512], src)) for i in range(2)]
                jobs[1].update(act_step=squares, dve_step=residual)
                gemm(jobs, ring=5, pool=rows_io)
            keep.close()

        def chan_norm(buf, to, kt, slices, gain, width, tag):
            n_tok = buf.shape[2]
            with ExitStack() as st:
                sq = sb(st, f"cn_sq{tag}", [P, kt, n_tok])
                rs = sb(st, f"cn_rs{tag}", [P, n_tok])
                b = {n: base(f"cn_{n}", c) for n, c in (("sq", 1), ("mm", 1), ("mean", len(slices)), ("root", 1),
                                                       ("x", kt), ("hi", kt))}
                block = st.enter_context(nc.Block())

                @block.scalar
                def _(act):
                    act.activation(sq[:, :, :], buf[:, :, :], ACT.Square).then_inc(S("cn_sq"), 1)
                    act.wait_ge(S("cn_mean"), b["mean"] + len(slices))
                    act.activation(rs[:, :], rs[:, :], ACT.Sqrt).then_inc(S("cn_root"), 1)
                    for k in range(kt):
                        act.wait_ge(S("cn_x"), b["x"] + k + 1)
                        high(act, to[0][:, k, :], buf[:, k, :]).then_inc(S("cn_hi"), 1)

                @block.tensor
                def _(pe):
                    pe.wait_ge(S("cn_sq"), b["sq"] + 1)
                    for n, (o, w) in enumerate(slices):
                        for k in range(kt):
                            mm = pe.matmul(ps[:, n, 0:w], ones[:, :], sq[:, k, o:o + w], start=(k == 0), stop=(k == kt - 1))
                    mm.then_inc(S("cn_mm"), 1)

                @block.vector
                def _(dve):
                    link = Link(dve, "dve_link")
                    dve.wait_ge(S("cn_mm"), b["mm"] + 1)
                    for n, (o, w) in enumerate(slices):
                        dve.tensor_scalar(rs[:, o:o + w], ps[:, n, 0:w], 1.0 / width, EPS, ALU.mult, ALU.add
                                          ).then_inc(S("cn_mean"), 1)
                    dve.wait_ge(S("cn_root"), b["root"] + 1)
                    link(dve.reciprocal(rs[:, :], rs[:, :]))
                    for k in range(kt):
                        dve.scalar_tensor_tensor(buf[:, k, :], buf[:, k, :], gain[:, k:k + 1], rs[:, :], ALU.mult, ALU.mult
                                                 ).then_inc(S("cn_x"), 1)
                    for k in range(kt):
                        dve.wait_ge(S("cn_hi"), b["hi"] + k + 1)
                        low(dve, to[1][:, k, :], buf[:, k, :], to[0][:, k, :])

        def head_norm_rope(parts):
            with ExitStack() as st:
                tiles = [(n, t) for n, (_b, nt, _g) in enumerate(parts) for t in range(nt)]
                ss = [sb(st, f"hn_ss{n}", [P, nt, HEADS]) for n, (_b, nt, _g) in enumerate(parts)]
                sq = sb(st, "hn_sq", [P, 2, HEADS, QKD])
                tmp = [[sb(st, f"hn_t{n}{i}", [P, 2, HEADS, ROPE]) for i in range(2)] for n in range(2)]
                rope = sb(st, "hn_rope", [P, NT, 2, ROPE])
                load([(rope[:, :, :, :].rearrange("p t a c -> p t (a c)"),
                       A["c_rope"].rearrange("(t p) a c -> p t (a c)", p=P))])
                block = st.enter_context(nc.Block())

                def finish(eng, n, name):
                    link = Link(eng, name)
                    buf, nt, gain_row = parts[n]
                    for t in range(nt):
                        t1, t2 = (x[:, t % 2] for x in tmp[n])
                        link(eng.tensor_tensor(buf[:, t, :, :], buf[:, t, :, :],
                                               ss[n][:, t, :].unsqueeze(2).to_broadcast([P, HEADS, QKD]), ALU.mult))
                        link(eng.tensor_tensor(buf[:, t, :, :], buf[:, t, :, :],
                                               gain_row.unsqueeze(1).to_broadcast([P, HEADS, QKD]), ALU.mult))
                        if t < NT:
                            xr = buf[:, t, :, NOPE:QKD]
                            tab = lambda i: rope[:, t, i, :].unsqueeze(1).to_broadcast([P, HEADS, ROPE])
                            halves = lambda ap, s: ap.rearrange("p h (a s e) -> p h a s e", a=2, s=2)[:, :, :, s, :]
                            eng.tensor_tensor(t1, xr, tab(0), ALU.mult)
                            eng.tensor_copy(halves(t2, 0), halves(xr, 1))
                            link(eng.tensor_copy(halves(t2, 1), halves(xr, 0)))
                            link(eng.tensor_tensor(t2, t2, tab(1), ALU.mult))
                            link(eng.tensor_tensor(xr, t1, t2, ALU.add))

                @block.scalar
                def _(act):
                    for i, (n, t) in enumerate(tiles):
                        if i >= 2:
                            act.wait_ge(S("hn_ss"), i - 1)
                        act.activation(sq[:, i % 2, :, :], parts[n][0][:, t, :, :], ACT.Square).then_inc(S("hn_sq"), 1)
                    for n in range(2):
                        act.wait_ge(S("hn_mean"), n + 1)
                        act.activation(ss[n][:, :, :], ss[n][:, :, :], ACT.Sqrt).then_inc(S("hn_root"), 1)

                @block.vector
                def _(dve):
                    i = 0
                    for n, (_b, nt, _g) in enumerate(parts):
                        for t in range(nt):
                            dve.wait_ge(S("hn_sq"), i + 1)
                            dve.tensor_reduce(ss[n][:, t, :], sq[:, i % 2, :, :], X, ALU.add).then_inc(S("hn_ss"), 1)
                            i += 1
                        dve.wait_ge(S("hn_ss"), i)
                        dve.tensor_scalar(ss[n][:, :, :], ss[n][:, :, :], 1.0 / QKD, EPS, ALU.mult, ALU.add
                                          ).then_inc(S("hn_mean"), 1)
                    for n in range(2):
                        dve.wait_ge(S("hn_root"), n + 1)
                        dve.reciprocal(ss[n][:, :, :], ss[n][:, :, :]).then_inc(S("hn_rcp"), 1)
                    dve.wait_ge(S("hn_rcp"), 2)
                    finish(dve, 1, "dve_link")

                @block.gpsimd
                def _(gp):
                    gp.wait_ge(S("hn_rcp"), 1)
                    finish(gp, 0, "pool_link")

        def second():
            w_in2 = A["w_in_2"][0]
            with nc.Block() as block:
                @block.vector
                def _(dve):
                    for dst, g, s, v in ((1, 7, 1, 0), (3, 7, 1, 1), (5, 8, 4, 0)):
                        dve.scalar_tensor_tensor(gains[:, dst, :], modv[:, s, :, v], 1.0, gains[:, g, :], ALU.add, ALU.mult)
                    for dst, s, v in ((2, 0, 0), (4, 0, 1), (6, 3, 0)):
                        dve.tensor_copy(gains[:, dst, :], modv[:, s, :, v])

                @block.sync
                def _(sp):
                    with nc.allow_non_contiguous_dma("per-channel vectors"):
                        for i, s in enumerate((2, 5)):
                            sp.dma_start(vec(res_gates_d[i]), modv[:, s, :, 0]).then_inc(S("mod_out"), 16)
                    sp.wait_ge(S("mod_out"), 32)
            mix = ExitStack()
            fT = sb(mix, "fT", [P, 4, T])
            low_rank = ExitStack()
            cq = sb(low_rank, "cq", [P, 3, T])
            ckv = sb(low_rank, "ckv", [P, 2, NKEY])
            kpe = sb(low_rank, "kpe", [P, NKT, ROPE])
            with ExitStack() as st:
                hA = pair(st, "hA", [P, KD, NKEY])
                go = sb(st, "go2", [P, 4, 512])
                norm_T(x1_d, NT, gains[:, 1, :], gains[:, 2, :], tuple(h[:, :, 0:T] for h in hA), tag="n2")
                norm_T(A["ctx_2"][0], NTC, gains[:, 3, :], gains[:, 4, :], tuple(h[:, :, T:NKEY] for h in hA), tag="n3")

                def gate(kind, act, src, m, x):
                    n = 2 * m + x
                    if n >= 4:
                        act.wait_ge(S(f"g2_out{n % 4}"), 16 * (n // 4))
                    return act.activation(go[:, n % 4, :], src, ACT.Sigmoid)

                def gate_out(act, m, x, done):
                    n = 2 * m + x
                    act.wait_ge(*done)
                    act.dma_start(gates2_d[:, m, x * 512:(x + 1) * 512], go[:, n % 4, :]).then_inc(S(f"g2_out{n % 4}"), 16)
                    if n == 31:
                        for i in range(4):
                            act.wait_ge(S(f"g2_out{i}"), 16 * 8)

                latent = tuple(h[:, :, 0:T] for h in hA)
                put = lambda dst: lambda kind, eng, src, m, x: copy(
                    kind, eng, dst[:, m, x * 512:min((x + 1) * 512, dst.shape[2])],
                    src[:, 0:min(512, dst.shape[2] - x * 512)])
                gemm([dict(w=wcols(w_in2, 0, QL), mode="T", act=whole(latent), tiles=2, evac=put(cq)),
                      dict(w=wcols(w_in2, QL, QL + KVL), mode="T", tiles=3, evac=put(ckv),
                           act=lambda k, x: tuple(h[:, k, x * 512:min((x + 1) * 512, NKEY)] for h in hA)),
                      dict(w=wcols(w_in2, QL + KVL, OFF_F), mode="N", act=token_tiles(hA), tiles=NKT,
                           evac=lambda kind, eng, src, m, x: copy(kind, eng, kpe[:, m, :], src[:, 0:ROPE])),
                      dict(w=wcols(w_in2, OFF_F, OFF_F + 512), mode="T", act=whole(latent), tiles=2, evac=put(fT)),
                      dict(w=wcols(w_in2, OFF_GA, OFF_GA + 2 * D), mode="T", act=whole(latent), tiles=2, evac=gate,
                           on="act", act_step=gate_out)])

            with ExitStack() as st:
                foT = fT
                dc = sb(st, "dft_ch", [P, 2 * P])
                dp = sb(st, "dft_pos", [P, 4, 4, 512])
                ab = sb(st, "dft_ab", [P, NT, 4, 2, P])
                fold = sb(st, "dft_fold", [P, 4, 2, 4, 2, P])
                load([(dc[:, :], A["c_dft_ch"]), (dp[:, :, :, :].rearrange("p t a k -> p t (a k)"),
                                                  A["c_dft_pos"].rearrange("(t p) a b k -> p t (a b k)", p=P))])
                block = st.enter_context(nc.Block())

                @block.tensor
                def _(pe):
                    for tt in range(NT):
                        if tt >= 4:
                            pe.wait_ge(S("ft_ab"), 2 * (tt - 3))
                        for g in range(4):
                            mm = pe.matmul(ps[:, 2 * (tt % 4) + g // 2, (g % 2) * 256:(g % 2 + 1) * 256],
                                           fT[:, g, tt * P:(tt + 1) * P], dc[:, :], start=True, stop=True)
                        mm.then_inc(S("ft_mm"), 1)
                    pe.wait_ge(S("ft_fold"), 8)
                    for n, (g, par) in enumerate([(g, par) for g in range(4) for par in range(2)]):
                        for pt_ in range(4):
                            for x in range(2):
                                mm = pe.matmul(ps[:, n, :], fold[:, pt_, par, g, x, :], dp[:, pt_, 2 * par + x, :],
                                               start=(pt_ + x == 0), stop=(pt_ + x == 4))
                        mm.then_inc(S("ft_out"), 1)

                @block.scalar
                def _(act):
                    for tt in range(NT):
                        act.wait_ge(S("ft_mm"), tt + 1)
                        for x in range(2):
                            act.activation(ab[:, tt, 2 * x:2 * x + 2, :, :].rearrange("p g x c -> p (g x c)"),
                                           ps[:, 2 * (tt % 4) + x, :], ACT.Copy).then_inc(S("ft_ab"), 1)

                @block.vector
                def _(dve):
                    flat = lambda ap: ap.rearrange("p g x c -> p (g x c)")
                    dve.wait_ge(S("ft_ab"), 2 * NT)
                    for tt in range(4):
                        for par, op in ((0, ALU.add), (1, ALU.subtract)):
                            dve.tensor_tensor(flat(fold[:, tt, par]), flat(ab[:, tt]), flat(ab[:, tt + 4]), op
                                              ).then_inc(S("ft_fold"), 1)
                    for n in range(8):
                        g, par = divmod(n, 2)
                        dve.wait_ge(S("ft_out"), n + 1)
                        dve.tensor_copy(foT[:, g, par::2], ps[:, n, :]).then_inc(S("ft_done"), 1)

                @block.sync
                def _(sp):
                    sp.wait_ge(S("ft_done"), 8)
                    sp.dma_start(four_d, foT[:, :, :]).then_inc(S("ft_stored"), 16)
                    sp.wait_ge(S("ft_stored"), 16)

            kv_slices = [(0, 512), (512, 512), (1024, 256)]
            mla = ExitStack()
            q = sb(mla, "mla_q", [P, NT, HEADS, QKD])
            kb = sb(mla, "mla_k", [P, NKT, HEADS, QKD])
            vb = sb(mla, "mla_v", [P, NKT, HEADS, VD])
            rowg = sb(mla, "mla_rowg", [P, 2, QKD])
            with ExitStack() as st:
                gv = sb(st, "mla_gv", [P, 5])
                rowv = lambda ap: bass.AP(tensor=ap.tensor, offset=ap.offset, ap=[[0, P], [1, QKD]])
                load([(gv[:, 0:3], vec(A["q_a_norm_g_2"][0], 3)), (gv[:, 3:5], vec(A["kv_a_norm_g_2"][0], 2)),
                      (rowg[:, 0, :], rowv(A["q_norm_g_2"][0])), (rowg[:, 1, :], rowv(A["k_norm_g_2"][0]))])
                cqp = pair(st, "cqp", [P, 3, T])
                ckvp = pair(st, "ckvp", [P, 2, NKEY])
                chan_norm(cq, cqp, 3, [(0, 512), (512, 512)], gv[:, 0:3], QL, "q")
                chan_norm(ckv, ckvp, 2, kv_slices, gv[:, 3:5], KVL, "kv")
                wq = A["w_q_up_2"][0]
                qf = q[:, :, :, :].rearrange("p t h c -> p t (h c)")

                def split_kv(kind, eng, src, m, ci):
                    s4 = src.rearrange("p (h c) -> p h c", c=P)
                    copy(kind, eng, kb[:, m, 4 * ci:4 * ci + 4, 0:NOPE], s4[:, :, 0:NOPE])
                    return copy(kind, eng, vb[:, m, 4 * ci:4 * ci + 4, :], s4[:, :, NOPE:])
                gemm([dict(w=wcols(wq, 384 * i, 384 * i + 384), mode="N", act=token_tiles(cqp), tiles=NT,
                           evac=lambda kind, eng, src, m, x, i=i: copy(
                               kind, eng, qf[:, m, i * 384:(i + 1) * 384], src[:, 0:384])) for i in range(2)]
                     + [dict(w=wcols(A["w_kv_up_2"][0], 512 * i, 512 * i + 512), mode="N", act=token_tiles(ckvp), tiles=NKT,
                             evac=lambda kind, eng, src, m, x, i=i: split_kv(kind, eng, src, m, i)) for i in range(2)],
                     ring=4)
                with nc.Block() as block:
                    @block.vector
                    def _(dve):
                        for t in range(NKT):
                            dve.tensor_copy(kb[:, t, :, NOPE:QKD],
                                            kpe[:, t, :].unsqueeze(1).to_broadcast([P, HEADS, ROPE]))
                head_norm_rope([(q, NT, rowg[:, 0, :]), (kb, NKT, rowg[:, 1, :])])
            dump("q", q[:, :, :, :].rearrange("p t h c -> p (t h c)"))
            dump("k", kb[:, :, :, :].rearrange("p t h c -> p (t h c)"))
            SC = QKD ** -0.5
            with ExitStack() as st:
                qT = pair(st, "qT", [QKD, 2, T])
                kT = pair(st, "kT", [QKD, 2, NKEY])
                pr = sb(st, "mla_p", [P, 2, NKEY])
                pT = sb(st, "mla_pT", [P, 2, NKT, P])
                nm = sb(st, "mla_nm", [P, HEADS * NT])
                den = sb(st, "mla_den", [P, HEADS * NT])
                ao = fT[:, :, :].rearrange("p c t -> p (c t)").rearrange("p (t c) -> p t c", c=512)
                block = st.enter_context(nc.Block())
                its = [(h, t) for h in range(HEADS) for t in range(NT)]
                GR = [(0, 4), (4, 4), (8, 2)]

                N = len(its)
                s3 = lambda n: ps[:, 3 * (n % 2):3 * (n % 2) + 3, :].rearrange("p a b -> p (a b)")[:, 0:NKEY]
                out_bank = lambda n: ps[:, 3 * ((n + 1) % 2) + 2, 256:256 + VD]

                def head_group(h, i):
                    src, dst, t0, n_ = (q, qT, 4 * i, NT) if i < 2 else (kb, kT, 4 * (i - 2), NKT)
                    return src, t0, min(4, n_ - t0), dst

                def next_head(n):
                    h, t = its[n]
                    return (h + 1, t - 1) if 1 <= t <= 5 and h + 1 < HEADS else None

                @block.tensor
                def _(pe):
                    def head(h, i):
                        src, t0, w, _d = head_group(h, i)
                        n = 5 * h + i
                        if n:
                            pe.wait_ge(S("ml_hlo"), n)
                        for j in range(w):
                            tr = pe.transpose(ps[0:QKD, 7, j * P:(j + 1) * P], src[:, t0 + j, h, :], ident[:, :])
                        tr.then_inc(S("ml_htr"), 1)

                    def scores(n):
                        h, t = its[n]
                        if t == 0:
                            pe.wait_ge(S("ml_hlo"), 5 * h + 5)
                        if n >= 2:
                            pe.wait_ge(S("ml_e"), n - 1)
                        for i in range(3):
                            w = 512 if i < 2 else 256
                            if i == 2 and n >= 3:
                                pe.wait_ge(S("ml_o"), n - 2)
                            mm = products(pe, ps[:, 3 * (n % 2) + i, 0:w],
                                          tuple(a[:, h % 2, t * P:(t + 1) * P] for a in qT),
                                          tuple(a[:, h % 2, i * 512:i * 512 + w] for a in kT), True, True)
                        mm.then_inc(S("ml_s"), 1)

                    def transposes(n, i):
                        g0, w = GR[i]
                        for j in range(w):
                            tr = pe.transpose(ps[:, 6 + i % 2, j * P:(j + 1) * P],
                                              pr[:, n % 2, (g0 + j) * P:(g0 + j + 1) * P], ident[:, :])
                        tr.then_inc(S("ml_t"), 1)

                    def output(n):
                        h = its[n][0]
                        pe.wait_ge(S("ml_pd"), n + 1)
                        pe.wait_ge(S("ml_pa"), 2 * n + 2)
                        for k in range(NKT):
                            mm = pe.matmul(out_bank(n), pT[:, n % 2, k, :], vb[:, k, h, :],
                                           start=(k == 0), stop=(k == NKT - 1))
                        mm.then_inc(S("ml_pv"), 1)

                    for i in range(5):
                        head(0, i)
                    scores(0)
                    for n in range(N):
                        if n + 1 < N:
                            scores(n + 1)
                        pe.wait_ge(S("ml_e"), n + 1)
                        if n:
                            pe.wait_ge(S("ml_pa"), 2 * n)
                            pe.wait_ge(S("ml_pd"), n)
                        if n and next_head(n - 1):
                            hh, i = next_head(n - 1)
                            pe.wait_ge(S("ml_hlo"), 5 * hh + i + 1)
                        transposes(n, 0)
                        transposes(n, 1)
                        if n:
                            output(n - 1)
                        pe.wait_ge(S("ml_pa"), 2 * n + 1)
                        transposes(n, 2)
                        if next_head(n):
                            pe.wait_ge(S("ml_pd"), n + 1)
                            head(*next_head(n))
                    output(N - 1)

                @block.scalar
                def _(act):
                    def exponentials(n):
                        act.wait_ge(S("ml_m"), n + 1)
                        if n >= 2:
                            act.wait_ge(S("ml_t"), 3 * (n - 1))
                        act.activation(pr[:, n % 2, :], s3(n), ACT.Exp, bias=nm[:, n:n + 1], scale=SC,
                                       accum_out=den[:, n:n + 1]).then_inc(S("ml_e"), 1)

                    def probs(n, i):
                        g0, w = GR[i]
                        act.wait_ge(S("ml_t"), 3 * n + i + 1)
                        if i == 0 and n >= 2:
                            act.wait_ge(S("ml_pv"), n - 1)
                        act.activation(pT[:, n % 2, g0:g0 + w, :].rearrange("p k t -> p (k t)"), ps[:, 6, 0:w * P],
                                       ACT.Copy).then_inc(S("ml_pa"), 1)

                    def head(h, i):
                        _s, t0, w, dst = head_group(h, i)
                        act.wait_ge(S("ml_htr"), 5 * h + i + 1)
                        high(act, dst[0][:, h % 2, t0 * P:(t0 + w) * P], ps[0:QKD, 7, 0:w * P]).then_inc(S("ml_hev"), 1)

                    for i in range(5):
                        head(0, i)
                    exponentials(0)
                    for n in range(N):
                        probs(n, 0)
                        if n + 1 < N:
                            exponentials(n + 1)
                        probs(n, 2)
                        if next_head(n):
                            head(*next_head(n))

                @block.vector
                def _(dve):
                    link = Link(dve, "dve_link")

                    def head(h, i):
                        _s, t0, w, dst = head_group(h, i)
                        dve.wait_ge(S("ml_hev"), 5 * h + i + 1)
                        at = (slice(None), h % 2, slice(t0 * P, (t0 + w) * P))
                        low(dve, dst[1][at], ps[0:QKD, 7, 0:w * P], dst[0][at]).then_inc(S("ml_hlo"), 1)

                    def row_max(n):
                        dve.wait_ge(S("ml_s"), n + 1)
                        link(dve.tensor_reduce(nm[:, n:n + 1], s3(n), X, ALU.max))
                        dve.tensor_scalar(nm[:, n:n + 1], nm[:, n:n + 1], -SC, None, ALU.mult).then_inc(S("ml_m"), 1)

                    def output(n):
                        h, t = its[n]
                        dve.wait_ge(S("ml_e"), n + 1)
                        link(dve.reciprocal(den[:, n:n + 1], den[:, n:n + 1]))
                        dve.wait_ge(S("ml_pv"), n + 1)
                        dve.tensor_scalar(ao[:, t, h * VD:(h + 1) * VD], out_bank(n), den[:, n:n + 1], None, ALU.mult
                                          ).then_inc(S("ml_o"), 1)

                    for i in range(5):
                        head(0, i)
                    row_max(0)
                    for n in range(N):
                        if n + 1 < N:
                            row_max(n + 1)
                        dve.wait_ge(S("ml_t"), 3 * n + 2)
                        if n >= 2:
                            dve.wait_ge(S("ml_pv"), n - 1)
                        dve.tensor_copy(pT[:, n % 2, 4:8, :].rearrange("p k t -> p (k t)"), ps[:, 7, :]
                                        ).then_inc(S("ml_pd"), 1)
                        if n:
                            output(n - 1)
                        if next_head(n):
                            head(*next_head(n))
                    output(N - 1)
            mla.close()
            low_rank.close()

            merged = pair(mix, "merged2", [P, KD, T])
            with ExitStack() as st:
                oa = pair(st, "oa2", [P, 4, T])
                of = pair(st, "of2", [P, 4, T])
                with ExitStack() as s2:
                    fr = sb(s2, "four_raw", [P, 4, T])
                    block = s2.enter_context(nc.Block())

                    @block.sync
                    def _(sp):
                        for c in range(4):
                            sp.dma_start(fr[:, c, :], four_d[:, c, :]).then_inc(S(f"m2_in{c}"), 16)

                    @block.tensor
                    def _(pe):
                        for t in range(NT):
                            for c in range(4):
                                tr = pe.transpose(ps[:, t, c * P:(c + 1) * P], ao[:, t, c * P:(c + 1) * P], ident[:, :])
                            tr.then_inc(S("m2_tr"), 1)

                    @block.scalar
                    def _(act):
                        for t in range(NT):
                            act.wait_ge(S("m2_tr"), t + 1)
                            high(act, oa[0][:, :, t * P:(t + 1) * P], ps[:, t, :].rearrange("p (c x) -> p c x", x=P)
                                 ).then_inc(S("m2_hi"), 1)
                        for c in range(4):
                            act.wait_ge(S(f"m2_in{c}"), 16)
                            high(act, of[0][:, c, :], fr[:, c, :]).then_inc(S("m2_hi"), 1)

                    @block.vector
                    def _(dve):
                        for t in range(NT):
                            tok = slice(t * P, (t + 1) * P)
                            dve.wait_ge(S("m2_hi"), t + 1)
                            low(dve, oa[1][:, :, tok], ps[:, t, :].rearrange("p (c x) -> p c x", x=P), oa[0][:, :, tok])
                        for c in range(4):
                            dve.wait_ge(S("m2_hi"), NT + c + 1)
                            low(dve, of[1][:, c, :], fr[:, c, :], of[0][:, c, :])
                merge(merged, gates2_d, A["w_o_attn_2"][0], A["w_fourier_2"][0], oa, of, "2")
            with ExitStack() as st:
                g1r = sb(st, "g1r", [P, D])
                x2 = sb(st, "x2_sum", [P, NT, D])

                def rows_io(gp, ev):
                    gp.dma_start(g1r[:, :], row(res_gates_d[0])).then_inc(S("r2_in"), 16)
                    gp.dma_start(x2[:, :, :], x1_d.rearrange("(t p) d -> p t d", p=P)).then_inc(S("r2_in"), 16)
                    for t in range(NT):
                        gp.wait_ge(S("r2_x"), t + 1)
                        gp.dma_start(x2_d[t * P:(t + 1) * P, :], x2[:, t, :]).then_inc(S("r2_out"), 16)
                    gp.wait_ge(S("r2_out"), 16 * NT)

                link = [None]
                prod = sb(st, "g1_prod", [P, 512])

                def add(kind, dve, src, m, i):
                    cols = slice(i * 512, (i + 1) * 512)
                    if link[0] is None:
                        link[0] = Link(dve, "dve_link")
                        dve.wait_ge(S("r2_in"), 32)
                    link[0](dve.tensor_tensor(prod[:, :], src, g1r[:, cols], ALU.mult))
                    link[0](dve.tensor_tensor(x2[:, m, cols], x2[:, m, cols], prod[:, :], ALU.add))
                    if i == 1:
                        dve.engine_nop().then_inc(S("r2_x"), 1)
                    return dve.engine_nop()
                gemm([dict(w=wcols(A["w_out_2"][0], 512 * i, 512 * i + 512), mode="N", act=token_tiles(merged), tiles=NT,
                           on="dve", evac=lambda kind, eng, src, m, x, i=i: add(kind, eng, src, m, i))
                      for i in range(2)], pool=rows_io)
            mix.close()

            xn_d = dram("xn_rows", [T, D])
            y_d = dram("y_rows", [T, D])
            moe = ExitStack()
            slot = sb(moe, "slot", [P, NT, NE])
            sel = sb(moe, "sel", [P, NE, 2])
            idx = sb(moe, "idx", [P, NE], U32)
            iota = sb(moe, "iota", [P, CAP])
            with ExitStack() as st:
                h2T = sb(st, "h2T", [P, KD, T])
                wr = sb(st, "wr", [P, KD, NE])
                load([(wr[:, :, :], A["w_router_2"][0].rearrange("(k p) e -> p k e", p=P))])

                def logits(pe, t):
                    for k in range(KD):
                        mm = pe.matmul(ps[:, 7, t * NE:(t + 1) * NE], h2T[:, k, t * P:(t + 1) * P], wr[:, k, :],
                                       start=(k == 0), stop=(k == KD - 1))
                    if t == NT - 1:
                        mm.then_inc(S("ro_l"), 1)
                norm_T(x2_d, NT, gains[:, 5, :], gains[:, 6, :], None, dst=h2T, rows_out=xn_d, banks=6, after=logits,
                       tag="n4")
                tg = sb(st, "tg", [P, NT, NE, 5], BF16)
                left = sb(st, "left", [P, NT, NE])
                tok = sb(st, "tok", [P, NT, 2])
                lg = sb(st, "lg", [P, NT, NE])
                m1 = sb(st, "lg_m", [P, NT])
                affT = sb(st, "affT", [NE, T])
                work = sb(st, "work", [NE, T])
                one = sb(st, "one", [NE, T])
                m8 = sb(st, "m8", [NE, 8])
                zero = sb(st, "zero", [P, D])
                picked = sb(st, "picked", [P, NE, 5])
                oh = sb(st, "oh", [P, 2, NT, CAP], BF16)
                load([(tok[:, :], A["c_tok"]),
                      (iota[:, :], A["c_slot"])])
                block = st.enter_context(nc.Block())

                @block.tensor
                def _(pe):
                    pe.wait_ge(S("ro_a"), 1)
                    for t in range(NT):
                        tr = pe.transpose(ps[0:NE, 1 + t // 4, (t % 4) * P:(t % 4 + 1) * P], lg[:, t, :], ident[:, :])
                    tr.then_inc(S("ro_t"), 1)
                    pe.wait_ge(S("ro_s"), 1)
                    for t in range(NT):
                        tr = pe.transpose(ps[:, 3, t * NE:(t + 1) * NE], work[:, t * P:(t + 1) * P], ident[0:NE, 0:NE])
                    tr.then_inc(S("ro_st"), 1)
                    for e in range(NE):
                        pe.wait_ge(S("ro_oh"), e + 1)
                        for t in range(NT):
                            mm = pe.matmul(ps[:, 4, 5 * e:5 * e + 5], oh[:, e % 2, t, :], tg[:, t, e, :],
                                           start=(t == 0), stop=(t == NT - 1))
                        mm.then_inc(S("ro_sel"), 1)

                @block.scalar
                def _(act):
                    act.wait_ge(S("ro_m"), 1)
                    act.activation(lg[:, :, :], lg[:, :, :], ACT.Exp).then_inc(S("ro_e"), 1)

                @block.sync
                def _(sp):
                    sp.wait_ge(S("ro_zero"), 1)
                    for t in range(NT):
                        sp.dma_start(y_d[t * P:(t + 1) * P, :], zero[:, :]).then_inc(S("ro_y0"), 16)
                    sp.wait_ge(S("ro_y0"), 16 * NT)

                @block.vector
                def _(dve):
                    link = Link(dve, "dve_link")
                    dve.memset(zero[:, :], 0.0).then_inc(S("ro_zero"), 1)
                    link(dve.memset(one[:, :], 1.0))
                    dve.wait_ge(S("ro_l"), 1)
                    lgp = ps[:, 7, 0:NT * NE].rearrange("p (t e) -> p t e", e=NE)
                    wide = lambda ap: ap.unsqueeze(2).to_broadcast([P, NT, NE])
                    link(dve.tensor_reduce(m1[:, :], lgp, X, ALU.max))
                    dve.tensor_tensor(lg[:, :, :], lgp, wide(m1[:, :]), ALU.subtract).then_inc(S("ro_m"), 1)
                    dve.wait_ge(S("ro_e"), 1)
                    link(dve.tensor_reduce(m1[:, :], lg[:, :, :], X, ALU.add))
                    link(dve.reciprocal(m1[:, :], m1[:, :]))
                    dve.tensor_tensor(lg[:, :, :], lg[:, :, :], wide(m1[:, :]), ALU.mult).then_inc(S("ro_a"), 1)
                    dve.wait_ge(S("ro_a"), 1)
                    for i in range(2):
                        dve.tensor_copy(tg[:, :, :, i], wide(tok[:, :, i]))
                    for i in range(3):
                        src = lg if i == 0 else left
                        link(dve.tensor_copy(tg[:, :, :, 2 + i], src[:, :, :]))
                        if i < 2:
                            link(dve.tensor_tensor(left[:, :, :], src[:, :, :], tg[:, :, :, 2 + i], ALU.subtract))
                    dve.wait_ge(S("ro_t"), 1)
                    for dst in (affT, work):
                        ins = dve.tensor_copy(dst[:, :].rearrange("p (a b) -> p a b", a=2), ps[0:NE, 1:3, :])
                    link(ins)
                    for _i in range(CAP // 8):
                        link(dve.max(m8[:, :], work[:, :]))
                        link(dve.match_replace(work[:, :], m8[:, :], work[:, :], -1.0))
                    link(dve.tensor_scalar(work[:, :], work[:, :], 0.0, None, ALU.is_lt))
                    link(dve.tensor_tensor_scan(affT[:, :], one[:, :], work[:, :], 0.0, ALU.mult, ALU.add))
                    link(dve.tensor_tensor(work[:, :], affT[:, :], work[:, :], ALU.mult))
                    dve.tensor_scalar(work[:, :], work[:, :], -1.0, None, ALU.add).then_inc(S("ro_s"), 1)
                    dve.wait_ge(S("ro_st"), 1)
                    link(dve.tensor_copy(slot[:, :, :].rearrange("p t e -> p (t e)"), ps[:, 3, 0:NT * NE]))
                    for e in range(NE):
                        if e >= 2:
                            dve.wait_ge(S("ro_sel"), e - 1)
                        dve.tensor_tensor(oh[:, e % 2, :, :], iota[:, :].unsqueeze(1).to_broadcast([P, NT, CAP]),
                                          slot[:, :, e:e + 1].to_broadcast([P, NT, CAP]), ALU.is_equal
                                          ).then_inc(S("ro_oh"), 1)
                    dve.wait_ge(S("ro_sel"), NE)
                    link(dve.tensor_copy(picked[:, :, :].rearrange("p e x -> p (e x)"), ps[:, 4, 0:5 * NE]))
                    dve.tensor_tensor(sel[:, :, 0], picked[:, :, 0], picked[:, :, 1], ALU.add)
                    link(dve.tensor_tensor(sel[:, :, 1], picked[:, :, 2], picked[:, :, 3], ALU.add))
                    link(dve.tensor_tensor(sel[:, :, 1], sel[:, :, 1], picked[:, :, 4], ALU.add))
                    dve.tensor_copy(idx[:, :], sel[:, :, 0])
            dump("sel", sel[:, :, :].rearrange("p e x -> p (e x)"))

            with ExitStack() as st:
                xe = sb(st, "xe", [P, 2, D])
                xm = sb(st, "xm", [P, 2, 4, P])
                xT = pair(st, "xT", [P, 2, KD, P])
                ag = sb(st, "ag", [P, DE])
                au = sb(st, "au", [P, 2, DE])
                aT = pair(st, "aT", [P, 2, 4, P])
                ye = sb(st, "ye", [P, 2, D])
                lk = [None]

                def rows_io(gp, ev):
                    def gather(e):
                        if e >= 2:
                            gp.wait_ge(S("mo_xt"), e - 1)
                        gp.indirect_dma_start(xe[:, e % 2, :], None, xn_d,
                                              bass.IndirectOffsetOnAxis(ap=idx[:, e:e + 1], axis=0),
                                              ).then_inc(S(f"mo_x{e % 2}"), 16)
                    gather(0)
                    gather(1)
                    for e in range(NE):
                        if e + 2 < NE:
                            gather(e + 2)
                        gp.wait_ge(*ev(down_done[e]))
                        if e:
                            gp.wait_ge(S("mo_y"), 16 * e)
                        gp.indirect_dma_start(y_d, bass.IndirectOffsetOnAxis(ap=idx[:, e:e + 1], axis=0),
                                              ye[:, e % 2, :], None, compute_op=ALU.add).then_inc(S("mo_y"), 16)
                    gp.wait_ge(S("mo_y"), 16 * NE)

                def pe_step(pe, step):
                    for what, e in step:
                        if what == "x":
                            pe.wait_ge(S(f"mo_x{e % 2}"), 16 * (e // 2 + 1))
                            if e:
                                pe.wait_ge(S("mo_xm"), 2 * e)
                            if e >= 2:
                                pe.wait_ge(S("mo_hlo"), e - 1)
                            for k in range(KD):
                                tr = pe.transpose(ps[:, 6 + k // 4, (k % 4) * P:(k % 4 + 1) * P],
                                                  xe[:, e % 2, k * P:(k + 1) * P], ident[:, :])
                            tr.then_inc(S("mo_xt"), 1)
                        else:
                            pe.wait_ge(S("mo_h"), e + 1)
                            pe.wait_ge(S("mo_xm"), 2 * min(e + 2, NE))
                            for f in range(4):
                                tr = pe.transpose(ps[:, 6, f * P:(f + 1) * P], au[:, e % 2, f * P:(f + 1) * P], ident[:, :])
                            tr.then_inc(S("mo_ht"), 1)

                def act_step(act, step):
                    for what, e in step:
                        if what == "x":
                            for b in range(2):
                                act.wait_ge(S("mo_xm"), 2 * e + b + 1)
                                if e >= 2 and b == 0:
                                    act.wait_ge(S("mo_h"), e - 1)
                                high(act, xT[0][:, e % 2, 4 * b:4 * b + 4, :], xm[:, b, :, :]).then_inc(S("mo_xhi"), 1)
                        else:
                            act.wait_ge(S("mo_ht"), e + 1)
                            high(act, aT[0][:, e % 2, :, :].rearrange("p f t -> p (f t)"), ps[:, 6, :]
                                 ).then_inc(S("mo_hhi"), 1)

                def dve_step(dve, step):
                    wide = lambda v, b: v[:, 4 * b:4 * b + 4].unsqueeze(2).to_broadcast([P, 4, P])
                    for what, e in step:
                        if what == "x":
                            for b in range(2):
                                dve.wait_ge(S("mo_xt"), e + 1)
                                if e:
                                    dve.wait_ge(S("mo_xlo"), 2 * (e - 1) + b + 1)
                                lk[0](dve.tensor_tensor(xm[:, b], ps[:, 6 + b, :].rearrange("p (k t) -> p k t", t=P),
                                                        wide(gains[:, 5, :], b), ALU.mult))
                                dve.tensor_tensor(xm[:, b], xm[:, b], wide(gains[:, 6, :], b), ALU.add
                                                  ).then_inc(S("mo_xm"), 1)
                            for b in range(2):
                                dve.wait_ge(S("mo_xhi"), 2 * e + b + 1)
                                at = (slice(None), e % 2, slice(4 * b, 4 * b + 4))
                                low(dve, xT[1][at], xm[:, b, :, :], xT[0][at]).then_inc(S("mo_xlo"), 1)
                        else:
                            dve.wait_ge(S("mo_hhi"), e + 1)
                            low(dve, aT[1][:, e % 2, :, :].rearrange("p f t -> p (f t)"), ps[:, 6, :],
                                aT[0][:, e % 2, :, :].rearrange("p f t -> p (f t)")).then_inc(S("mo_hlo"), 1)

                def gate_job(e):
                    def silu(kind, act, src, m, x):
                        if e:
                            act.wait_ge(S("mo_h"), e)
                        return act.activation(ag[:, :], src, ACT.Silu)
                    return dict(w=A["w_e_gate_2"][0, e].rearrange("(k p) f -> p k f", p=P), mode="N", tiles=1, on="act",
                                act=lambda k, m: tuple(h[:, e % 2, k, :] for h in xT), ready=[("mo_xlo", 2 * e + 2)],
                                evac=silu, dve_step=lambda dve, m, x, done: gate_done.append(done))

                gate_done = []

                def up_job(e):
                    def mult(kind, dve, src, m, x):
                        dve.wait_ge(*gate_done.pop())
                        if e >= 2:
                            dve.wait_ge(S("mo_ht"), e - 1)
                        return dve.tensor_tensor(au[:, e % 2, :], src, ag[:, :], ALU.mult)

                    def told(dve, m, x, done):
                        dve.wait_ge(*done)
                        dve.engine_nop().then_inc(S("mo_h"), 1)
                    return dict(w=A["w_e_up_2"][0, e].rearrange("(k p) f -> p k f", p=P), mode="N", tiles=1, on="dve",
                                act=lambda k, m: tuple(h[:, e % 2, k, :] for h in xT), evac=mult, dve_step=told)

                def down_job(e, c):
                    def scaled(kind, act, src, m, x):
                        if c == 0 and e >= 2:
                            act.wait_ge(S("mo_y"), 16 * (e - 1))
                        return act.activation(ye[:, e % 2, c * 512:(c + 1) * 512], src, ACT.Copy, scale=sel[:, e, 1:2])
                    return dict(w=A["w_e_down_2"][0, e].rearrange("(k p) n -> p k n", p=P)[:, :, c * 512:(c + 1) * 512],
                                mode="N", tiles=1, on="act", act=lambda k, m: tuple(h[:, e % 2, k, :] for h in aT),
                                ready=[("mo_hlo", e + 1)], evac=scaled)

                jobs, steps, down_done = [], {}, []
                for e in range(NE + 1):
                    if e < NE:
                        jobs += [gate_job(e), up_job(e)]
                        if e + 1 < NE:
                            steps[len(jobs) - 1] = [("x", e + 1)]
                    if e:
                        jobs += [down_job(e - 1, 0), down_job(e - 1, 1)]
                        down_done.append(len(jobs) - 1)
                    if e < NE:
                        steps[len(jobs) - 1] = steps.get(len(jobs) - 1, []) + [("h", e)]

                def first(kind, eng):
                    if kind == "dve":
                        lk[0] = Link(eng, "dve_link")
                    dict(pe=pe_step, act=act_step, dve=dve_step)[kind](eng, [("x", 0)])
                gemm(jobs, ring=12, raws=8, banks=6, pool=rows_io,
                     side={"at": steps, "pe": pe_step, "act": act_step, "dve": dve_step, "first": first})
            moe.close()

            with ExitStack() as st:
                xf = sb(st, "xf", [P, NT, D])
                yf = sb(st, "yf", [P, NT, D])
                g2r = sb(st, "g2r", [P, D])
                block = st.enter_context(nc.Block())

                @block.sync
                def _(sp):
                    sp.dma_start(g2r[:, :], row(res_gates_d[1])).then_inc(S("fi_g"), 16)
                    for t in range(NT):
                        sp.dma_start(yf[:, t, :], y_d[t * P:(t + 1) * P, :]).then_inc(S(f"fi_in{t}"), 16)
                        sp.dma_start(xf[:, t, :], x2_d[t * P:(t + 1) * P, :]).then_inc(S(f"fi_in{t}"), 16)

                @block.gpsimd
                def _(gp):
                    for t in range(NT):
                        gp.wait_ge(S("fi_x"), t + 1)
                        gp.dma_start(out[0, t * P:(t + 1) * P, :], xf[:, t, :]).then_inc(S("fi_out"), 16)
                    gp.wait_ge(S("fi_out"), 16 * NT)

                @block.vector
                def _(dve):
                    link = Link(dve, "dve_link")
                    dve.wait_ge(S("fi_g"), 16)
                    for t in range(NT):
                        dve.wait_ge(S(f"fi_in{t}"), 32)
                        link(dve.tensor_tensor(yf[:, t, :], yf[:, t, :], g2r[:, :], ALU.mult))
                        dve.tensor_tensor(xf[:, t, :], xf[:, t, :], yf[:, t, :], ALU.add).then_inc(S("fi_x"), 1)

        w_in = A["w_in"][0]
        x_rows = A["x"][0]
        x1_d = dram("x1_rows", [T, D])
        x2_d = dram("x2_rows", [T, D])
        h_d = dram("h", [P, KD, T])
        orw_d = dram("o_rwkv", [P, 4, T])
        four_d = dram("fourier", [P, 4, T])
        gates_d = dram("gates", [P, 24, T])
        gates2_d = dram("gates2", [P, 16, T])
        res_gates_d = dram("res_gates", [2, D])
        line_d = dram("bias_line", [3, HEADS, 384])
        lines_d = dram("bias_lines", [3, HEADS, P, 384])
        h_stack = ExitStack()
        hT = sb(h_stack, "hT", [P, KD, T])
        bias_lines()
        rwkv()
        h_stack.close()
        merge_first()
        if debug is not None and "x1_in" in debug:
            with nc.Block() as block:
                @block.sync
                def _(sp):
                    sp.dma_start(x1_d, A["x1_in"]).then_inc(S("dbgx"), 16)
                    sp.wait_ge(S("dbgx"), 16)
        if debug is None or debug.get("second", 1):
            second()
        dump("end", ident[:, :])


def kernel(**inputs):
    import numpy as _np
    import concourse.bacc as _bacc
    from concourse import mybir as _mybir
    from concourse.bass_utils import run_bass_kernel_spmd as _run

    nc = _bacc.Bacc("TRN2", target_bir_lowering=False, num_devices=1)
    arrays, aps = {}, {}
    for name, a in list(inputs.items()) + list(constants().items()):
        a = _np.ascontiguousarray(a)
        if name == "c_ctx_2":
            a = a.reshape(1, -1)
        arrays[name] = a
        aps[name] = nc.dram_tensor(name, a.shape, _mybir.dt.from_np(a.dtype), kind="ExternalInput").ap()
    out = nc.dram_tensor("out_0", (1, T, D), F32, kind="ExternalOutput").ap()
    build(nc, aps, out)
    r = _run(nc, [arrays], core_ids=[0])
    return r.results[0]["out_0"]
```
